# Optimizing a Trainium2 kernel written in Bass

```python
import math
import jax
import jax.numpy as jnp
from jax import lax
import numpy as np
import jax, jax.numpy as jnp

D_MODEL = 1024
BATCH = 1
SEQ = 256
DEPTH = 2

HEAD_DIM = 64
CHUNK = 64
FOX_HEADS = 4
FOX_BLOCK = 128
GLA_HEADS = 4
GLA_LOWRANK = 16
GLA_TAU = 16.0
RET_HEADS = 4
ROPE_THETA = 10000.0
SSD_HEADS = 8
SSD_GROUPS = 2
SSD_STATE = 64
SSD_CONV = 4
SSD_INNER = SSD_HEADS * HEAD_DIM
SSD_CONV_CH = SSD_INNER + 2 * SSD_GROUPS * SSD_STATE
FOX_W = FOX_HEADS * HEAD_DIM
GLA_W = GLA_HEADS * HEAD_DIM
RET_W = RET_HEADS * HEAD_DIM
N_BRANCH = 4
FFN_HIDDEN = ((8 * D_MODEL + 3 * 256 - 1) // (3 * 256)) * 256
NORM_EPS = 1e-6
IN_SPLITS = (FOX_W, FOX_W, FOX_W, FOX_HEADS,
             GLA_W, GLA_W, GLA_W, GLA_LOWRANK, GLA_W,
             RET_W, RET_W, RET_W, RET_W,
             SSD_INNER, SSD_CONV_CH, SSD_HEADS,
             N_BRANCH * D_MODEL)
N_IN = sum(IN_SPLITS)


def rms_norm(x, g):
    xf = x.astype(jnp.float32)
    y = xf * lax.rsqrt(jnp.mean(xf * xf, axis=-1, keepdims=True) + NORM_EPS)
    return (y * g.astype(jnp.float32)).astype(x.dtype)

def split_cols(u, sizes):
    return jnp.split(u, np.cumsum(sizes)[:-1].tolist(), axis=-1)

def rotary_tables(positions):
    half = HEAD_DIM // 2
    inv = ROPE_THETA ** (-jnp.arange(half, dtype=jnp.float32) / half)
    ang = positions.astype(jnp.float32)[..., None] * inv
    return jnp.cos(ang)[:, :, None, :], jnp.sin(ang)[:, :, None, :]

def apply_rotary(x, cos, sin):
    half = x.shape[-1] // 2
    xf = x.astype(jnp.float32)
    x1, x2 = xf[..., :half], xf[..., half:]
    return jnp.concatenate([x1 * cos - x2 * sin, x1 * sin + x2 * cos], axis=-1).astype(x.dtype)

def causal_depthwise_conv(x, w, b):
    k_w, ch = w.shape
    y = lax.conv_general_dilated(x, w[:, None, :], window_strides=(1,), padding=[(k_w - 1, 0)],
                                 dimension_numbers=('NWC', 'WIO', 'NWC'), feature_group_count=ch)
    return y + b

def forgetting_attention(q, k, v, f_logit, q_gain, k_gain):
    bsz, seq, nh, dh = q.shape
    nb = seq // FOX_BLOCK
    qf = rms_norm(q, q_gain).astype(jnp.float32) * (dh ** -0.5)
    kf = rms_norm(k, k_gain).astype(jnp.float32)
    vf = v.astype(jnp.float32)
    c = jnp.cumsum(jax.nn.log_sigmoid(f_logit.astype(jnp.float32)), axis=1)
    qb = qf.reshape(bsz, nb, FOX_BLOCK, nh, dh).transpose(1, 0, 3, 2, 4)
    cb = c.reshape(bsz, nb, FOX_BLOCK, nh).transpose(1, 0, 3, 2)
    ck = c.transpose(0, 2, 1)
    kpos = jnp.arange(seq)

    def block(args):
        q_blk, c_blk, i = args
        s = jnp.einsum('bhqd,bkhd->bhqk', q_blk, kf) + c_blk[..., :, None] - ck[..., None, :]
        qpos = i * FOX_BLOCK + jnp.arange(FOX_BLOCK)
        s = jnp.where(kpos[None, :] <= qpos[:, None], s, -jnp.inf)
        p = jax.nn.softmax(s, axis=-1)
        return jnp.einsum('bhqk,bkhd->bqhd', p, vf)

    o = lax.map(block, (qb, cb, jnp.arange(nb)))
    return o.transpose(1, 0, 2, 3, 4).reshape(bsz, seq, nh * dh).astype(v.dtype)

def gla_chunked(q, k, v, log_a):
    bsz, seq, nh, dk = q.shape
    dv = v.shape[-1]
    nc = seq // CHUNK
    qf = (q.astype(jnp.float32) * (dk ** -0.5)).reshape(bsz, nc, CHUNK, nh, dk)
    kf = k.astype(jnp.float32).reshape(bsz, nc, CHUNK, nh, dk)
    vf = v.astype(jnp.float32).reshape(bsz, nc, CHUNK, nh, dv)
    b = jnp.cumsum(log_a.astype(jnp.float32).reshape(bsz, nc, CHUNK, nh, dk), axis=2)
    b_last = b[:, :, -1]
    q_dec = qf * jnp.exp(b)
    k_inv = kf * jnp.exp(-b)
    k_end = kf * jnp.exp(b_last[:, :, None] - b)
    mask = jnp.tril(jnp.ones((CHUNK, CHUNK), dtype=bool))
    attn = jnp.where(mask, jnp.einsum('bcthd,bcshd->bchts', q_dec, k_inv), 0.0)
    o_intra = jnp.einsum('bchts,bcshv->bcthv', attn, vf)
    kv = jnp.einsum('bcshd,bcshv->bchdv', k_end, vf)

    def step(state, inp):
        kv_c, dec_c = inp
        return state * dec_c[..., None] + kv_c, state

    s0 = jnp.zeros((bsz, nh, dk, dv), jnp.float32)
    _, s_in = lax.scan(step, s0, (jnp.moveaxis(kv, 1, 0), jnp.moveaxis(jnp.exp(b_last), 1, 0)))
    s_in = jnp.moveaxis(s_in, 0, 1)
    o_inter = jnp.einsum('bcthd,bchdv->bcthv', q_dec, s_in)
    return (o_intra + o_inter).reshape(bsz, seq, nh, dv).astype(v.dtype)

def retention_chunked(q, k, v, log_gamma):
    bsz, seq, nh, dk = q.shape
    dv = v.shape[-1]
    nc = seq // CHUNK
    qf = q.astype(jnp.float32).reshape(bsz, nc, CHUNK, nh, dk)
    kf = (k.astype(jnp.float32) * (dk ** -0.5)).reshape(bsz, nc, CHUNK, nh, dk)
    vf = v.astype(jnp.float32).reshape(bsz, nc, CHUNK, nh, dv)
    idx = jnp.arange(CHUNK, dtype=jnp.float32)
    rel = idx[:, None] - idx[None, :]
    decay = jnp.where(rel >= 0, jnp.exp(jnp.maximum(rel, 0.0)[None] * log_gamma[:, None, None]), 0.0)
    scores = jnp.einsum('bcthd,bcshd->bchts', qf, kf) * decay
    o_intra = jnp.einsum('bchts,bcshv->bcthv', scores, vf)
    q_w = jnp.exp((idx + 1.0)[:, None] * log_gamma)
    k_w = jnp.exp((CHUNK - 1.0 - idx)[:, None] * log_gamma)
    kv = jnp.einsum('bcshd,sh,bcshv->bchdv', kf, k_w, vf)
    chunk_decay = jnp.exp(CHUNK * log_gamma)

    def step(state, kv_c):
        return state * chunk_decay[:, None, None] + kv_c, state

    s0 = jnp.zeros((bsz, nh, dk, dv), jnp.float32)
    _, s_in = lax.scan(step, s0, jnp.moveaxis(kv, 1, 0))
    s_in = jnp.moveaxis(s_in, 0, 1)
    o_inter = jnp.einsum('bcthd,th,bchdv->bcthv', qf, q_w, s_in)
    return (o_intra + o_inter).reshape(bsz, seq, nh, dv).astype(v.dtype)

def ssd_chunked(x, dt, a, bmat, cmat):
    bsz, seq, nh, hp = x.shape
    ng, ns = bmat.shape[2], bmat.shape[3]
    r = nh // ng
    nc = seq // CHUNK
    xf = x.astype(jnp.float32).reshape(bsz, nc, CHUNK, ng, r, hp)
    dtf = dt.astype(jnp.float32).reshape(bsz, nc, CHUNK, ng, r)
    bf = bmat.astype(jnp.float32).reshape(bsz, nc, CHUNK, ng, ns)
    cf = cmat.astype(jnp.float32).reshape(bsz, nc, CHUNK, ng, ns)
    xdt = xf * dtf[..., None]
    cs = jnp.cumsum(dtf * a.astype(jnp.float32).reshape(ng, r), axis=2)
    cs_h = jnp.moveaxis(cs, 2, -1)
    mask = jnp.tril(jnp.ones((CHUNK, CHUNK), dtype=bool))
    seg = cs_h[..., :, None] - cs_h[..., None, :]
    decay = jnp.exp(jnp.where(mask, seg, -jnp.inf))
    cb = jnp.einsum('bctgn,bcsgn->bcgts', cf, bf)
    y_intra = jnp.einsum('bcgts,bcgrts,bcsgrp->bctgrp', cb, decay, xdt)
    cs_last = cs[:, :, -1]
    w_end = jnp.exp(cs_last[:, :, None] - cs)
    contrib = jnp.einsum('bcsgn,bcsgr,bcsgrp->bcgrpn', bf, w_end, xdt)

    def step(h, inp):
        c_c, d_c = inp
        return h * d_c[..., None, None] + c_c, h

    h0 = jnp.zeros((bsz, ng, r, hp, ns), jnp.float32)
    _, h_in = lax.scan(step, h0, (jnp.moveaxis(contrib, 1, 0), jnp.moveaxis(jnp.exp(cs_last), 1, 0)))
    h_in = jnp.moveaxis(h_in, 0, 1)
    y_inter = jnp.einsum('bctgn,bcgrpn,bctgr->bctgrp', cf, h_in, jnp.exp(cs))
    return (y_intra + y_inter).reshape(bsz, seq, nh, hp).astype(x.dtype)

def mixer_block(h, cos, sin, w_in, fox_bf, fox_qn, fox_kn, gla_w2, gla_b, gla_norm, ret_norm,
                conv_w, conv_b, dt_bias, a_log, d_skip, ssd_norm, w_up_a, w_up_b, w_up_c, w_up_d, w_out):
    bsz, seq, _ = h.shape
    u = h @ w_in
    (fq, fk, fv, ff, gq, gk, gv, glr, gr, rq, rk, rv, rg, z, xbc, dt, gates) = split_cols(u, IN_SPLITS)
    heads = lambda t: t.reshape(bsz, seq, -1, HEAD_DIM)
    y_a = forgetting_attention(heads(fq), heads(fk), heads(fv), ff + fox_bf, fox_qn, fox_kn)
    log_a = jax.nn.log_sigmoid((glr @ gla_w2 + gla_b).astype(jnp.float32)) / GLA_TAU
    o_b = gla_chunked(heads(gq), heads(gk), heads(gv), heads(log_a))
    y_b = (rms_norm(o_b, gla_norm) * jax.nn.silu(heads(gr))).reshape(bsz, seq, GLA_W)
    log_gamma = jnp.log(1.0 - 2.0 ** (-5.0 - jnp.arange(RET_HEADS, dtype=jnp.float32)))
    o_c = retention_chunked(apply_rotary(heads(rq), cos, sin), apply_rotary(heads(rk), cos, sin), heads(rv), log_gamma)
    y_c = (rms_norm(o_c, ret_norm) * jax.nn.silu(heads(rg))).reshape(bsz, seq, RET_W)
    xbc = jax.nn.silu(causal_depthwise_conv(xbc, conv_w, conv_b))
    xs, bm, cm = jnp.split(xbc, [SSD_INNER, SSD_INNER + SSD_GROUPS * SSD_STATE], axis=-1)
    dt = jax.nn.softplus((dt + dt_bias).astype(jnp.float32))
    a = -jnp.exp(a_log.astype(jnp.float32))
    xs_h = heads(xs)
    o_d = ssd_chunked(xs_h, dt, a, bm.reshape(bsz, seq, SSD_GROUPS, SSD_STATE), cm.reshape(bsz, seq, SSD_GROUPS, SSD_STATE))
    o_d = o_d + d_skip[:, None] * xs_h
    y_d = (o_d.reshape(bsz, seq, SSD_INNER) * jax.nn.silu(z)).reshape(bsz, seq, SSD_GROUPS, -1)
    y_d = rms_norm(y_d, ssd_norm.reshape(SSD_GROUPS, -1)).reshape(bsz, seq, SSD_INNER)
    g = jax.nn.sigmoid(gates.reshape(bsz, seq, N_BRANCH, D_MODEL))
    merged = (g[:, :, 0] * (y_a @ w_up_a) + g[:, :, 1] * (y_b @ w_up_b)
              + g[:, :, 2] * (y_c @ w_up_c) + g[:, :, 3] * (y_d @ w_up_d))
    return merged @ w_out

def swiglu(h, w_in, w_out):
    gate, up = jnp.split(h @ w_in, 2, axis=-1)
    return (jax.nn.silu(gate) * up) @ w_out

def first_inputs(seed: int = 0) -> dict:
    key = jax.random.key(seed)
    ks = jax.random.split(key, 26)
    f32 = jnp.float32
    L = DEPTH

    def normal(k, shape, fan_in):
        return jax.random.normal(k, shape, f32) * (fan_in ** -0.5)

    def gain(k, shape):
        return 1.0 + 0.02 * jax.random.normal(k, shape, f32)

    x = jax.random.normal(ks[0], (BATCH, SEQ, D_MODEL), f32)
    start = jax.random.randint(ks[1], (BATCH, 1), 0, 1024, dtype=jnp.int32)
    positions = start + jnp.arange(SEQ, dtype=jnp.int32)[None, :]
    dt0 = jnp.exp(jax.random.uniform(ks[14], (L, SSD_HEADS), f32, math.log(1e-3), math.log(1e-1)))
    return {
        'x': x,
        'positions': positions,
        'ln1': gain(ks[2], (L, D_MODEL)),
        'ln2': gain(ks[3], (L, D_MODEL)),
        'w_in': normal(ks[4], (L, D_MODEL, N_IN), D_MODEL),
        'fox_bf': jax.random.uniform(ks[5], (L, FOX_HEADS), f32, 1.0, 5.0),
        'fox_qn': gain(ks[6], (L, HEAD_DIM)),
        'fox_kn': gain(ks[7], (L, HEAD_DIM)),
        'gla_w2': normal(ks[8], (L, GLA_LOWRANK, GLA_W), GLA_LOWRANK),
        'gla_b': 0.1 * jax.random.normal(ks[9], (L, GLA_W), f32),
        'gla_norm': gain(ks[10], (L, HEAD_DIM)),
        'ret_norm': gain(ks[11], (L, HEAD_DIM)),
        'ssd_conv_w': normal(ks[12], (L, SSD_CONV, SSD_CONV_CH), SSD_CONV),
        'ssd_conv_b': 0.01 * jax.random.normal(ks[13], (L, SSD_CONV_CH), f32),
        'ssd_dt_bias': dt0 + jnp.log(-jnp.expm1(-dt0)),
        'ssd_a_log': jnp.log(jax.random.uniform(ks[15], (L, SSD_HEADS), f32, 1.0, 16.0)),
        'ssd_d': 1.0 + 0.1 * jax.random.normal(ks[16], (L, SSD_HEADS), f32),
        'ssd_norm': gain(ks[17], (L, SSD_INNER)),
        'w_up_a': normal(ks[18], (L, FOX_W, D_MODEL), FOX_W),
        'w_up_b': normal(ks[19], (L, GLA_W, D_MODEL), GLA_W),
        'w_up_c': normal(ks[20], (L, RET_W, D_MODEL), RET_W),
        'w_up_d': normal(ks[21], (L, SSD_INNER, D_MODEL), SSD_INNER),
        'w_out': normal(ks[22], (L, D_MODEL, D_MODEL), D_MODEL),
        'w_ffn_in': normal(ks[23], (L, D_MODEL, 2 * FFN_HIDDEN), D_MODEL),
        'w_ffn_out': normal(ks[24], (L, FFN_HIDDEN, D_MODEL), FFN_HIDDEN),
    }

def first_block(x, positions, ln1, ln2, w_in, fox_bf, fox_qn, fox_kn, gla_w2, gla_b, gla_norm, ret_norm,
              ssd_conv_w, ssd_conv_b, ssd_dt_bias, ssd_a_log, ssd_d, ssd_norm,
              w_up_a, w_up_b, w_up_c, w_up_d, w_out, w_ffn_in, w_ffn_out):
    cos, sin = rotary_tables(positions)
    for l in range(DEPTH):
        h = rms_norm(x, ln1[l])
        x = x + mixer_block(h, cos, sin, w_in[l], fox_bf[l], fox_qn[l], fox_kn[l], gla_w2[l], gla_b[l],
                            gla_norm[l], ret_norm[l], ssd_conv_w[l], ssd_conv_b[l], ssd_dt_bias[l],
                            ssd_a_log[l], ssd_d[l], ssd_norm[l], w_up_a[l], w_up_b[l], w_up_c[l],
                            w_up_d[l], w_out[l])
        h = rms_norm(x, ln2[l])
        x = x + swiglu(h, w_ffn_in[l], w_ffn_out[l])
    return x


N_BRANCHES = 4
BRANCH_WIDTH = D_MODEL // N_BRANCHES
MOBA_HEADS = 4
MOBA_HEAD_DIM = BRANCH_WIDTH // MOBA_HEADS
MOBA_BLOCK = 256
MOBA_TOPK = 3
Q_BLOCK = 128
CONV_WIDTH = 3
POOL_WINDOWS = (2, 4, 8, 16)
POOL_GROUP = BRANCH_WIDTH // len(POOL_WINDOWS)
DIFF_HEADS = 4
DIFF_V_DIM = BRANCH_WIDTH // DIFF_HEADS
DIFF_QK_DIM = DIFF_V_DIM // 2
REL_BUCKETS = 32
REL_MAX_DIST = 128
N_ATTN_HEADS = MOBA_HEADS + DIFF_HEADS
N_MIX_SLICES = 10
W_IN_WIDTH = N_MIX_SLICES * BRANCH_WIDTH + N_BRANCHES * D_MODEL
D_FF_DENSE = 2816
N_EXPERTS = 8
TOP_K_EXPERTS = 2
D_FF_EXPERT = 3584
N_DENSE = (DEPTH + 1) // 2
N_MOE = DEPTH // 2
RMS_EPS = 1e-6
SUBLN_EPS = 1e-5
NEG_INF = -1e30


def rmsnorm(x, g, eps=RMS_EPS):
    xf = x.astype(jnp.float32)
    r = lax.rsqrt(jnp.mean(xf * xf, axis=-1, keepdims=True) + eps)
    return (xf * r).astype(x.dtype) * g

def rel_bucket(dist):
    n = jnp.maximum(dist, 0)
    max_exact = REL_BUCKETS // 2
    nf = jnp.maximum(n, max_exact).astype(jnp.float32)
    large = max_exact + (jnp.log(nf / max_exact) / math.log(REL_MAX_DIST / max_exact)
                         * (REL_BUCKETS - max_exact)).astype(jnp.int32)
    large = jnp.minimum(large, REL_BUCKETS - 1)
    return jnp.where(n < max_exact, n, large)

def moba_attention(q, k, v, bias_tab):
    _, H, S, dh = q.shape
    n_blk = -(-S // MOBA_BLOCK)
    s_pad = n_blk * MOBA_BLOCK
    topk = min(MOBA_TOPK, n_blk)
    n_qc = s_pad // Q_BLOCK
    scale = dh ** -0.5
    pad = ((0, 0), (0, s_pad - S), (0, 0))
    head_ix = jnp.arange(H)[:, None, None, None]

    def per_seq(args):
        qb, kb, vb = args
        qb = jnp.pad(qb, pad) * scale
        k_blocks = jnp.pad(kb, pad).reshape(H, n_blk, MOBA_BLOCK, dh)
        v_blocks = jnp.pad(vb, pad).reshape(H, n_blk, MOBA_BLOCK, dh)
        k_mean = jnp.mean(k_blocks.astype(jnp.float32), axis=2).astype(kb.dtype)
        q_chunks = qb.reshape(H, n_qc, Q_BLOCK, dh).transpose(1, 0, 2, 3)

        def per_chunk(args2):
            qc, ci = args2
            t_pos = ci * Q_BLOCK + jnp.arange(Q_BLOCK)
            own = (ci * Q_BLOCK) // MOBA_BLOCK
            gate = jnp.einsum('hqd,hnd->hqn', qc, k_mean)
            gate = jnp.where(jnp.arange(n_blk) < own, gate, NEG_INF)
            _, sel = lax.top_k(gate, topk)
            valid = jnp.arange(topk) < own
            k_sel = jax.vmap(lambda kbh, ix: kbh[ix])(k_blocks, sel)
            v_sel = jax.vmap(lambda vbh, ix: vbh[ix])(v_blocks, sel)
            key_pos_sel = sel[..., None] * MOBA_BLOCK + jnp.arange(MOBA_BLOCK)
            bias_sel = bias_tab[head_ix, rel_bucket(t_pos[None, :, None, None] - key_pos_sel)]
            logit_sel = jnp.einsum('hqd,hqnkd->hqnk', qc, k_sel) + bias_sel
            logit_sel = jnp.where(valid[:, None], logit_sel, NEG_INF)
            k_own = lax.dynamic_index_in_dim(k_blocks, own, axis=1, keepdims=False)
            v_own = lax.dynamic_index_in_dim(v_blocks, own, axis=1, keepdims=False)
            rel_own = t_pos[:, None] - (own * MOBA_BLOCK + jnp.arange(MOBA_BLOCK))[None, :]
            logit_own = jnp.einsum('hqd,hkd->hqk', qc, k_own) + bias_tab[:, rel_bucket(rel_own)]
            logit_own = jnp.where(rel_own >= 0, logit_own, NEG_INF)
            logits = jnp.concatenate(
                [logit_sel.reshape(H, Q_BLOCK, topk * MOBA_BLOCK), logit_own], axis=-1)
            p = jax.nn.softmax(logits.astype(jnp.float32), axis=-1).astype(vb.dtype)
            p_sel = p[..., :topk * MOBA_BLOCK].reshape(H, Q_BLOCK, topk, MOBA_BLOCK)
            p_own = p[..., topk * MOBA_BLOCK:]
            return (jnp.einsum('hqnk,hqnkd->hqd', p_sel, v_sel)
                    + jnp.einsum('hqk,hkd->hqd', p_own, v_own))

        out = lax.map(per_chunk, (q_chunks, jnp.arange(n_qc)))
        return out.transpose(1, 0, 2, 3).reshape(H, s_pad, dh)[:, :S]

    return lax.map(per_seq, (q, k, v))

def diff_attention(q, k, v, bias_tab, lam, subln_g, lam_init):
    B_, H, _, S, dq = q.shape
    dv = v.shape[-1]
    n_qc = S // Q_BLOCK
    q = q * dq ** -0.5
    q_chunks = q.reshape(B_, H, 2, n_qc, Q_BLOCK, dq).transpose(3, 0, 1, 2, 4, 5)
    key_pos = jnp.arange(S)

    def per_chunk(args):
        qc, ci = args
        t_pos = ci * Q_BLOCK + jnp.arange(Q_BLOCK)
        rel = t_pos[:, None] - key_pos[None, :]
        bias = bias_tab[:, rel_bucket(rel)]
        logits = jnp.einsum('bhmqd,bhmsd->bhmqs', qc, k) + bias[None, :, None]
        logits = jnp.where(rel >= 0, logits, NEG_INF).astype(jnp.float32)
        p = jax.nn.softmax(logits, axis=-1)
        a = (p[:, :, 0] - lam * p[:, :, 1]).astype(v.dtype)
        return jnp.einsum('bhqs,bhsd->bhqd', a, v)

    o = lax.map(per_chunk, (q_chunks, jnp.arange(n_qc)))
    o = o.transpose(1, 2, 0, 3, 4).reshape(B_, H, S, dv)
    return rmsnorm(o, subln_g, SUBLN_EPS) * (1.0 - lam_init)

def short_conv(xt, b_gate, c_gate, w_conv):
    S = xt.shape[1]
    u = c_gate * xt
    up = jnp.pad(u, ((0, 0), (CONV_WIDTH - 1, 0), (0, 0)))
    conv = w_conv[0] * up[:, 0:S]
    for i in range(1, CONV_WIDTH):
        conv = conv + w_conv[i] * up[:, i:i + S]
    return b_gate * conv

def multiscale_pool(u, w_grp, scale):
    B_, S, _ = u.shape
    ug = u.reshape(B_, S, len(POOL_WINDOWS), POOL_GROUP)
    cs = jnp.cumsum(ug.astype(jnp.float32), axis=1)
    outs = []
    for g, w in enumerate(POOL_WINDOWS):
        c = cs[:, :, g]
        lag = jnp.pad(c, ((0, 0), (w, 0), (0, 0)))[:, :S]
        cnt = jnp.minimum(jnp.arange(1, S + 1), w).astype(jnp.float32)[None, :, None]
        outs.append((c - lag) / cnt)
    pooled = jnp.stack(outs, axis=2).astype(u.dtype) - ug
    y = jnp.einsum('bsgc,gcd->bsgd', pooled, w_grp).reshape(B_, S, BRANCH_WIDTH)
    return y * scale

def token_mixers(h, w_in, conv_w, pool_w, pool_scale, diff_lam, subln_g, branch_proj, w_out,
                 bias_table, layer_idx):
    B_, S, _ = h.shape
    u = h @ w_in
    split_pts = [BRANCH_WIDTH * i for i in range(1, N_MIX_SLICES + 1)]
    qa, ka, va, xb, bb, cb, pc, qd, kd, vd, gates = jnp.split(u, split_pts, axis=-1)

    def heads_a(t):
        return t.reshape(B_, S, MOBA_HEADS, MOBA_HEAD_DIM).transpose(0, 2, 1, 3)

    y_a = moba_attention(heads_a(qa), heads_a(ka), heads_a(va), bias_table[:, :MOBA_HEADS].T)
    y_a = y_a.transpose(0, 2, 1, 3).reshape(B_, S, BRANCH_WIDTH)

    y_b = short_conv(xb, bb, cb, conv_w)
    y_c = multiscale_pool(pc, pool_w, pool_scale)

    lam_init = 0.8 - 0.6 * math.exp(-0.3 * layer_idx)
    lam = (jnp.exp(jnp.sum(diff_lam[0] * diff_lam[1]).astype(jnp.float32))
           - jnp.exp(jnp.sum(diff_lam[2] * diff_lam[3]).astype(jnp.float32)) + lam_init)
    q_d = qd.reshape(B_, S, DIFF_HEADS, 2, DIFF_QK_DIM).transpose(0, 2, 3, 1, 4)
    k_d = kd.reshape(B_, S, DIFF_HEADS, 2, DIFF_QK_DIM).transpose(0, 2, 3, 1, 4)
    v_d = vd.reshape(B_, S, DIFF_HEADS, DIFF_V_DIM).transpose(0, 2, 1, 3)
    y_d = diff_attention(q_d, k_d, v_d, bias_table[:, MOBA_HEADS:].T, lam, subln_g, lam_init)
    y_d = y_d.transpose(0, 2, 1, 3).reshape(B_, S, BRANCH_WIDTH)

    g = jax.nn.sigmoid(gates.reshape(B_, S, N_BRANCHES, D_MODEL))
    merged = g[:, :, 0] * (y_a @ branch_proj[0])
    merged = merged + g[:, :, 1] * (y_b @ branch_proj[1])
    merged = merged + g[:, :, 2] * (y_c @ branch_proj[2])
    merged = merged + g[:, :, 3] * (y_d @ branch_proj[3])
    return merged @ w_out

def swiglu_2(h, w1, w3, w2):
    return (jax.nn.silu(h @ w1) * (h @ w3)) @ w2

def moe_swiglu(h, router, w1, w3, w2):
    logits = (h @ router).astype(jnp.float32)
    top_v, top_i = lax.top_k(logits, TOP_K_EXPERTS)
    top_w = jax.nn.softmax(top_v, axis=-1)
    out = jnp.zeros_like(h)
    for e in range(N_EXPERTS):
        gate_e = jnp.sum(jnp.where(top_i == e, top_w, 0.0), axis=-1, keepdims=True).astype(h.dtype)
        out = out + gate_e * swiglu_2(h, w1[e], w3[e], w2[e])
    return out

def second_inputs(seed: int = 0) -> dict:
    key = jax.random.key(seed)
    ks = jax.random.split(key, 20)

    def nrm(k, shape, scale):
        return jax.random.normal(k, shape, jnp.float32) * scale

    return {
        "x": nrm(ks[0], (BATCH, SEQ, D_MODEL), 1.0),
        "bias_table": nrm(ks[1], (REL_BUCKETS, N_ATTN_HEADS), 0.5),
        "mix_norm_g": 1.0 + nrm(ks[2], (DEPTH, D_MODEL), 0.05),
        "w_in": nrm(ks[3], (DEPTH, D_MODEL, W_IN_WIDTH), D_MODEL ** -0.5),
        "conv_w": nrm(ks[4], (DEPTH, CONV_WIDTH, BRANCH_WIDTH), CONV_WIDTH ** -0.5),
        "pool_w": nrm(ks[5], (DEPTH, len(POOL_WINDOWS), POOL_GROUP, POOL_GROUP), POOL_GROUP ** -0.5),
        "pool_scale": 1.0 + nrm(ks[6], (DEPTH, BRANCH_WIDTH), 0.1),
        "diff_lambda": nrm(ks[7], (DEPTH, 4, DIFF_QK_DIM), 0.1),
        "diff_subln_g": 1.0 + nrm(ks[8], (DEPTH, DIFF_V_DIM), 0.05),
        "branch_proj": nrm(ks[9], (DEPTH, N_BRANCHES, BRANCH_WIDTH, D_MODEL), BRANCH_WIDTH ** -0.5),
        "w_out": nrm(ks[10], (DEPTH, D_MODEL, D_MODEL), D_MODEL ** -0.5),
        "ffn_norm_g": 1.0 + nrm(ks[11], (DEPTH, D_MODEL), 0.05),
        "dense_w1": nrm(ks[12], (N_DENSE, D_MODEL, D_FF_DENSE), D_MODEL ** -0.5),
        "dense_w3": nrm(ks[13], (N_DENSE, D_MODEL, D_FF_DENSE), D_MODEL ** -0.5),
        "dense_w2": nrm(ks[14], (N_DENSE, D_FF_DENSE, D_MODEL), D_FF_DENSE ** -0.5),
        "moe_router": nrm(ks[15], (N_MOE, D_MODEL, N_EXPERTS), D_MODEL ** -0.5),
        "moe_w1": nrm(ks[16], (N_MOE, N_EXPERTS, D_MODEL, D_FF_EXPERT), D_MODEL ** -0.5),
        "moe_w3": nrm(ks[17], (N_MOE, N_EXPERTS, D_MODEL, D_FF_EXPERT), D_MODEL ** -0.5),
        "moe_w2": nrm(ks[18], (N_MOE, N_EXPERTS, D_FF_EXPERT, D_MODEL), D_FF_EXPERT ** -0.5),
        "final_norm_g": 1.0 + nrm(ks[19], (D_MODEL,), 0.05),
    }

def second_block(x, bias_table, mix_norm_g, w_in, conv_w, pool_w, pool_scale, diff_lambda,
              diff_subln_g, branch_proj, w_out, ffn_norm_g, dense_w1, dense_w3, dense_w2,
              moe_router, moe_w1, moe_w3, moe_w2, final_norm_g):
    for i in range(DEPTH):
        h = rmsnorm(x, mix_norm_g[i])
        x = x + token_mixers(h, w_in[i], conv_w[i], pool_w[i], pool_scale[i], diff_lambda[i],
                             diff_subln_g[i], branch_proj[i], w_out[i], bias_table, i)
        h = rmsnorm(x, ffn_norm_g[i])
        if i % 2 == 0:
            j = i // 2
            x = x + swiglu_2(h, dense_w1[j], dense_w3[j], dense_w2[j])
        else:
            j = i // 2
            x = x + moe_swiglu(h, moe_router[j], moe_w1[j], moe_w3[j], moe_w2[j])
    return rmsnorm(x, final_norm_g)


def setup_inputs(seed=0):
    out = dict(first_inputs(seed))
    for name, value in second_inputs(seed + 1).items():
        if name != "x":
            out[name + "_2"] = value
    return out


def reference(
    x, positions, ln1, ln2, w_in, fox_bf, fox_qn, fox_kn, gla_w2, gla_b, gla_norm, ret_norm,
    ssd_conv_w, ssd_conv_b, ssd_dt_bias, ssd_a_log, ssd_d, ssd_norm, w_up_a, w_up_b, w_up_c,
    w_up_d, w_out, w_ffn_in, w_ffn_out, bias_table_2, mix_norm_g_2, w_in_2, conv_w_2, pool_w_2,
    pool_scale_2, diff_lambda_2, diff_subln_g_2, branch_proj_2, w_out_2, ffn_norm_g_2,
    dense_w1_2, dense_w3_2, dense_w2_2, moe_router_2, moe_w1_2, moe_w3_2, moe_w2_2,
    final_norm_g_2,
):
    x = first_block(
        x, positions, ln1, ln2, w_in, fox_bf, fox_qn, fox_kn, gla_w2, gla_b, gla_norm, ret_norm,
        ssd_conv_w, ssd_conv_b, ssd_dt_bias, ssd_a_log, ssd_d, ssd_norm, w_up_a, w_up_b, w_up_c,
        w_up_d, w_out, w_ffn_in, w_ffn_out,
    )
    return second_block(
        x, bias_table_2, mix_norm_g_2, w_in_2, conv_w_2, pool_w_2, pool_scale_2, diff_lambda_2,
        diff_subln_g_2, branch_proj_2, w_out_2, ffn_norm_g_2, dense_w1_2, dense_w3_2,
        dense_w2_2, moe_router_2, moe_w1_2, moe_w3_2, moe_w2_2, final_norm_g_2,
    )


_drawn_inputs = setup_inputs


def setup_inputs(seed=0):
    import zlib

    import numpy as np

    out = dict(_drawn_inputs(seed))
    spreads = {}
    factors = {'fox_qn': 3.825,
     'fox_kn': 5.695,
     'gla_norm': 2.858,
     'ret_norm': 2.851,
     'ssd_conv_b': 3.059,
     'diff_lambda_2': 2.89,
     'ssd_norm': 2.985,
     'diff_subln_g_2': 3.668,
     'pool_scale_2': 2.999,
     'ffn_norm_g_2': 2.861}
    for name, (base, spread) in spreads.items():
        noise = np.random.default_rng([zlib.crc32(name.encode()), seed]).standard_normal(out[name].shape)
        drawn = base * np.exp(spread * noise) if base else spread * noise
        out[name] = jnp.asarray(drawn.astype(out[name].dtype))
    for name, factor in factors.items():
        out[name] = (out[name] * factor).astype(out[name].dtype)
    return out
```

```python
import math
from contextlib import ExitStack

import numpy as np
import concourse.bass as bass
from concourse import mybir

F32 = mybir.dt.float32
F32R = mybir.dt.float32r
I32 = mybir.dt.int32
U32 = mybir.dt.uint32
ALU = mybir.AluOpType
ACT = mybir.ActivationFunctionType
AX = mybir.AxisListType.X

P = 128
D = 1024
S = 256
KT = D // P
NT = S // P
L1 = 2
HD = 64
RH = 4
FH1 = 2816
FH2 = 3584
NE = 8
FB = 256
BLK = 512
RAW = 6
HI = 3
BIG = 3.0e38
NEG = -1.0e30

U1 = dict(fq=0, fk=256, fv=512, gq=768, gk=1024, gv=1280, gr=1536, rq=1792, rk=2048, rv=2304, rg=2560, z=2816, xbc=3328)
W1RUNS = [[(0, 512)], [(512, 256), (772, 256)], [(1028, 512)]] + [[(1556 + 512 * i, 512)] for i in range(5)] \
    + [[(4124 + 512 * i, 512)] for i in range(8)]
W1SMALL = [(1540, 16), (768, 4), (4116, 8)]
U2 = dict(qa=0, ka=256, va=512, xb=768, bb=1024, cb=1280, pc=1536, qd=1792, kd=2048, vd=2304)
W2RUNS = [[(512 * i, 512)] for i in range(13)]

CST = {}


def constants():
    a = np.arange(P)
    j, t = a[:, None], a[None, :]
    parts = [
        ("ident", (j == t) * 1.0),
        ("triu", (j <= t) * 1.0),
        ("ones", np.ones((P, P))),
        ("after", (j > t) * 1.0),
        ("trimid", (j <= t) * 1.0 - (j <= 63) * 1.0),
        ("clamp", np.concatenate([(j <= t) * BIG, np.full((P, P), BIG), (j <= t) * BIG], 1)),
        ("negmask", (t > j) * NEG),
        ("rel", np.concatenate([np.where(t >= j, t - j, 1e30), P + t - j], 1)),
        ("flip", (j + t == P - 1) * 1.0),
        ("half", (j // 64 == np.arange(2)[None]) * 1.0),
        ("halfs", (j // 64 == np.arange(2)[None]) * 0.125),
        ("quarter", (j // 32 == np.arange(4)[None]) * 32 ** -0.5),
        ("experts", np.zeros((P, 1)) + np.arange(NE)[None]),
        ("freq", np.zeros((P, 1)) + (np.float32(10000.0) ** (-np.arange(32, dtype=np.float32) / np.float32(32)))[None]),
    ]
    at = 0
    for name, m in parts:
        CST[name] = (at, m.shape[1])
        at += m.shape[1]
    return np.concatenate([m.astype(np.float32) for _, m in parts], 1)


def bias_buckets():
    d = 255 - np.arange(384)
    n = np.maximum(d, 0)
    nf = np.maximum(n, 16).astype(np.float32)
    large = 16 + (np.log(nf / np.float32(16)) / np.float32(math.log(8.0)) * np.float32(16)).astype(np.int32)
    bucket = np.where(n < 16, n, np.minimum(large, 31))
    return np.concatenate([(bucket[None] == np.arange(32)[:, None]) * 1.0, (d < 0)[None] * NEG], 0).astype(np.float32)


def pool_matrices():
    s, t = np.arange(S)[:, None], np.arange(S)[None]
    out = []
    for w in (2, 4, 8, 16):
        m = ((s <= t) & (s > t - w)) / np.minimum(t + 1, w) - (s == t)
        out.append(np.concatenate([m[:P, :], m[P:, P:]], 1))
    return np.stack(out, 1).astype(np.float32)


constants()


G1 = {
    0: [("small", [0])], 1: [("glrT", [1])], 2: [("zg", [2])],
    4: [("fqk", [0, 1])], 5: [("cum", [2, 3])],
    6: [("fs0", [0]), ("fs1", [1])], 7: [("fs2", [2]), ("fs3", [3])],
    8: [("ft0", [0]), ("ft1", [1])], 9: [("ft2", [2]), ("ft3", [3])],
    10: [("fy", [0])], 11: [("gt", [1, 2, 3])],
    13: [(f"gs{h}", [h]) for h in range(4)], 15: [("gy", [0])],
    16: [("rt", [1, 3])], 18: [(f"rs{h}", [h]) for h in range(4)], 20: [("ry", [0])],
    21: [("xt", [1, 2, 3])], 24: [("xs", [0, 1]), ("cb", [2, 3])],
    26: [(f"sg{h}", [h]) for h in range(4)], 28: [("sy0", [0])],
    29: [(f"sg{h + 4}", [h]) for h in range(4)], 31: [("sy1", [0])],
}
G2 = {
    2: [("aqk", [0, 1])], 3: [(f"as{h}", [h]) for h in range(4)], 5: [(f"at{h}", [h]) for h in range(4)],
    6: [("cx", [0, 1])], 7: [("ay", [2])], 8: [("pl", [0, 1])], 9: [("py", [2])],
    10: [("dqk", [0, 1])], 12: [(f"ds{i}", [i]) for i in range(4)], 14: [("dt0", [0]), ("dt1", [1])], 15: [("dy0", [2])],
    17: [(f"ds{i + 4}", [i]) for i in range(4)], 19: [("dt2", [0]), ("dt3", [1])], 20: [("dy1", [2])],
}


def program(nc, a, out, stop=99):
    ctx = ExitStack()
    with ctx:
        ctx.enter_context(nc.allow_non_contiguous_dma("small parameters"))

        room = nc.sbuf_bytes_remaining - 64 
        room -= room % 64
        base = nc.sbuf_base 
        ctx.enter_context(nc.sbuf_tensor("slab", [P, room // 4], F32))
        top = [base + (-base) % 64]

        def sb(name, shape, dtype=F32, at=None):
            size = int(np.prod(shape[1:])) * 4
            if at is None:
                at = top[0]
                top[0] += size + (-size) % 32
                assert top[0] <= base + room, (name, top[0] - base, room)
            return nc.alloc_sbuf_tensor_at(name, shape, dtype, offset=at)

        ring_at = top[0]
        raw = sb("raw", [P, RAW, 2048])
        lo = sb("w_lo", [P, RAW, 2048], F32R, at=ring_at)
        hi = sb("w_hi", [P, HI, 2048], F32R)
        xhi = sb("xhi", [P, 10, S], F32R)
        xlo = sb("xlo", [P, 10, S], F32R)
        x = sb("x", [P, NT, D])
        u_at = top[0]
        u = sb("u", [P, NT, 4096])
        g_at = top[0]
        gates = sb("gates", [P, NT, 4096])
        ghi = sb("ghi", [P, 2, NT, P], F32R, at=u_at)
        glo = sb("glo", [P, 2, NT, P], F32R, at=u_at + 2048)
        silu = sb("silu", [P, NT, FB], at=u_at + 4096)
        gprod = sb("gprod", [P, NT, FB], at=u_at + 6144)
        hrow = sb("hrow", [P, NT, D], at=g_at)
        rope_t = sb("rope_t", [P, 3, NT, 8, 32], at=g_at + 8192)
        sq = sb("sq", [P, NT, 512], at=g_at + 16384)
        fgain = sb("fgain", [P, D], at=g_at + 16384)
        NC = max(v[0] + v[1] for v in CST.values())
        cst = sb("cst", [P, NC])

        def C(name, lo_=0, n=None):
            at, w = CST[name]
            return cst[:, at + lo_:at + (w if n is None else lo_ + n)]

        cols1 = sb("cols1", [P, L1, 60])
        cols2 = sb("cols2", [P, L1, 25])
        heads8 = sb("heads8", [P, L1, 16])
        lam_in = sb("lam_in", [P, L1, 4, 32])
        lam = sb("lam", [P, L1, 6])
        small = sb("small", [P, 64])
        epst = sb("epst", [P, 2])
        conv2 = sb("conv2", [P, L1, 6])
        nstat = sb("nstat", [P, 8])
        type1_at = top[0]
        brow = sb("brow", [1, L1, 28])
        wsm = sb("wsm", [P, L1, KT, 28])
        gw2 = sb("gw2", [17, L1, 256])
        rot = sb("rot", [P, 2, NT, 32])
        glrT = sb("glrT", [17, S])
        z = sb("z", [P, NT, 268])
        dtv = sb("dtv", [P, NT, 8])
        E_at = top[0]
        E = sb("E", [P, 6, 256])
        zlog = sb("zlog", [P, NT, 268], at=E_at)
        tg = sb("tg", [P, NT, 256], at=E_at)
        ysq = sb("ysq", [P, NT, 256], at=E_at + 2048)
        tgz = sb("tgz", [P, NT, 512], at=E_at)
        us = sb("us", [P, NT, P], at=top[0])
        Bld = sb("Bld", [P, 4, 384])
        Pm = sb("Pm", [P, 4, 384])
        kT = sb("kT", [P, 2, S])
        qM = sb("qM", [P, 2, 2, S])
        kE_at = top[0]
        kE = sb("kE", [P, 2, P])
        qD = sb("qD", [P, 2, 2, P])
        cbm = sb("cbm", [P, 2, 384], at=kE_at)
        type1_end = top[0]
        top[0] = type1_at
        router = sb("router", [P, KT, NE])
        wgrp = sb("wgrp", [64, L1, 4, 64])
        biasT = sb("biasT", [P, 8, S])
        poolw = sb("poolw", [P, 4, 384])
        tab = sb("tab", [33, 8])
        tabT = sb("tabT", [8, 384])
        P2m = sb("P2m", [P, 4, 384])
        kT2 = sb("kT2", [P, 2, S])
        qM2 = sb("qM2", [P, 4, 2, S])
        type2_end = top[0]
        top[0] = max(type1_end, type2_end)
        ybT = sb("ybT", [P, 2, S], at=u_at + 4 * 2560)
        plT = sb("plT", [64, 4, S], at=u_at + 4 * 2560 + 2048)
        onehot = sb("onehot", [33, 384], at=g_at + 24576)
        ang = sb("ang", [P, 4, NT, 32], at=g_at + 24576)
        posi = sb("posi", [P, NT], I32, at=g_at + 28672)
        posf = sb("posf", [P, NT], at=g_at + 28672 + 64)
        gate8 = sb("gate8", [P, NT, 8])
        m8 = sb("m8", [P, NT, 8])
        i8 = sb("i8", [P, NT, 8], U32)
        i8f = sb("i8f", [P, NT, 2])
        lg8 = sb("lg8", [P, NT, 8])
        top2 = sb("top2", [P, NT, 4])
        if top[0] > base + room:
            raise ValueError("SBUF")

        bank = [ctx.enter_context(nc.psum_tensor(f"bank{i}", [P, 512], F32)) for i in range(8)]
        X = [4, 5, 6, 7]
        scratch = nc.dram_tensor("bias_rows", (8, 384), F32, kind="Internal").ap()

        def sem(name):
            return ctx.enter_context(nc.semaphore(name))

        full = [sem(f"bank_full{i}") for i in range(8)]
        free = [sem(f"bank_free{i}") for i in range(8)]
        raw_full = [sem(f"raw_full{i}") for i in range(RAW)]
        hi_ready = sem("hi_ready")
        lo_ready = sem("lo_ready")
        w_used = sem("w_used")
        x_loaded, cst_loaded, par_loaded = sem("x_loaded"), sem("cst_loaded"), sem("par_loaded")
        par2_loaded, rows_out, bias_in, fgain_in, stored = (sem(n) for n in
            ("par2_loaded", "bias_rows_out", "bias_in", "final_gain_in", "stored"))
        setup_v, setup_s, setup2_v = sem("setup_vector"), sem("setup_scalar"), sem("setup2_vector")
        norm_ss, norm_rstd, norm_h, norm_hi = sem("norm_sumsq"), sem("norm_rstd"), sem("norm_rows"), sem("norm_hi")
        silu_done, ghi_done = sem("silu_done"), sem("gated_hi")
        route_m, route_e, routed = sem("route_max"), sem("route_exp"), sem("routed")
        dve_link, act_link, pool_link = sem("vector_link"), sem("scalar_link"), sem("pool_link")
        STEPS = dict(z_abs=1, z_log=1, decay=1, fox_ss=1, fox_rstd=1, fox_qn=1, builds=12, fox_max=4,
                     gla_prod=1, gla_p=4, gate_exp=2, br_ss=3, br_rstd=3, y_gla=1, y_ret=1, rope=1, ret_decay=4,
                     conv_out=3, conv_exp=3, xbc=3, ssd_c=1, ssd_x=1, cb=1, ssd_p=8, ssd_dx=2, z_exp=1, y_ssd=1,
                     gate_one=8, y_hi=5, merged=12, m_hi=4,
                     moba_max=4, conv_in=1, dif_max=8, dif_p=4, d_ss=1, d_rstd=1, y_dif=1, y_conv=1,
                     gate_one_b=8, y_hi_b=4, merged_b=12, m_hi_b=4)
        T = {name: sem(name) for name in STEPS}

        def at(name, l, n=1):
            return l * STEPS[name] + n

        uses, fulls = [0] * 8, [0] * 8
        USE, FULL, CH, FFB = {}, {}, {}, {}

        def claim(key, *banks, streamed=False):
            for b in banks:
                uses[b] += 1
                USE[key, b] = uses[b]
                if not streamed:
                    fulls[b] += 1
                    FULL[key, b] = fulls[b]

        phases = []
        for l in range(L1):
            phases += [("norm", l, "mix1"), ("mix1", l), ("norm", l, "ffn1"), ("ffn1", l)]
        for l in range(L1):
            f = "ffn2" if l == 0 else "moe"
            phases += [("norm", l, "mix2"), ("mix2", l), ("norm", l, f), (f, l)]
        phases = phases[:2 * stop]
        c = ffb = 0
        XREADY = []
        last_x = None
        for k in phases:
            XREADY.append(last_x)
            if k[0] == "norm":
                for i in range(4):
                    claim(k, X[i])
                continue
            CH[k] = c
            if k[0] in ("mix1", "mix2"):
                nb, groups, ny = (16, G1, 5) if k[0] == "mix1" else (13, G2, 4)
                if k[0] == "mix2" and k[1] == 0:
                    claim("bias_rows", X[0])
                for pos in range(2 * nb):
                    if pos % 2 == 0:
                        claim((k, "gemm", pos // 2), *(2 * (pos // 2 % 2) + t for t in range(NT)), streamed=True)
                    for g, bs in groups.get(pos, []):
                        claim((k, g), *(X[b] for b in bs))
                for i in range(ny):
                    claim((k, "yT", i), X[i % 4])
                for br in range(4):
                    claim((k, "up", br), *((0, 1, 2, 3) if br % 2 == 0 else X), streamed=True)
                for i in range(4):
                    claim((k, "mT", i), X[i])
                claim((k, "out"), 0, 1, 2, 3, streamed=True)
                c += 2 * nb + ny + 4
                last_x = [(b, USE[(k, "out"), b] + 1) for b in range(4)]
            else:
                J = FFJ[k[0]]
                FFB[k] = ffb
                if k[0] == "moe":
                    claim((k, "router"), X[0])
                for e in range(NE if k[0] == "moe" else 1):
                    for j in range(J):
                        for t in range(NT):
                            claim((k, e, "U", j), 2 * (j % 2) + t, streamed=True)
                            claim((k, e, "T", j), 2 * (j % 2) + t)
                    claim((k, e, "D"), *X, streamed=True)
                    c += 3 * J
                    ffb += 2 * J
                last_x = [(b, USE[(k, e, "D"), b] + 1) for b in X]
        END = c
        MOE0 = CH.get(("moe", 1), END)

        def use(key, b):
            return USE[key, b]

        def ev(key, b):
            return USE[key, b] + 1

        def fl(key, b):
            return FULL[key, b]

        def gbank(n, t):
            return 2 * (n % 2) + t

        def walk(eng, J, u0, tr, u1, dn):
            u0(0, 0, 0)
            u1(0, 0, 1)
            u0(1, 0, 2)
            tr(0, 0)
            u1(1, 0, 3)
            dn(0, 0, 4)
            n = (J - 3) // 2
            with eng.Fori(0, n) as it:
                for j in (1, 2):
                    u0(j + 1, it, 2 + 3 * j)
                    tr(j, it)
                    u1(j + 1, it, 3 + 3 * j)
                    dn(j, it, 4 + 3 * j)
            for j in range(1 + 2 * n, J - 1):
                u0(j + 1, 0, 2 + 3 * j)
                tr(j, 0)
                u1(j + 1, 0, 3 + 3 * j)
                dn(j, 0, 4 + 3 * j)
            tr(J - 1, 0)
            dn(J - 1, 0, 3 * J - 1)

        block = ctx.enter_context(nc.Block())

        @block.sync
        def _(sp):
            def slot(c, it=0, eo=0, per=0):
                if c >= RAW:
                    sp.wait_ge(w_used, c - RAW + 1 + 6 * it + per * eo)
                return c % RAW

            def columns(c, w, k0, runs):
                s = slot(c)
                dst = raw[:, s, :].rearrange("p (k n) -> p k n", k=4)
                src = w.rearrange("(k p) n -> p k n", p=P)[:, k0:k0 + 4]
                if len(runs) == 1:
                    (f, n), = runs
                    sp.dma_start(dst[:, 0:2], src[:, 0:2, f:f + n]).then_inc(raw_full[s], 16)
                    sp.dma_start(dst[:, 2:4], src[:, 2:4, f:f + n]).then_inc(raw_full[s], 16)
                else:
                    for i, (f, n) in enumerate(runs):
                        sp.dma_start(dst[:, :, 256 * i:256 * i + n], src[:, :, f:f + n]).then_inc(raw_full[s], 16)

            def rows(c, w, k0):
                s = slot(c)
                for i in range(2):
                    sp.dma_start(raw[:, s, 1024 * i:1024 * i + 1024],
                                 w[(k0 + i) * P:(k0 + i + 1) * P, :]).then_inc(raw_full[s], 16)

            def feed_forward(c0, J, wa, wb, wd, eo=0, per=0):
                va, vb = (w.rearrange("(k p) n -> p k n", p=P) for w in (wa, wb))

                def up(j, it, c, k0):
                    s = slot(c0 + c, it, eo, per)
                    dst = raw[:, s, :].rearrange("p (k n) -> p k n", k=4)
                    f = j * FB + it * (2 * FB)
                    sp.dma_start(dst[:, :, 0:FB], va[:, k0:k0 + 4, bass.ds(f, FB)]).then_inc(raw_full[s], 16)
                    sp.dma_start(dst[:, :, FB:2 * FB], vb[:, k0:k0 + 4, bass.ds(f, FB)]).then_inc(raw_full[s], 16)

                def down(j, it, c):
                    s = slot(c0 + c, it, eo, per)
                    for i in range(2):
                        f = j * FB + i * P + it * (2 * FB)
                        sp.dma_start(raw[:, s, 1024 * i:1024 * i + 1024], wd[bass.ds(f, P), :]).then_inc(raw_full[s], 16)

                walk(sp, J, lambda j, it, c: up(j, it, c, 0), lambda j, it: None,
                     lambda j, it, c: up(j, it, c, 4), down)

            for k in phases:
                if k[0] == "norm":
                    continue
                c0, l = CH[k], k[1]
                if k[0] in ("mix1", "mix2"):
                    w, runs, ups, wo = ((a["w_in"][l], W1RUNS, [a["w_up_a"][l], a["w_up_b"][l], a["w_up_c"][l], a["w_up_d"][l]],
                                         a["w_out"][l]) if k[0] == "mix1" else
                                        (a["w_in_2"][l], W2RUNS, [a["branch_proj_2"][l, i] for i in range(4)], a["w_out_2"][l]))
                    for n, run in enumerate(runs):
                        columns(c0, w, 0, run)
                        columns(c0 + 1, w, 4, run)
                        c0 += 2
                    for wu in ups:
                        for k0 in range(0, wu.shape[0] // P, 2):
                            rows(c0, wu, k0)
                            c0 += 1
                    for k0 in range(0, KT, 2):
                        rows(c0, wo, k0)
                        c0 += 1
                elif k[0] == "ffn1":
                    feed_forward(c0, FFJ[k[0]], a["w_ffn_in"][l][:, 0:FH1], a["w_ffn_in"][l][:, FH1:2 * FH1], a["w_ffn_out"][l])
                elif k[0] == "ffn2":
                    feed_forward(c0, FFJ[k[0]], a["dense_w1_2"][0], a["dense_w3_2"][0], a["dense_w2_2"][0])
                else:
                    J = FFJ[k[0]]
                    with sp.Fori(0, NE) as e:
                        feed_forward(c0, J, a["moe_w1_2"][0][bass.ds(e, 1)].rearrange("a k n -> (a k) n"),
                                     a["moe_w3_2"][0][bass.ds(e, 1)].rearrange("a k n -> (a k) n"),
                                     a["moe_w2_2"][0][bass.ds(e, 1)].rearrange("a k n -> (a k) n"), e, 3 * J)
            sp.wait_ge(norm_h, 2 * len([k for k in phases if k[0] == "norm"]) + 2)
            sp.dma_start(out.rearrange("(t p) n -> p t n", p=P), hrow[:, :, :]).then_inc(stored, 16)
            sp.wait_ge(stored, 16)

        @block.tensor
        def _(pe):
            mm = nc.tensor.matmul
            ident = C("ident")

            def tr(dst, src):
                return nc.tensor.transpose(dst, src, ident)

            def gemm_half(banks, c, k0, start, stop, it=0, eo=0, per=0):
                s, h = c % RAW, c % HI
                pe.wait_ge(lo_ready, c + 1 + 6 * it + per * eo)
                for k in range(4):
                    for t in range(NT):
                        tok = slice(t * P, t * P + P)
                        wh, wl = (w[:, i, k * 512:k * 512 + 512] for w, i in ((hi, h), (lo, s)))
                        mm(bank[banks[t]][:, :], xhi[:, k0 + k, tok], wh, start=start and k == 0, stop=False)
                        mm(bank[banks[t]][:, :], xlo[:, k0 + k, tok], wh, start=False, stop=False)
                        last = mm(bank[banks[t]][:, :], xhi[:, k0 + k, tok], wl, start=False, stop=stop and k == 3)
                last.then_inc(w_used, 1)

            def gemm_rows(banks, c, lhs, first, final, it=0, eo=0, per=0):
                s, h = c % RAW, c % HI
                pe.wait_ge(lo_ready, c + 1 + 6 * it + per * eo)
                for k in range(2):
                    for t in range(NT):
                        xh, xl = lhs(k, t)
                        for n in range(2):
                            b = bank[banks[2 * t + n]][:, :]
                            o = k * 1024 + n * 512
                            mm(b, xh, hi[:, h, o:o + 512], start=first and k == 0, stop=False)
                            mm(b, xl, hi[:, h, o:o + 512], start=False, stop=False)
                            last = mm(b, xh, lo[:, s, o:o + 512], start=False, stop=final and k == 1)
                last.then_inc(w_used, 1)

            def xt(kt):
                return lambda k, t: (xhi[:, kt + k, t * P:t * P + P], xlo[:, kt + k, t * P:t * P + P])

            def transposes_to(key, b, srcs):
                pe.wait_ge(free[b], use(key, b))
                for i, src in enumerate(srcs):
                    last = tr(bank[b][:, i * P:(i + 1) * P], src)
                last.then_inc(full[b], 1)

            def norm(k, n):
                pe.wait_ge(norm_h, 2 * n + 2)
                for i in range(4):
                    transposes_to(k, X[i], [hrow[:, t, (2 * i + kk) * P:(2 * i + kk + 1) * P] for kk in range(2) for t in range(NT)])

            def values(key, b, off, heads, pblk, v0):
                for h in range(heads):
                    v = [u[:, t, v0 + h * HD:v0 + h * HD + HD] for t in range(NT)]
                    mm(bank[b][:, h * HD:h * HD + HD], pblk(h)[:, 0:P], v[0], start=True, stop=True)
                    mm(bank[b][:, 256 + h * HD:256 + h * HD + HD], pblk(h)[:, P:2 * P], v[0], start=True, stop=False)
                    last = mm(bank[b][:, 256 + h * HD:256 + h * HD + HD], pblk(h)[:, 2 * P:3 * P], v[1], start=False, stop=True)
                last.then_inc(full[b], 1)

            def gemm_waits(k, n):
                for t in range(NT):
                    pe.wait_ge(free[gbank(n, t)], ev((k, "gemm", n), gbank(n, t)))

            def attend1(k, pos):
                l = k[1]
                if pos == 0:
                    b, key = X[0], (k, "small")
                    pe.wait_ge(free[b], use(key, b))
                    if l == 0:
                        pe.wait_ge(par_loaded, 16 * NPAR)
                        pe.wait_ge(setup_v, 1)
                    for t in range(NT):
                        o = bank[b][:, t * 32:t * 32 + 28]
                        for kt in range(KT):
                            for j, xx in enumerate((xhi, xlo)):
                                mm(o, xx[:, kt, t * P:t * P + P].bitcast(F32), wsm[:, l, kt, :], start=kt == 0 and j == 0, stop=False)
                        last = mm(o, C("ones")[0:1, :], brow[0:1, l, :], start=False, stop=True)
                    last.then_inc(full[b], 1)
                elif pos == 1:
                    pe.wait_ge(free[X[0]], ev((k, "small"), X[0]))
                    transposes_to((k, "glrT"), X[1], [us[:, t, :] for t in range(NT)])
                elif pos == 2:
                    b, key = X[2], (k, "zg")
                    pe.wait_ge(free[X[1]], ev((k, "glrT"), X[1]))
                    pe.wait_ge(free[b], use(key, b))
                    for t in range(NT):
                        last = mm(bank[b][:, t * 256:t * 256 + 256], glrT[0:17, t * P:t * P + P], gw2[0:17, l, :], start=True, stop=True)
                    last.then_inc(full[b], 1)
                elif pos == 4:
                    pe.wait_ge(T["fox_qn"], at("fox_qn", l))
                    for i, o in ((0, U1["fq"]), (1, U1["fk"])):
                        transposes_to((k, "fqk"), X[i], [u[:, t, o + p * P:o + p * P + P] for p in range(2) for t in range(NT)])
                elif pos == 5:
                    pe.wait_ge(T["decay"], at("decay", l))
                    for i, mats in ((0, ("after", "trimid")), (1, ("trimid", "triu"))):
                        b = X[2 + i]
                        pe.wait_ge(free[b], use((k, "cum"), b))
                        for j, m in enumerate(mats):
                            last = mm(bank[b][:, j * 256:j * 256 + 256], C(m), z[:, i, 0:256], start=True, stop=True)
                        last.then_inc(full[b], 1)
                elif pos in (6, 7):
                    for h in (0, 1) if pos == 6 else (2, 3):
                        key, b, o = (k, f"fs{h}"), X[h], bank[X[h]]
                        pe.wait_ge(free[b], use(key, b))
                        for i in range(2):
                            pe.wait_ge(free[X[i]], ev((k, "fqk"), X[i]))
                        pe.wait_ge(T["builds"], at("builds", l, h + 1))
                        q, kk = qM[:, h % 2, h // 2, :], kT[:, h // 2, :]
                        mm(o[:, 0:P], q[:, 0:P], kk[:, 0:P], start=True, stop=False)
                        mm(o[:, 0:P], C("triu"), Bld[:, h, 0:P], start=False, stop=False)
                        mm(o[:, 0:P], ident, C("negmask"), start=False, stop=True)
                        mm(o[:, P:3 * P], q[:, P:2 * P], kk, start=True, stop=False)
                        mm(o[:, P:3 * P], C("triu"), Bld[:, h, P:3 * P], start=False, stop=False)
                        mm(o[:, P:2 * P], C("ones"), Bld[:, h, 0:P], start=False, stop=False)
                        mm(o[:, 2 * P:3 * P], ident, C("negmask"), start=False, stop=True).then_inc(full[b], 1)
                elif pos in (8, 9):
                    for h in (0, 1) if pos == 8 else (2, 3):
                        pe.wait_ge(free[X[h]], ev((k, f"fs{h}"), X[h]))
                        transposes_to((k, f"ft{h}"), X[h], [Pm[:, h, i * P:i * P + P] for i in range(3)])
                elif pos == 10:
                    for h in range(4):
                        pe.wait_ge(free[X[h]], ev((k, f"ft{h}"), X[h]))
                    values((k, "fy"), X[0], 0, 4, lambda h: Pm[:, h, :], U1["fv"])
                elif pos == 11:
                    pe.wait_ge(T["gla_prod"], at("gla_prod", l))
                    for i, es in ((1, ((2, 0), (4, 0), (2, 1), (4, 1))), (2, ((0, 0), (0, 1), (5, 0), (5, 1))),
                                  (3, ((1, 0), (3, 0), (1, 1), (3, 1)))):
                        transposes_to((k, "gt"), X[i], [E[:, e, p * P:p * P + P] for e, p in es])
                elif pos == 13:
                    for i in (1, 2, 3):
                        pe.wait_ge(free[X[i]], ev((k, "gt"), X[i]))
                    for h in range(4):
                        key, b, o, p, m = (k, f"gs{h}"), X[h], bank[X[h]], h // 2, h % 2
                        pe.wait_ge(free[b], use(key, b))
                        mm(o[:, 0:P], kT[:, p, 0:P], qM[:, m, p, 0:P], start=True, stop=True)
                        mm(o[:, P:2 * P], kE[:, p, :], qD[:, m, p, :], start=True, stop=True)
                        mm(o[:, 2 * P:3 * P], kT[:, p, P:2 * P], qM[:, m, p, P:2 * P], start=True, stop=True).then_inc(full[b], 1)
                elif pos == 15:
                    pe.wait_ge(free[X[0]], use((k, "gy"), X[0]))
                    pe.wait_ge(T["gla_p"], at("gla_p", l, 4))
                    values((k, "gy"), X[0], 0, 4, lambda h: Pm[:, h, :], U1["gv"])
                elif pos == 16:
                    pe.wait_ge(T["rope"], at("rope", l))
                    for i, o in ((1, U1["rk"]), (3, U1["rq"])):
                        transposes_to((k, "rt"), X[i], [u[:, t, o + p * P:o + p * P + P] for p in range(2) for t in range(NT)])
                elif pos == 18:
                    for i in (1, 3):
                        pe.wait_ge(free[X[i]], ev((k, "rt"), X[i]))
                    for h in range(4):
                        key, b, o, p, m = (k, f"rs{h}"), X[h], bank[X[h]], h // 2, h % 2
                        pe.wait_ge(free[b], use(key, b))
                        mm(o[:, 0:2 * P], kT[:, p, 0:P], qM[:, m, p, :], start=True, stop=True)
                        mm(o[:, 2 * P:3 * P], kT[:, p, P:2 * P], qM[:, m, p, P:2 * P], start=True, stop=True).then_inc(full[b], 1)
                elif pos == 20:
                    for h in range(4):
                        pe.wait_ge(free[X[h]], ev((k, f"rs{h}"), X[h]))
                    values((k, "ry"), X[0], 0, 4, lambda h: Pm[:, h, :], U1["rv"])
                elif pos == 21:
                    gemm_waits(k, 6)
                    gemm_waits(k, 7)
                    for i in range(3):
                        transposes_to((k, "xt"), X[1 + i], [u[:, t, U1["xbc"] + (2 * i + j) * P:U1["xbc"] + (2 * i + j + 1) * P]
                                                            for j in range(2) for t in range(NT)])
                elif pos == 24:
                    pe.wait_ge(T["xbc"], at("xbc", l, 3))
                    for t in range(NT):
                        transposes_to((k, "xs"), X[t], [E[:, i, t * P:t * P + P] for i in range(4)])
                    pe.wait_ge(T["ssd_c"], at("ssd_c", l))
                    for g in range(2):
                        b, o = X[2 + g], bank[X[2 + g]]
                        pe.wait_ge(free[b], use((k, "cb"), b))
                        mm(o[:, 0:2 * P], E[:, 4, 0:P], kT[:, g, :], start=True, stop=True)
                        mm(o[:, 2 * P:3 * P], E[:, 4, P:2 * P], kT[:, g, P:2 * P], start=True, stop=True).then_inc(full[b], 1)
                elif pos in (26, 29):
                    for h in range(4) if pos == 26 else range(4, 8):
                        key, b = (k, f"sg{h}"), X[h % 4]
                        o, i = bank[b], h % 4
                        pe.wait_ge(free[b], use(key, b))
                        pe.wait_ge(T["builds"], at("builds", l, 5 + h))
                        mm(o[:, 0:2 * P], Bld[:, i, 0:P], C("triu", 0, 2 * P), start=True, stop=False)
                        mm(o[:, P:2 * P], Bld[:, i, P:2 * P], C("triu"), start=False, stop=True)
                        mm(o[:, 2 * P:3 * P], Bld[:, i, 2 * P:3 * P], C("triu"), start=True, stop=True).then_inc(full[b], 1)
                elif pos in (28, 31):
                    r = 0 if pos == 28 else 1
                    pe.wait_ge(free[X[0]], use((k, f"sy{r}"), X[0]))
                    pe.wait_ge(T["ssd_x"], at("ssd_x", l))
                    pe.wait_ge(T["ssd_p"], at("ssd_p", l, 4 * r + 4))
                    values((k, f"sy{r}"), X[0], 0, 4, lambda h: Pm[:, h, :], 256 + 256 * r)

            def softmax_scores(k, key, b, q, kk, head):
                o = bank[b]
                pe.wait_ge(free[b], use(key, b))
                mm(o[:, 0:P], q[:, 0:P], kk[:, 0:P], start=True, stop=False)
                mm(o[:, 0:P], C("flip"), biasT[:, head, P:2 * P], start=False, stop=True)
                mm(o[:, P:3 * P], q[:, P:2 * P], kk, start=True, stop=False)
                mm(o[:, P:3 * P], C("flip"), biasT[:, head, :], start=False, stop=True).then_inc(full[b], 1)

            def attend2(k, pos):
                l = k[1]
                if pos == 2:
                    gemm_waits(k, 0)
                    for i, o in ((0, U2["qa"]), (1, U2["ka"])):
                        transposes_to((k, "aqk"), X[i], [u[:, t, o + p * P:o + p * P + P] for p in range(2) for t in range(NT)])
                elif pos == 3:
                    for i in range(2):
                        pe.wait_ge(free[X[i]], ev((k, "aqk"), X[i]))
                    if l == 0:
                        pe.wait_ge(bias_in, 16)
                    for h in range(4):
                        softmax_scores(k, (k, f"as{h}"), X[h], qM2[:, h % 2, h // 2, :], kT2[:, h // 2, :], h)
                elif pos == 5:
                    for h in range(4):
                        pe.wait_ge(free[X[h]], ev((k, f"as{h}"), X[h]))
                        transposes_to((k, f"at{h}"), X[h], [P2m[:, h, i * P:i * P + P] for i in range(3)])
                elif pos == 6:
                    pe.wait_ge(T["conv_in"], at("conv_in", l))
                    for i, o in ((0, U2["cb"]), (1, U2["bb"])):
                        transposes_to((k, "cx"), X[i], [u[:, t, o + p * P:o + p * P + P] for p in range(2) for t in range(NT)])
                elif pos == 7:
                    pe.wait_ge(free[X[2]], use((k, "ay"), X[2]))
                    for h in range(4):
                        pe.wait_ge(free[X[h]], ev((k, f"at{h}"), X[h]))
                    values((k, "ay"), X[2], 0, 4, lambda h: P2m[:, h, :], U2["va"])
                elif pos == 8:
                    gemm_waits(k, 3)
                    if l == 0:
                        pe.wait_ge(par2_loaded, 16 * NPAR2)
                    for b_ in range(2):
                        b = X[b_]
                        pe.wait_ge(free[b], use((k, "pl"), b))
                        for gg in range(2):
                            g = 2 * b_ + gg
                            o = bank[b][0:64, gg * 256:gg * 256 + 256]
                            us_ = [u[:, t, U2["pc"] + g * 64:U2["pc"] + g * 64 + 64] for t in range(NT)]
                            mm(o, us_[0], poolw[:, g, 0:256], start=True, stop=False)
                            last = mm(o[:, P:2 * P], us_[1], poolw[:, g, 256:384], start=False, stop=True)
                        last.then_inc(full[b], 1)
                elif pos == 9:
                    b, key = X[2], (k, "py")
                    for i in range(2):
                        pe.wait_ge(free[X[i]], ev((k, "pl"), X[i]))
                    pe.wait_ge(free[b], use(key, b))
                    for t in range(NT):
                        for g in range(4):
                            last = mm(bank[b][:, t * 256 + g * 64:t * 256 + g * 64 + 64], plT[:, g, t * P:t * P + P],
                                      wgrp[:, l, g, :], start=True, stop=True)
                    last.then_inc(full[b], 1)
                elif pos == 10:
                    gemm_waits(k, 4)
                    for i, o in ((0, U2["qd"]), (1, U2["kd"])):
                        transposes_to((k, "dqk"), X[i], [u[:, t, o + p * P:o + p * P + P] for p in range(2) for t in range(NT)])
                elif pos in (12, 17):
                    r = 0 if pos == 12 else 1
                    for i in range(2):
                        pe.wait_ge(free[X[i]], ev((k, "dqk"), X[i]))
                    for i in range(4):
                        softmax_scores(k, (k, f"ds{4 * r + i}"), X[i], qM2[:, i, r, :], kT2[:, r, :], 4 + 2 * r + i // 2)
                elif pos in (14, 19):
                    r = 0 if pos == 14 else 1
                    for i in range(2):
                        pe.wait_ge(T["dif_p"], at("dif_p", l, 2 * r + i + 1))
                        transposes_to((k, f"dt{2 * r + i}"), X[i], [P2m[:, 2 * i, j * P:j * P + P] for j in range(3)])
                elif pos in (15, 20):
                    r = 0 if pos == 15 else 1
                    b = X[2]
                    pe.wait_ge(free[b], use((k, f"dy{r}"), b))
                    for i in range(2):
                        pe.wait_ge(free[X[i]], ev((k, f"dt{2 * r + i}"), X[i]))
                    values((k, f"dy{r}"), b, 0, 2, lambda h: P2m[:, 2 * h, :], U2["vd"] + 128 * r)

            def mixer(k):
                c0, l = CH[k], k[1]
                first = k[0] == "mix1"
                nb, attend, ny = (16, attend1, 5) if first else (13, attend2, 4)
                for i in range(4):
                    pe.wait_ge(free[X[i]], ev(("norm", l, k[0]), X[i]))
                if k == ("mix2", 0):
                    pe.wait_ge(par2_loaded, 16 * NPAR2)
                    pe.wait_ge(setup2_v, 1)
                    pe.wait_ge(free[X[0]], use("bias_rows", X[0]))
                    mm(bank[X[0]][0:8, 0:384], tab[0:33, :], onehot[0:33, :], start=True, stop=True).then_inc(full[X[0]], 1)
                for pos in range(2 * nb):
                    n, half = divmod(pos, 2)
                    banks = [gbank(n, t) for t in range(NT)]
                    if half == 0:
                        for b in banks:
                            pe.wait_ge(free[b], use((k, "gemm", n), b))
                    gemm_half(banks, c0 + pos, 4 * half, half == 0, half == 1)
                    attend(k, pos)
                if first:
                    ys = [U1["fq"] + i * P for i in range(2)] + [U1["gq"] + i * P for i in range(2)] \
                        + [U1["rq"] + i * P for i in range(2)] + [U1["xbc"] + i * P for i in range(4)]
                    pe.wait_ge(free[X[0]], ev((k, "fy"), X[0]))
                    pe.wait_ge(T["y_gla"], at("y_gla", l))
                    pe.wait_ge(T["y_ret"], at("y_ret", l))
                else:
                    ys = [U2["qa"] + i * P for i in range(2)] + [None, None] + [U2["pc"] + i * P for i in range(2)] \
                        + [U2["qd"] + i * P for i in range(2)]
                    pe.wait_ge(free[X[2]], ev((k, "ay"), X[2]))
                    pe.wait_ge(free[X[2]], ev((k, "py"), X[2]))
                    pe.wait_ge(T["y_dif"], at("y_dif", l))
                for i in range(ny):
                    if first and i == 3:
                        pe.wait_ge(T["y_ssd"], at("y_ssd", l))
                    if not first and i == 1:
                        b = X[i % 4]
                        pe.wait_ge(T["y_conv"], at("y_conv", l))
                        pe.wait_ge(free[b], use((k, "yT", i), b))
                        mm(bank[b][:, :], ident, ybT[:, :, :].rearrange("p a b -> p (a b)"), start=True, stop=True).then_inc(full[b], 1)
                    else:
                        transposes_to((k, "yT", i), X[i % 4], [u[:, t, ys[2 * i + j]:ys[2 * i + j] + P] for j in range(2) for t in range(NT)])
                c = c0 + 2 * nb
                kt = 0
                for br in range(4):
                    banks = (0, 1, 2, 3) if br % 2 == 0 else X
                    tiles = 4 if first and br == 3 else 2
                    for b in banks:
                        pe.wait_ge(free[b], use((k, "up", br), b))
                    for j in range(0, tiles, 2):
                        i = kt // 2
                        pe.wait_ge(free[X[i % 4]], ev((k, "yT", i), X[i % 4]))
                        gemm_rows(banks, c, xt(kt), j == 0, j == tiles - 2)
                        c += 1
                        kt += 2
                name = "merged" if first else "merged_b"
                pe.wait_ge(T[name], at(name, l, 12))
                for i in range(4):
                    transposes_to((k, "mT", i), X[i], [u[:, t, (2 * i + j) * P:(2 * i + j + 1) * P] for j in range(2) for t in range(NT)])
                for b in range(4):
                    pe.wait_ge(free[b], use((k, "out"), b))
                for i in range(4):
                    pe.wait_ge(free[X[i]], ev((k, "mT", i), X[i]))
                    gemm_rows((0, 1, 2, 3), c, xt(2 * i), i == 0, i == 3)
                    c += 1

            def feed_forward(k, J, eo=0):
                c0, per = CH[k], 3 * J
                for i in range(4):
                    pe.wait_ge(free[X[i]], ev(("norm", k[1], k[0]), X[i]))

                def up(j, it, c, half):
                    banks = [gbank(j, t) for t in range(NT)]
                    if half == 0:
                        for b in banks:
                            pe.wait_ge(free[b], use((k, 0, "U", j), b) + 2 * it + J * eo)
                    gemm_half(banks, c0 + c, 4 * half, half == 0, half == 1, it, eo, per)

                def turn(j, it):
                    for t in range(NT):
                        b = gbank(j, t)
                        pe.wait_ge(free[b], use((k, 0, "T", j), b) + 2 * it + J * eo)
                        tr(bank[b][:, 0:P], gprod[:, t, 0:P])
                        tr(bank[b][:, P:2 * P], gprod[:, t, P:2 * P]).then_inc(full[b], 1)

                def down(j, it, c):
                    if j == 0:
                        for b in X:
                            pe.wait_ge(free[b], use((k, 0, "D"), b) + eo)
                    for t in range(NT):
                        b = gbank(j, t)
                        pe.wait_ge(free[b], ev((k, 0, "T", j), b) + 2 * it + J * eo)
                    gemm_rows(X, c0 + c, lambda kk, t: (ghi[:, kk, t, :], glo[:, kk, t, :]), j == 0, j == J - 1, it, eo, per)

                walk(pe, J, lambda j, it, c: up(j, it, c, 0), turn, lambda j, it, c: up(j, it, c, 1), down)

            pe.wait_ge(cst_loaded, 16)
            n = 0
            for k in phases:
                if k[0] == "norm":
                    norm(k, n)
                    n += 1
                elif k[0] in ("mix1", "mix2"):
                    mixer(k)
                elif k[0] != "moe":
                    feed_forward(k, FFJ[k[0]])
                else:
                    b, key = X[0], (k, "router")
                    for i in range(4):
                        pe.wait_ge(free[X[i]], ev(("norm", k[1], "moe"), X[i]))
                    for t in range(NT):
                        for kt in range(KT):
                            for j, xx in enumerate((xhi, xlo)):
                                last = mm(bank[b][:, t * 8:t * 8 + 8], xx[:, kt, t * P:t * P + P].bitcast(F32), router[:, kt, :],
                                          start=kt == 0 and j == 0, stop=kt == KT - 1 and j == 1)
                    last.then_inc(full[b], 1)
                    with pe.Fori(0, NE) as e:
                        feed_forward(k, FFJ["moe"], e)

        @block.scalar
        def _(act):
            links = [0]

            def link(ins):
                links[0] += 1
                ins.then_inc(act_link, 1)
                act.wait_ge(act_link, links[0])

            def go(dst, src, f, **kw):
                return nc.scalar.activation(dst, src, f, **kw)

            def conv(c, it=0, eo=0, per=0):
                if c >= END or (c >= MOE0 and not per):
                    return
                act.wait_ge(raw_full[c % RAW], 32 * (c // RAW + 1) + 32 * it + 32 * (per // RAW) * eo)
                if c >= HI:
                    act.wait_ge(w_used, c - HI + 1 + 6 * it + per * eo)
                go(hi[:, c % HI, :], raw[:, c % RAW, :], ACT.Copy).then_inc(hi_ready, 1)

            def rsqrt(dst, src, n, eps, done):
                link(go(dst, src, ACT.Ln, scale=1.0 / n, bias=eps))
                go(dst, dst, ACT.Exp, scale=-0.5).then_inc(done, 1)

            def norm(k, n, ready):
                for b, v in ready or []:
                    act.wait_ge(free[b], v)
                for t in range(NT):
                    last = go(hrow[:, t, :], x[:, t, :], ACT.Square, accum_out=nstat[:, t:t + 1])
                link(last)
                rsqrt(nstat[:, 4:6], nstat[:, 0:2], D, eps1, norm_rstd)
                if k[2] is None:
                    return
                for i in range(4):
                    b = X[i]
                    act.wait_ge(full[b], fl(k, b))
                    for j in range(2):
                        kt = 2 * i + j
                        last = go(xhi[:, kt, :], bank[b][:, j * 256:j * 256 + 256], ACT.Copy, scale=gain_col(k, kt))
                    last.then_inc(norm_hi, 1)

            def gain_col(k, kt):
                l, f = k[1], k[2]
                return cols1[:, l, kt:kt + 1] if f == "mix1" else cols1[:, l, 8 + kt:9 + kt] if f == "ffn1" \
                    else cols2[:, l, kt:kt + 1] if f == "mix2" else cols2[:, l, 8 + kt:9 + kt]

            def softmax_exp(key, b, h, dst, max_sem, max_val):
                act.wait_ge(max_sem, max_val)
                go(dst[:, 0:P], bank[b][:, 0:P], ACT.Exp, bias=small[:, 16 + 2 * h:17 + 2 * h], accum_out=small[:, 32 + h:33 + h])
                go(dst[:, P:3 * P], bank[b][:, P:3 * P], ACT.Exp, bias=small[:, 17 + 2 * h:18 + 2 * h],
                   accum_out=small[:, 36 + h:37 + h]).then_inc(free[b], 1)

            def evac(key, b, dst, src, f=ACT.Copy, **kw):
                go(dst, src, f, **kw).then_inc(free[b], 1)

            def gemm_out(k, n):
                first = k[0] == "mix1"
                mixb = 8 if first else 5
                act.wait_ge(w_used, CH[k] + 2 * n + 2)
                for t in range(NT):
                    b = gbank(n, t)
                    if n < mixb:
                        evac((k, "gemm", n), b, u[:, t, n * 512:n * 512 + 512], bank[b][:, :])
                    else:
                        o = (n - mixb) * 512
                        evac((k, "gemm", n), b, gates[:, t, o:o + 512], bank[b][:, :], ACT.Exp, scale=-1.0)

            def wait_full(key, b):
                act.wait_ge(full[b], fl(key, b))

            def own_gemm(k, n):
                for t in range(NT):
                    act.wait_ge(free[gbank(n, t)], ev((k, "gemm", n), gbank(n, t)))

            def work1(k, pos):
                l = k[1]
                if pos % 2 == 1:
                    gemm_out(k, pos // 2)
                if pos == 0:
                    wait_full((k, "small"), X[0])
                    evac(0, X[0], us[:, :, 0:28], bank[X[0]][:, 0:64].rearrange("p (t n) -> p t n", t=2)[:, :, 0:28])
                elif pos == 1:
                    wait_full((k, "glrT"), X[1])
                    evac(0, X[1], glrT[0:16, :], bank[X[1]][0:16, 0:256])
                elif pos == 2:
                    act.wait_ge(T["z_abs"], at("z_abs", l))
                    link(go(zlog[:, :, :], zlog[:, :, :], ACT.Exp, scale=-1.0))
                    go(zlog[:, :, :], zlog[:, :, :], ACT.Ln, bias=1.0).then_inc(T["z_log"], 1)
                    act.wait_ge(T["fox_ss"], at("fox_ss", l))
                    rsqrt(small[:, 0:16], small[:, 0:16], HD, eps1, T["fox_rstd"])
                elif pos == 4:
                    wait_full((k, "fqk"), X[1])
                    evac(0, X[1], kT[:, :, :].rearrange("p a b -> p (a b)"), bank[X[1]][:, :], scale=cols1[:, l, 27:28])
                    wait_full((k, "fqk"), X[0])
                    for m in range(2):
                        last = go(qM[:, m].rearrange("p a b -> p (a b)"), bank[X[0]][:, :], ACT.Copy, scale=cols1[:, l, 58 + m:59 + m])
                    last.then_inc(free[X[0]], 1)
                elif pos == 5:
                    for i in range(2):
                        b = X[2 + i]
                        wait_full((k, "cum"), b)
                        for j, (e, o, sc) in enumerate([(0, 0, 1.0), (1, 256, 1.0), (2, 256, -1.0)] if i == 0 else
                                                       [(3, 0, 1.0), (4, 0, -1.0), (5, 256, 1.0)]):
                            last = go(E[:, e, :], bank[b][:, o:o + 256], ACT.Exp, scale=sc)
                        last.then_inc(free[b], 1)
                elif pos in (6, 7):
                    for h in (0, 1) if pos == 6 else (2, 3):
                        softmax_exp((k, f"fs{h}"), X[h], h, Pm[:, h, :], T["fox_max"], at("fox_max", l, h + 1))
                elif pos in (8, 9):
                    h = 1 if pos == 8 else 3
                    wait_full((k, f"ft{h}"), X[h])
                    evac(0, X[h], Pm[:, h, :], bank[X[h]][:, 0:384])
                elif pos == 11:
                    wait_full((k, "gt"), X[1])
                    evac(0, X[1], kT[:, :, :].rearrange("p a b -> p (a b)"), bank[X[1]][:, :])
                    wait_full((k, "gt"), X[3])
                    for m in range(2):
                        last = go(qM[:, m].rearrange("p a b -> p (a b)"), bank[X[3]][:, :], ACT.Copy, scale=C("halfs", m, 1))
                    last.then_inc(free[X[3]], 1)
                elif pos == 12:
                    own_gemm(k, 3)
                    wait_full((k, "gt"), X[2])
                    wait_full((k, "gt"), X[3])
                    go(tg[:, :, :], u[:, :, U1["gr"]:U1["gr"] + 256], ACT.Exp, scale=-1.0).then_inc(T["gate_exp"], 1)
                elif pos == 15:
                    act.wait_ge(T["br_ss"], at("br_ss", l, 1))
                    rsqrt(small[:, 48:56], small[:, 48:56], HD, eps1, T["br_rstd"])
                elif pos == 16:
                    wait_full((k, "rt"), X[1])
                    evac(0, X[1], kT[:, :, :].rearrange("p a b -> p (a b)"), bank[X[1]][:, :])
                    wait_full((k, "rt"), X[3])
                    for m in range(2):
                        last = go(qM[:, m].rearrange("p a b -> p (a b)"), bank[X[3]][:, :], ACT.Copy, scale=C("halfs", m, 1))
                    last.then_inc(free[X[3]], 1)
                elif pos == 17:
                    act.wait_ge(T["y_gla"], at("y_gla", l))
                    go(tg[:, :, :], u[:, :, U1["rg"]:U1["rg"] + 256], ACT.Exp, scale=-1.0).then_inc(T["gate_exp"], 1)
                    for h in (0, 1):
                        go(decay_tile(h), C("rel"), ACT.Exp, scale=LOG_GAMMA[h]).then_inc(T["ret_decay"], 1)
                elif pos == 18:
                    for h in (2, 3):
                        act.wait_ge(free[X[h - 2]], ev((k, f"rs{h - 2}"), X[h - 2]))
                        go(decay_tile(h), C("rel"), ACT.Exp, scale=LOG_GAMMA[h]).then_inc(T["ret_decay"], 1)
                elif pos == 20:
                    act.wait_ge(T["br_ss"], at("br_ss", l, 2))
                    rsqrt(small[:, 48:56], small[:, 48:56], HD, eps1, T["br_rstd"])
                elif pos in (21, 22, 23):
                    i = pos - 21
                    act.wait_ge(T["conv_out"], at("conv_out", l, i + 1))
                    go(qM[:, i % 2], E[:, 2 * i:2 * i + 2, :], ACT.Exp, scale=-1.0).then_inc(T["conv_exp"], 1)
                elif pos == 24:
                    for t in range(NT):
                        wait_full((k, "xs"), X[t])
                        evac(0, X[t], u[:, t, U1["xbc"]:U1["xbc"] + 512], bank[X[t]][:, :])
                elif pos == 25:
                    for g in range(2):
                        wait_full((k, "cb"), X[2 + g])
                    go(tgz[:, :, :], u[:, :, U1["z"]:U1["z"] + 512], ACT.Exp, scale=-1.0).then_inc(T["z_exp"], 1)
                elif pos in (26, 29):
                    for h in range(4) if pos == 26 else range(4, 8):
                        wait_full((k, f"sg{h}"), X[h % 4])
                        evac(0, X[h % 4], Pm[:, h % 4, :], bank[X[h % 4]][:, 0:384], ACT.Exp)
                elif pos == 31:
                    act.wait_ge(T["br_ss"], at("br_ss", l, 3))
                    rsqrt(small[:, 48:52], small[:, 48:52], 256, eps1, T["br_rstd"])

            def decay_tile(h):
                return qD[:, h % 2].rearrange("p a b -> p (a b)")

            def work2(k, pos):
                l = k[1]
                if pos % 2 == 1:
                    gemm_out(k, pos // 2)
                if pos in (2, 10):
                    key = (k, "aqk" if pos == 2 else "dqk")
                    wait_full(key, X[1])
                    evac(0, X[1], kT2[:, :, :].rearrange("p a b -> p (a b)"), bank[X[1]][:, :])
                    wait_full(key, X[0])
                    for m in range(2 if pos == 2 else 4):
                        last = go(qM2[:, m].rearrange("p a b -> p (a b)"), bank[X[0]][:, :], ACT.Copy,
                                  scale=C("halfs", m, 1) if pos == 2 else C("quarter", m, 1))
                    last.then_inc(free[X[0]], 1)
                elif pos == 3:
                    for h in range(4):
                        softmax_exp((k, f"as{h}"), X[h], h, P2m[:, h, :], T["moba_max"], at("moba_max", l, h + 1))
                elif pos == 5:
                    for h in (1, 3):
                        wait_full((k, f"at{h}"), X[h])
                        evac(0, X[h], P2m[:, h, :], bank[X[h]][:, 0:384])
                elif pos == 8:
                    for i in range(2):
                        wait_full((k, "pl"), X[i])
                        evac(0, X[i], plT[:, 2 * i:2 * i + 2, :].rearrange("p a b -> p (a b)"), bank[X[i]][0:64, :])
                elif pos == 9:
                    wait_full((k, "py"), X[2])
                    evac(0, X[2], u[:, :, U2["pc"]:U2["pc"] + 256], bank[X[2]][:, :].rearrange("p (t n) -> p t n", t=2))
                elif pos in (12, 17):
                    r = 0 if pos == 12 else 1
                    for i in range(4):
                        softmax_exp((k, f"ds{4 * r + i}"), X[i], i, P2m[:, i, :], T["dif_max"], at("dif_max", l, 4 * r + i + 1))
                elif pos in (14, 19):
                    r = 0 if pos == 14 else 1
                    i = 1
                    wait_full((k, f"dt{2 * r + i}"), X[i])
                    evac(0, X[i], P2m[:, 2 * i, :], bank[X[i]][:, 0:384])
                elif pos == 21:
                    act.wait_ge(T["d_ss"], at("d_ss", l))
                    rsqrt(small[:, 48:56], small[:, 48:56], HD, eps2, T["d_rstd"])

            def hi_tiles(k, what, i, name, l, ycol):
                b = X[i % 4]
                wait_full((k, what, i), b)
                for j in range(2):
                    kt = 2 * i + j
                    kw = dict(scale=ycol[:, kt:kt + 1]) if ycol is not None else {}
                    last = go(xhi[:, kt, :], bank[b][:, j * 256:j * 256 + 256], ACT.Copy, **kw)
                last.then_inc(T[name], 1)

            def mixer(k):
                c0, l = CH[k], k[1]
                first = k[0] == "mix1"
                nb, work, ny = (16, work1, 5) if first else (13, work2, 4)
                for pos in range(2 * nb):
                    conv(c0 + pos + 2)
                    work(k, pos)
                yc = cols1[:, l, 16:26] if first else cols2[:, l, 17:25]
                for i in range(ny):
                    hi_tiles(k, "yT", i, "y_hi" if first else "y_hi_b", l, yc)
                for pos in range(2 * nb, 2 * nb + ny):
                    conv(c0 + pos + 2)
                for i in range(4):
                    hi_tiles(k, "mT", i, "m_hi" if first else "m_hi_b", l, None)
                for pos in range(2 * nb + ny, 2 * nb + ny + 4):
                    conv(c0 + pos + 2)

            def feed_forward(k, J, eo=0):
                c0, per, f0 = CH[k], 3 * J, FFB[k]

                def up_done(j, it, c):
                    conv_in_expert(c, it)
                    for t in range(NT):
                        b = gbank(j, t)
                        act.wait_ge(w_used, c0 + c + 1 + 6 * it + per * eo)
                        go(silu[:, t, :], bank[b][:, 0:FB], ACT.Silu).then_inc(silu_done, 1)

                def conv_in_expert(c, it):
                    if k[0] != "moe" or c + 2 < per:
                        conv(c0 + c + 2, it, eo, per)

                def turn(j, it):
                    for t in range(NT):
                        b = gbank(j, t)
                        act.wait_ge(full[b], fl((k, 0, "T", j), b) + it + (J // 2) * eo)
                        go(ghi[:, :, t, :], bank[b][:, 0:FB].rearrange("p (a b) -> p a b", a=2), ACT.Copy).then_inc(ghi_done, 1)

                if k[0] == "moe":
                    conv(c0, 0, eo, per)
                    conv(c0 + 1, 0, eo, per)
                walk(act, J, lambda j, it, c: conv_in_expert(c, it), turn, up_done, lambda j, it, c: conv_in_expert(c, it))

            eps1, eps2 = epst[:, 0:1], epst[:, 1:2]
            act.wait_ge(setup_v, 1)
            for i in range(2):
                last = go(rot[:, i], ang[:, i], ACT.Sin)
            for l in range(L1):
                last = go(heads8[:, l, 0:8], heads8[:, l, 0:8], ACT.Exp)
            last.then_inc(setup_s, 1)
            act.wait_ge(x_loaded, 16)
            conv(0)
            conv(1)
            n = 0
            for k, ready in zip(phases, XREADY):
                if k[0] == "norm":
                    norm(k, n, ready)
                    n += 1
                elif k[0] in ("mix1", "mix2"):
                    if k == ("mix2", 0):
                        act.wait_ge(setup2_v, 1)
                        go(lam[:, :, 0:2], lam[:, :, 0:2], ACT.Exp).then_inc(setup_s, 1)
                    mixer(k)
                elif k[0] != "moe":
                    feed_forward(k, FFJ[k[0]])
                else:
                    act.wait_ge(route_m, 1)
                    for t in range(NT):
                        last = go(top2[:, t, 0:1], m8[:, t, 1:2], ACT.Exp, bias=top2[:, t, 1:2])
                    last.then_inc(route_e, 1)
                    with act.Fori(0, NE) as e:
                        feed_forward(k, FFJ["moe"], e)
            norm(("norm", 0, None), n, last_x)

        @block.vector
        def _(dve):
            links = [0]
            V = nc.vector

            def link(ins):
                links[0] += 1
                ins.then_inc(dve_link, 1)
                dve.wait_ge(dve_link, links[0])

            def conv(c, it=0, eo=0, per=0):
                if c >= END or (c >= MOE0 and not per):
                    return
                dve.wait_ge(hi_ready, c + 1 + 6 * it + per * eo)
                V.tensor_tensor(lo[:, c % RAW, :], raw[:, c % RAW, :], hi[:, c % HI, :].bitcast(F32),
                                ALU.subtract).then_inc(lo_ready, 1)

            def lo_tiles(b, hi_sem, hi_val, i, gain):
                dve.wait_ge(hi_sem, hi_val)
                for j in range(2):
                    kt = 2 * i + j
                    src = bank[b][:, j * 256:j * 256 + 256]
                    g = gain(kt)
                    last = V.scalar_tensor_tensor(out=xlo[:, kt, :], in0=src, scalar=g, in1=xhi[:, kt, :].bitcast(F32),
                                                  op0=ALU.mult, op1=ALU.subtract)
                last.then_inc(free[b], 1)

            def norm(k, n):
                l, f = k[1], k[2]
                dve.wait_ge(norm_rstd, n + 1)
                for t in range(NT):
                    if f is None:
                        if t == 0:
                            dve.wait_ge(fgain_in, 16)
                        V.scalar_tensor_tensor(out=hrow[:, t, :], in0=x[:, t, :], scalar=nstat[:, 4 + t:5 + t], in1=fgain[:, :],
                                               op0=ALU.mult, op1=ALU.mult).then_inc(norm_h, 1)
                    else:
                        V.tensor_scalar(hrow[:, t, :], x[:, t, :], nstat[:, 4 + t:5 + t], None, ALU.mult).then_inc(norm_h, 1)
                if f is None:
                    return
                col = (lambda kt: cols1[:, l, kt:kt + 1]) if f == "mix1" else (lambda kt: cols1[:, l, 8 + kt:9 + kt]) if f == "ffn1" \
                    else (lambda kt: cols2[:, l, kt:kt + 1]) if f == "mix2" else (lambda kt: cols2[:, l, 8 + kt:9 + kt])
                for i in range(4):
                    lo_tiles(X[i], norm_hi, 4 * n + i + 1, i, col)

            def wait_full(key, b):
                dve.wait_ge(full[b], fl(key, b))

            def out_of(k, n):
                for t in range(NT):
                    dve.wait_ge(free[gbank(n, t)], ev((k, "gemm", n), gbank(n, t)))

            def maxima(key, b, h, name, l, n):
                wait_full(key, b)
                V.tensor_reduce(small[:, 16 + 2 * h:17 + 2 * h], bank[b][:, 0:P], AX, ALU.max, negate=True)
                V.tensor_reduce(small[:, 17 + 2 * h:18 + 2 * h], bank[b][:, P:3 * P], AX, ALU.max, negate=True).then_inc(T[name], 1)

            def gates_one(k, n, first):
                mixb = 8 if first else 5
                o = (n - mixb) * 512
                out_of(k, n)
                gg = gates[:, :, o:o + 512]
                link(V.tensor_scalar_add(gg, gg, 1.0))
                V.reciprocal(gg, gg).then_inc(T["gate_one" if first else "gate_one_b"], 1)

            def heads(ap, d=HD):
                return ap.rearrange("p t (h d) -> p t h d", d=d)

            def bc(ap, n):
                return ap.unsqueeze(3).to_broadcast([P, NT, ap.shape[2], n])

            def two(ap):
                return ap.rearrange("p (t n) -> p t n", t=2)

            def sumsq(yv, scr, d, stat, done):
                link(V.tensor_tensor(scr, yv, yv, ALU.mult))
                V.tensor_reduce(stat, heads(scr, d), AX, ALU.add).then_inc(done, 1)

            def gated_norm(k, key, yo, go, which, done):
                l = k[1]
                b = X[0]
                wait_full(key, b)
                yv = u[:, :, yo:yo + 256]
                V.tensor_copy(yv, two(bank[b][:, :])).then_inc(free[b], 1)
                dve.wait_ge(free[b], ev(key, b))
                sumsq(yv, ysq[:, :, :], HD, small[:, 48:56].rearrange("p (t h) -> p t h", t=2), T["br_ss"])
                dve.wait_ge(T["gate_exp"], at("gate_exp", l, which))
                link(V.tensor_scalar_add(tg[:, :, :], tg[:, :, :], 1.0))
                link(V.reciprocal(tg[:, :, :], tg[:, :, :]))
                link(V.tensor_tensor(tg[:, :, :], tg[:, :, :], u[:, :, go:go + 256], ALU.mult))
                dve.wait_ge(T["br_rstd"], at("br_rstd", l, which))
                link(V.tensor_tensor(heads(yv), heads(yv), bc(small[:, 48:56].rearrange("p (t h) -> p t h", t=2), HD), ALU.mult))
                V.tensor_tensor(yv, yv, tg[:, :, :], ALU.mult).then_inc(T[done], 1)

            def clamp_to(dst, b, key, done=None):
                wait_full(key, b)
                V.tensor_tensor(dst, bank[b][:, 0:384], C("clamp"), ALU.min).then_inc(free[b], 1)
                dve.wait_ge(free[b], ev(key, b))
                r = V.scalar_tensor_tensor(out=dst, in0=C("clamp"), scalar=-1.0, in1=dst, op0=ALU.mult, op1=ALU.max)
                if done is not None:
                    r.then_inc(done, 1)
                return r

            def work1(k, pos):
                l = k[1]
                if pos % 2 == 1 and pos >= 17:
                    gates_one(k, pos // 2, True)
                if pos == 1:
                    out_of(k, 0)
                    sumsq(u[:, :, 0:512], sq[:, :, :], HD, small[:, 0:16].rearrange("p (t h) -> p t h", t=2), T["fox_ss"])
                elif pos == 2:
                    wait_full((k, "zg"), X[2])
                    V.tensor_copy(z[:, :, 0:256], two(bank[X[2]][:, :])).then_inc(free[X[2]], 1)
                    dve.wait_ge(free[X[0]], ev((k, "small"), X[0]))
                    link(V.tensor_copy(z[:, :, 256:268], us[:, :, 16:28]))
                    V.scalar_tensor_tensor(out=zlog[:, :, :], in0=z[:, :, :], scalar=-1.0, in1=z[:, :, :], op0=ALU.mult,
                                           op1=ALU.max).then_inc(T["z_abs"], 1)
                elif pos == 3:
                    dve.wait_ge(T["z_log"], at("z_log", l))
                    V.scalar_tensor_tensor(out=dtv[:, :, :], in0=z[:, :, 260:268], scalar=0.0, in1=zlog[:, :, 260:268],
                                           op0=ALU.max, op1=ALU.add)
                    link(V.scalar_tensor_tensor(out=z[:, :, 0:260], in0=z[:, :, 0:260], scalar=0.0, in1=zlog[:, :, 0:260],
                                                op0=ALU.min, op1=ALU.subtract))
                    V.tensor_scalar(z[:, :, 0:256], z[:, :, 0:256], 1.0 / 16.0, None, ALU.mult)
                    if l == 0:
                        dve.wait_ge(setup_s, 1)
                    V.scalar_tensor_tensor(out=z[:, :, 260:268], in0=dtv[:, :, :], scalar=-1.0,
                                           in1=heads8[:, l, 0:8].unsqueeze(1).to_broadcast([P, NT, 8]), op0=ALU.mult,
                                           op1=ALU.mult).then_inc(T["decay"], 1)
                    dve.wait_ge(T["fox_rstd"], at("fox_rstd", l))
                    q = heads(u[:, :, 0:512])
                    V.tensor_tensor(q, q, bc(small[:, 0:16].rearrange("p (t h) -> p t h", t=2), HD), ALU.mult).then_inc(T["fox_qn"], 1)
                elif pos in (6, 7):
                    for h in (0, 1) if pos == 6 else (2, 3):
                        maxima((k, f"fs{h}"), X[h], h, "fox_max", l, h + 1)
                    if pos == 6:
                        for i in (2, 3):
                            dve.wait_ge(free[X[i]], ev((k, "cum"), X[i]))
                        out_of(k, 1)
                        out_of(k, 2)
                        for e, t, o in ((2, 0, "gk"), (0, 0, "gk"), (1, 0, "gq"), (4, 1, "gk"), (3, 1, "gq"), (5, 1, "gq")):
                            last = V.tensor_tensor(E[:, e, :], E[:, e, :], u[:, t, U1[o]:U1[o] + 256], ALU.mult)
                        last.then_inc(T["gla_prod"], 1)
                elif pos in (8, 9):
                    h = 0 if pos == 8 else 2
                    wait_full((k, f"ft{h}"), X[h])
                    V.tensor_copy(Pm[:, h, :], bank[X[h]][:, 0:384]).then_inc(free[X[h]], 1)
                elif pos == 10:
                    for h in range(4):
                        dve.wait_ge(free[X[h]], ev((k, f"fs{h}"), X[h]))
                    link(V.reciprocal(small[:, 40:48], small[:, 32:40]))
                    wait_full((k, "fy"), X[0])
                    V.tensor_tensor(heads(u[:, :, 0:256]), heads(two(bank[X[0]][:, :])),
                                    bc(small[:, 40:48].rearrange("p (t h) -> p t h", t=2), HD), ALU.mult).then_inc(free[X[0]], 1)
                elif pos == 11:
                    b = X[2]
                    wait_full((k, "gt"), b)
                    V.tensor_copy(kE[:, :, :].rearrange("p a b -> p (a b)"), bank[b][:, 0:256])
                    for m in range(2):
                        last = V.tensor_scalar(qD[:, m].rearrange("p a b -> p (a b)"), bank[b][:, 256:512], C("halfs", m, 1), None, ALU.mult)
                    last.then_inc(free[b], 1)
                elif pos == 13:
                    for h in range(4):
                        clamp_to(Pm[:, h, :], X[h], (k, f"gs{h}"), T["gla_p"])
                elif pos == 15:
                    gated_norm(k, (k, "gy"), U1["gq"], U1["gr"], 1, "y_gla")
                elif pos == 18:
                    for h in range(4):
                        b, r = X[h], qD[:, h % 2].rearrange("p a b -> p (a b)")
                        wait_full((k, f"rs{h}"), b)
                        dve.wait_ge(T["ret_decay"], at("ret_decay", l, h + 1))
                        V.tensor_tensor(Pm[:, h, 0:256], bank[b][:, 0:256], r, ALU.mult)
                        V.tensor_tensor(Pm[:, h, 256:384], bank[b][:, 256:384], r[:, 0:P], ALU.mult).then_inc(free[b], 1)
                elif pos == 20:
                    gated_norm(k, (k, "ry"), U1["rq"], U1["rg"], 2, "y_ret")
                elif pos in (21, 22, 23):
                    i = pos - 21
                    b = X[1 + i]
                    wait_full((k, "xt"), b)
                    cw = lambda tap, j: cols1[:, l, 28 + 6 * tap + j:29 + 6 * tap + j]
                    src = [bank[b][:, j * 256:j * 256 + 256] for j in range(2)]
                    for j in range(2):
                        last = V.tensor_scalar(E[:, 2 * i + j, :], src[j], cw(3, 2 * i + j), cols1[:, l, 52 + 2 * i + j:53 + 2 * i + j],
                                               ALU.mult, ALU.add)
                    link(last)
                    for sh in (1, 2, 3):
                        for j in range(2):
                            dst = E[:, 2 * i + j, sh:S]
                            last = V.scalar_tensor_tensor(out=dst, in0=src[j][:, 0:S - sh], scalar=cw(3 - sh, 2 * i + j), in1=dst,
                                                          op0=ALU.mult, op1=ALU.add)
                        if sh < 3:
                            link(last)
                    last.then_inc(free[b], 1)
                    dve.wait_ge(free[b], ev((k, "xt"), b))
                    V.memset(small[:, 60:61], 0.0).then_inc(T["conv_out"], 1)
                    dve.wait_ge(T["conv_exp"], at("conv_exp", l, i + 1))
                    e = qM[:, i % 2]
                    link(V.tensor_scalar_add(e, e, 1.0))
                    link(V.reciprocal(e, e))
                    xx = E[:, 2 * i:2 * i + 2, :]
                    V.tensor_tensor(xx, xx, e, ALU.mult).then_inc(T["xbc"], 1)
                    if pos == 23:
                        dve.wait_ge(T["xbc"], at("xbc", l, 3))
                        for g in range(2):
                            last = V.tensor_scalar(kT[:, g, :], E[:, 5, :], C("half", g, 1), None, ALU.mult)
                        last.then_inc(T["ssd_c"], 1)
                elif pos == 24:
                    for g in range(2):
                        link(clamp_to(cbm[:, g, :], X[2 + g], (k, "cb")))
                    for t in range(NT):
                        dve.wait_ge(free[X[t]], ev((k, "xs"), X[t]))
                    V.tensor_tensor(heads(u[:, :, 256:768]), heads(u[:, :, U1["xbc"]:U1["xbc"] + 512]), bc(dtv[:, :, :], HD),
                                    ALU.mult).then_inc(T["ssd_x"], 1)
                elif pos in (26, 29):
                    for h in range(4) if pos == 26 else range(4, 8):
                        dve.wait_ge(free[X[h % 4]], ev((k, f"sg{h}"), X[h % 4]))
                        V.tensor_tensor(Pm[:, h % 4, :], Pm[:, h % 4, :], cbm[:, h // 4, :], ALU.mult).then_inc(T["ssd_p"], 1)
                    if pos == 26:
                        dve.wait_ge(T["z_exp"], at("z_exp", l))
                        link(V.tensor_scalar_add(tgz[:, :, :], tgz[:, :, :], 1.0))
                        link(V.reciprocal(tgz[:, :, :], tgz[:, :, :]))
                        link(V.tensor_tensor(tgz[:, :, :], tgz[:, :, :], u[:, :, U1["z"]:U1["z"] + 512], ALU.mult))
                elif pos in (28, 31):
                    r = 0 if pos == 28 else 1
                    key, b = (k, f"sy{r}"), X[0]
                    wait_full(key, b)
                    dve.wait_ge(T["ssd_dx"], at("ssd_dx", l, r + 1))
                    V.tensor_tensor(u[:, :, U1["xbc"] + 256 * r:U1["xbc"] + 256 * r + 256], two(bank[b][:, :]), qM[:, r],
                                    ALU.add).then_inc(free[b], 1)
                    if r == 1:
                        dve.wait_ge(free[b], ev(key, b))
                        yv = u[:, :, U1["xbc"]:U1["xbc"] + 512]
                        link(V.tensor_tensor(yv, yv, tgz[:, :, :], ALU.mult))
                        scr = qM[:, :, :, :].rearrange("p a b c -> p (a b c)").rearrange("p (t n) -> p t n", t=2)
                        sumsq(yv, scr, 256, small[:, 48:52].rearrange("p (t h) -> p t h", t=2), T["br_ss"])
                        dve.wait_ge(T["br_rstd"], at("br_rstd", l, 3))
                        V.tensor_tensor(heads(yv, 256), heads(yv, 256), bc(small[:, 48:52].rearrange("p (t h) -> p t h", t=2), 256),
                                        ALU.mult).then_inc(T["y_ssd"], 1)

            def work2(k, pos):
                l = k[1]
                if pos % 2 == 1 and pos >= 11:
                    gates_one(k, pos // 2, False)
                if pos == 3:
                    for h in range(4):
                        maxima((k, f"as{h}"), X[h], h, "moba_max", l, h + 1)
                elif pos == 5:
                    for h in (0, 2):
                        wait_full((k, f"at{h}"), X[h])
                        V.tensor_copy(P2m[:, h, :], bank[X[h]][:, 0:384]).then_inc(free[X[h]], 1)
                    out_of(k, 1)
                    out_of(k, 2)
                    cx = u[:, :, U2["cb"]:U2["cb"] + 256]
                    V.tensor_tensor(cx, cx, u[:, :, U2["xb"]:U2["xb"] + 256], ALU.mult).then_inc(T["conv_in"], 1)
                elif pos == 6:
                    cw = lambda tap, j: conv2[:, l, 2 * tap + j:2 * tap + j + 1]
                    b = X[0]
                    wait_full((k, "cx"), b)
                    for j in range(2):
                        last = V.tensor_scalar(ybT[:, j, :], bank[b][:, j * 256:j * 256 + 256], cw(2, j), None, ALU.mult)
                    link(last)
                    for sh in (1, 2):
                        for j in range(2):
                            dst = ybT[:, j, sh:S]
                            last = V.scalar_tensor_tensor(out=dst, in0=bank[b][:, j * 256:j * 256 + S - sh], scalar=cw(2 - sh, j), in1=dst,
                                                          op0=ALU.mult, op1=ALU.add)
                        if sh == 1:
                            link(last)
                    last.then_inc(free[b], 1)
                    dve.wait_ge(free[b], ev((k, "cx"), b))
                    b = X[1]
                    wait_full((k, "cx"), b)
                    yb = ybT[:, :, :].rearrange("p a b -> p (a b)")
                    V.tensor_tensor(yb, yb, bank[b][:, :], ALU.mult).then_inc(free[b], 1)
                    dve.wait_ge(free[b], ev((k, "cx"), b))
                    V.memset(small[:, 60:61], 0.0).then_inc(T["y_conv"], 1)
                elif pos == 7:
                    for h in range(4):
                        dve.wait_ge(free[X[h]], ev((k, f"as{h}"), X[h]))
                    link(V.reciprocal(small[:, 40:48], small[:, 32:40]))
                    wait_full((k, "ay"), X[2])
                    V.tensor_tensor(heads(u[:, :, 0:256]), heads(two(bank[X[2]][:, :])),
                                    bc(small[:, 40:48].rearrange("p (t h) -> p t h", t=2), HD), ALU.mult).then_inc(free[X[2]], 1)
                elif pos in (12, 17):
                    r = 0 if pos == 12 else 1
                    for i in range(4):
                        maxima((k, f"ds{4 * r + i}"), X[i], i, "dif_max", l, 0)
                    for i in range(4):
                        dve.wait_ge(free[X[i]], ev((k, f"ds{4 * r + i}"), X[i]))
                    link(V.reciprocal(small[:, 40:48], small[:, 32:40]))
                    for t in range(NT):
                        for i in (1, 3):
                            cc = 40 + 4 * t + i
                            last = V.tensor_scalar(small[:, cc:cc + 1], small[:, cc:cc + 1], lam[:, l, 2:3], None, ALU.mult)
                    link(last)
                    for i in range(2):
                        for t, s in ((0, slice(0, P)), (1, slice(P, 3 * P))):
                            cc = 40 + 4 * t + 2 * i + 1
                            last = V.tensor_scalar(P2m[:, 2 * i + 1, s], P2m[:, 2 * i + 1, s], small[:, cc:cc + 1], None, ALU.mult)
                        link(last)
                        for t, s in ((0, slice(0, P)), (1, slice(P, 3 * P))):
                            cc = 40 + 4 * t + 2 * i
                            last = V.scalar_tensor_tensor(out=P2m[:, 2 * i, s], in0=P2m[:, 2 * i, s], scalar=small[:, cc:cc + 1],
                                                          in1=P2m[:, 2 * i + 1, s], op0=ALU.mult, op1=ALU.add)
                        last.then_inc(T["dif_p"], 1)
                elif pos in (14, 19):
                    r = 0 if pos == 14 else 1
                    wait_full((k, f"dt{2 * r}"), X[0])
                    V.tensor_copy(P2m[:, 0, :], bank[X[0]][:, 0:384]).then_inc(free[X[0]], 1)
                elif pos in (15, 20):
                    r = 0 if pos == 15 else 1
                    b, key = X[2], (k, f"dy{r}")
                    wait_full(key, b)
                    V.tensor_copy(u[:, :, U2["qd"] + 128 * r:U2["qd"] + 128 * r + 128], two(bank[b][:, :])[:, :, 0:128]).then_inc(free[b], 1)
                    if r == 1:
                        dve.wait_ge(free[b], ev(key, b))
                        yv = u[:, :, U2["qd"]:U2["qd"] + 256]
                        sumsq(yv, qM2[:, 0], HD, small[:, 48:56].rearrange("p (t h) -> p t h", t=2), T["d_ss"])
                elif pos == 21:
                    dve.wait_ge(T["d_rstd"], at("d_rstd", l))
                    yv = heads(u[:, :, U2["qd"]:U2["qd"] + 256])
                    V.tensor_tensor(yv, yv, bc(small[:, 48:56].rearrange("p (t h) -> p t h", t=2), HD), ALU.mult).then_inc(T["y_dif"], 1)

            def mixer(k):
                c0, l = CH[k], k[1]
                first = k[0] == "mix1"
                nb, work, ny = (16, work1, 5) if first else (13, work2, 4)
                for pos in range(2 * nb):
                    conv(c0 + pos + 2)
                    work(k, pos)
                yc = cols1[:, l, 16:26] if first else cols2[:, l, 17:25]
                for i in range(ny):
                    lo_tiles(X[i % 4], T["y_hi" if first else "y_hi_b"], at("y_hi" if first else "y_hi_b", l, i + 1), i,
                             lambda kt: yc[:, kt:kt + 1])
                pos = 2 * nb
                one = "gate_one" if first else "gate_one_b"
                for br in range(4):
                    banks = (0, 1, 2, 3) if br % 2 == 0 else X
                    for j in range(2 if first and br == 3 else 1):
                        conv(c0 + pos + 2)
                        pos += 1
                    dve.wait_ge(w_used, c0 + pos)
                    dve.wait_ge(T[one], at(one, l, 2 * br + 2))
                    for t in range(NT):
                        for n in range(2):
                            b = banks[2 * t + n]
                            gg = gates[:, t, br * 1024 + n * 512:br * 1024 + n * 512 + 512]
                            dst = u[:, t, n * 512:n * 512 + 512] if br == 0 else gg
                            V.tensor_tensor(dst, bank[b][:, :], gg, ALU.mult).then_inc(free[b], 1)
                for i in range(4):
                    lo_tiles(X[i], T["m_hi" if first else "m_hi_b"], at("m_hi" if first else "m_hi_b", l, i + 1), i, lambda kt: 1.0)
                for j in range(4):
                    conv(c0 + pos + 2)
                    pos += 1
                dve.wait_ge(w_used, c0 + pos)
                for t in range(NT):
                    for n in range(2):
                        b = 2 * t + n
                        xx = x[:, t, n * 512:n * 512 + 512]
                        V.tensor_tensor(xx, bank[b][:, :], xx, ALU.add).then_inc(free[b], 1)

            def feed_forward(k, J, eo=0):
                c0, per, f0 = CH[k], 3 * J, FFB[k]

                def cv(c, it):
                    if k[0] != "moe" or c + 2 < per:
                        conv(c0 + c + 2, it, eo, per)

                def up_done(j, it, c):
                    cv(c, it)
                    for t in range(NT):
                        b = gbank(j, t)
                        dve.wait_ge(silu_done, f0 + 2 * j + t + 1 + 4 * it + 2 * J * eo)
                        V.tensor_tensor(gprod[:, t, :], bank[b][:, FB:2 * FB], silu[:, t, :], ALU.mult).then_inc(free[b], 1)

                def turn(j, it):
                    for t in range(NT):
                        b = gbank(j, t)
                        dve.wait_ge(ghi_done, f0 + 2 * j + t + 1 + 4 * it + 2 * J * eo)
                        V.tensor_tensor(glo[:, :, t, :], bank[b][:, 0:FB].rearrange("p (a b) -> p a b", a=2),
                                        ghi[:, :, t, :].bitcast(F32), ALU.subtract).then_inc(free[b], 1)

                if k[0] == "moe":
                    conv(c0, 0, eo, per)
                    conv(c0 + 1, 0, eo, per)
                walk(dve, J, lambda j, it, c: cv(c, it), turn, up_done, lambda j, it, c: cv(c, it))
                dve.wait_ge(w_used, c0 + per + per * eo)
                for t in range(NT):
                    for n in range(2):
                        b = X[2 * t + n]
                        xx = x[:, t, n * 512:n * 512 + 512]
                        if k[0] == "moe":
                            V.scalar_tensor_tensor(out=xx, in0=bank[b][:, :], scalar=gate8[:, t, bass.ds(eo, 1)], in1=xx,
                                                   op0=ALU.mult, op1=ALU.add).then_inc(free[b], 1)
                        else:
                            V.tensor_tensor(xx, bank[b][:, :], xx, ALU.add).then_inc(free[b], 1)

            for b in range(8):
                V.memset(small[:, 56 + b:57 + b], 0.0).then_inc(free[b], 1)
            V.memset(epst[:, 0:1], 1e-6)
            V.memset(epst[:, 1:2], 1e-5)
            V.memset(us[:, :, :], 0.0)
            V.memset(glrT[:, :], 1.0)
            V.memset(cols1[:, :, 16:18], 1.0)
            V.memset(cols2[:, :, 17:21], 1.0)
            link(V.memset(brow[:, :, 0:16], 0.0))
            dve.wait_ge(cst_loaded, 16)
            dve.wait_ge(par_loaded, 16 * NPAR)
            link(V.tensor_copy(posf[:, :], posi[:, :]))
            for t in range(NT):
                last = V.tensor_scalar(ang[:, 0, t, :], C("freq"), posf[:, t:t + 1], None, ALU.mult)
            link(last)
            A, Kt_, R = ang[:, 0], ang[:, 2], ang[:, 3]
            link(V.tensor_scalar(Kt_, A, 1.0 / (2 * math.pi), 12582912.0, ALU.mult, ALU.add))
            link(V.tensor_scalar(Kt_, Kt_, 12582912.0, None, ALU.subtract))
            link(V.scalar_tensor_tensor(out=A, in0=Kt_, scalar=-6.28125, in1=A, op0=ALU.mult, op1=ALU.add))
            link(V.scalar_tensor_tensor(out=A, in0=Kt_, scalar=-TWO_PI_2, in1=A, op0=ALU.mult, op1=ALU.add))
            link(V.scalar_tensor_tensor(out=A, in0=Kt_, scalar=-TWO_PI_3, in1=A, op0=ALU.mult, op1=ALU.add))
            link(V.tensor_scalar(A, A, 3.1415925, -3.1415925, ALU.min, ALU.max))
            link(V.tensor_scalar(ang[:, 1], A, math.pi / 2, None, ALU.add))
            link(V.tensor_scalar(R, ang[:, 1], math.pi, -2 * math.pi, ALU.is_gt, ALU.mult))
            link(V.tensor_tensor(ang[:, 1], ang[:, 1], R, ALU.add))
            link(V.tensor_scalar(ang[:, 1], ang[:, 1], 3.1415925, -3.1415925, ALU.min, ALU.max))
            for l in range(L1):
                for m in range(2):
                    V.tensor_scalar(cols1[:, l, 58 + m:59 + m], cols1[:, l, 26:27], C("halfs", m, 1), None, ALU.mult)
                V.tensor_copy(cols1[:, l, 19:20], cols1[:, l, 18:19])
                last = V.tensor_copy(cols1[:, l, 21:22], cols1[:, l, 20:21])
            last.then_inc(setup_v, 1)
            conv(0)
            conv(1)
            n = 0
            for k in phases:
                if k[0] == "norm":
                    norm(k, n)
                    n += 1
                elif k[0] in ("mix1", "mix2"):
                    if k == ("mix2", 0):
                        for i in range(2):
                            last = V.tensor_tensor(lam_in[:, :, 2 * i], lam_in[:, :, 2 * i], lam_in[:, :, 2 * i + 1], ALU.mult)
                        link(last)
                        for i in range(2):
                            last = V.tensor_reduce(lam[:, :, i:i + 1], lam_in[:, :, 2 * i], AX, ALU.add)
                        for l in range(L1):
                            s = 1.0 - LAM_INIT[l]
                            last = V.tensor_scalar(cols2[:, l, 23:24], cols2[:, l, 23:24], s, None, ALU.mult)
                        link(last)
                        for l in range(L1):
                            last = V.tensor_copy(cols2[:, l, 24:25], cols2[:, l, 23:24])
                        last.then_inc(setup2_v, 1)
                        dve.wait_ge(setup_s, 2)
                        link(V.tensor_tensor(lam[:, :, 2:3], lam[:, :, 1:2], lam[:, :, 0:1], ALU.subtract))
                        for l in range(L1):
                            last = V.tensor_scalar(lam[:, l, 2:3], lam[:, l, 2:3], LAM_INIT[l], None, ALU.subtract)
                        link(last)
                        b = X[0]
                        wait_full("bias_rows", b)
                        V.tensor_copy(tabT[0:8, :], bank[b][0:8, 0:384]).then_inc(free[b], 1)
                    mixer(k)
                elif k[0] != "moe":
                    feed_forward(k, FFJ[k[0]])
                else:
                    b, key = X[0], (k, "router")
                    wait_full(key, b)
                    V.tensor_copy(lg8[:, :, :], bank[b][:, 0:16].rearrange("p (t n) -> p t n", t=2)).then_inc(free[b], 1)
                    dve.wait_ge(free[b], ev(key, b))
                    for t in range(NT):
                        last = V.max(m8[:, t, :], lg8[:, t, :])
                    link(last)
                    for t in range(NT):
                        V.max_index(i8[:, t, :], m8[:, t, :], lg8[:, t, :])
                        last = V.tensor_scalar(top2[:, t, 1:2], m8[:, t, 0:1], -1.0, None, ALU.mult)
                    last.then_inc(route_m, 1)
                    dve.wait_ge(route_m, 1)
                    link(V.tensor_copy(i8f[:, :, :], i8[:, :, 0:2]))
                    dve.wait_ge(route_e, 1)
                    link(V.tensor_scalar_add(top2[:, :, 2:3], top2[:, :, 0:1], 1.0))
                    link(V.reciprocal(top2[:, :, 2:3], top2[:, :, 2:3]))
                    link(V.tensor_tensor(top2[:, :, 3:4], top2[:, :, 2:3], top2[:, :, 0:1], ALU.mult))
                    for t in range(NT):
                        V.tensor_scalar(gate8[:, t, :], C("experts"), i8f[:, t, 0:1], top2[:, t, 2:3], ALU.is_equal, ALU.mult)
                        last = V.tensor_scalar(lg8[:, t, :], C("experts"), i8f[:, t, 1:2], top2[:, t, 3:4], ALU.is_equal, ALU.mult)
                    link(last)
                    link(V.tensor_tensor(gate8[:, :, :], gate8[:, :, :], lg8[:, :, :], ALU.add))
                    with dve.Fori(0, NE) as e:
                        feed_forward(k, FFJ["moe"], e)
            norm(("norm", 0, None), n)

        @block.gpsimd
        def _(pool):
            G = nc.gpsimd
            links = [0]
            loads = [0, 0]

            def link(ins):
                links[0] += 1
                ins.then_inc(pool_link, 1)
                pool.wait_ge(pool_link, links[0])

            def load(dst, src, second=False):
                loads[second] += 1
                pool.dma_start(dst, src).then_inc(par2_loaded if second else par_loaded, 16)

            pool.dma_start(x[:, :, :], a["x"][0].rearrange("(t p) d -> p t d", p=P)).then_inc(x_loaded, 16)
            pool.dma_start(cst[:, :], a["cst"]).then_inc(cst_loaded, 16)
            load(posi[:, :], a["positions"][0].rearrange("(t p) -> p t", p=P))
            for l in range(L1):
                load(cols1[:, l, 0:8], a["ln1"][l].rearrange("(k p) -> p k", p=P))
                load(cols1[:, l, 8:16], a["ln2"][l].rearrange("(k p) -> p k", p=P))
                load(cols1[:, l, 22:26], a["ssd_norm"][l].rearrange("(k p) -> p k", p=P))
                for tap in range(4):
                    load(cols1[:, l, 28 + 6 * tap:34 + 6 * tap], a["ssd_conv_w"][l, tap].rearrange("(k p) -> p k", p=P))
                load(cols1[:, l, 52:58], a["ssd_conv_b"][l].rearrange("(k p) -> p k", p=P))
                for name, cc in (("gla_norm", 18), ("ret_norm", 20), ("fox_qn", 26), ("fox_kn", 27)):
                    for h in range(2):
                        load(cols1[64 * h:64 * h + 64, l, cc:cc + 1], a[name][l].rearrange("(p o) -> p o", o=1))
                o = 0
                for f, w in W1SMALL:
                    load(wsm[:, l, :, o:o + w], a["w_in"][l].rearrange("(k p) n -> p k n", p=P)[:, :, f:f + w])
                    o += w
                load(gw2[0:16, l, :], a["gla_w2"][l])
                load(gw2[16:17, l, :], a["gla_b"][l:l + 1])
            load(brow[0:1, :, 16:20], a["fox_bf"].unsqueeze(0))
            load(brow[0:1, :, 20:28], a["ssd_dt_bias"].unsqueeze(0))
            load(heads8[:, :, 0:8], a["ssd_a_log"].partition_broadcast(P))
            load(heads8[:, :, 8:16], a["ssd_d"].partition_broadcast(P))
            for l in range(L1):
                load(cols2[:, l, 0:8], a["mix_norm_g_2"][l].rearrange("(k p) -> p k", p=P))
                load(cols2[:, l, 8:16], a["ffn_norm_g_2"][l].rearrange("(k p) -> p k", p=P))
                for tap in range(3):
                    load(conv2[:, l, 2 * tap:2 * tap + 2], a["conv_w_2"][l, tap].rearrange("(k p) -> p k", p=P))
                load(cols2[:, l, 21:23], a["pool_scale_2"][l].rearrange("(k p) -> p k", p=P))
                for h in range(2):
                    load(cols2[64 * h:64 * h + 64, l, 23:24], a["diff_subln_g_2"][l].rearrange("(p o) -> p o", o=1))
            load(lam_in[:, :, :, :], a["diff_lambda_2"].partition_broadcast(P))
            assert loads[0] == NPAR, loads

            def build(k, h, col, slot):
                for j, (m, t) in enumerate((("after", 0), ("ones", 1), ("after", 1))):
                    last = G.tensor_scalar(Bld[:, slot, j * P:j * P + P], C(m), z[:, t, col:col + 1], None, ALU.mult)
                last.then_inc(T["builds"], 1)

            def mix1(k):
                l, c0 = k[1], CH[k]
                pool.wait_ge(T["decay"], at("decay", l))
                for h in range(4):
                    build(k, h, 256 + h, h)
                for n in (3, 4):
                    for t in range(NT):
                        pool.wait_ge(free[gbank(n, t)], ev((k, "gemm", n), gbank(n, t)))
                if l == 0:
                    pool.wait_ge(setup_s, 1)
                for t in range(NT):
                    v = u[:, t, U1["rq"]:U1["rq"] + 512].rearrange("p (h j d) -> p h j d", j=2, d=32)
                    x1, x2 = v[:, :, 0, :], v[:, :, 1, :]
                    sn, cs = (rot[:, i, t, :].unsqueeze(1).to_broadcast([P, 8, 32]) for i in range(2))
                    t0, t1, t2 = (rope_t[:, i, t] for i in range(3))
                    G.tensor_tensor(t0, x1, cs, ALU.mult)
                    G.tensor_tensor(t1, x2, sn, ALU.mult)
                    link(G.tensor_tensor(t2, x1, sn, ALU.mult))
                    link(G.tensor_tensor(x1, t0, t1, ALU.subtract))
                    link(G.tensor_tensor(t0, x2, cs, ALU.mult))
                    last = G.tensor_tensor(x2, t2, t0, ALU.add)
                last.then_inc(T["rope"], 1)
                for h in range(4):
                    pool.wait_ge(full[X[h]], fl((k, f"fs{h}"), X[h]))
                    build(k, h, 260 + h, h)
                pool.wait_ge(T["xbc"], at("xbc", l, 3))
                for t in range(NT):
                    pool.wait_ge(free[X[t]], ev((k, "xs"), X[t]))
                for r in range(2):
                    for t in range(NT):
                        xs = u[:, t, U1["xbc"] + 256 * r:U1["xbc"] + 256 * r + 256].rearrange("p (h d) -> p h d", d=HD)
                        last = G.tensor_tensor(qM[:, r, t, :].rearrange("p (h d) -> p h d", d=HD), xs,
                                               heads8[:, l, 8 + 4 * r:12 + 4 * r].unsqueeze(2).to_broadcast([P, 4, HD]), ALU.mult)
                    last.then_inc(T["ssd_dx"], 1)
                for h in range(4, 8):
                    pool.wait_ge(full[X[h % 4]], fl((k, f"sg{h - 4}"), X[h % 4]))
                    build(k, h, 260 + h, h % 4)

            def merge(k):
                l, name = k[1], "merged" if k[0] == "mix1" else "merged_b"
                for br in range(1, 4):
                    banks = (0, 1, 2, 3) if br % 2 == 0 else X
                    for t in range(NT):
                        for n in range(2):
                            b0, b = 2 * t + n, banks[2 * t + n]
                            if br == 1:
                                pool.wait_ge(free[b0], ev((k, "up", 0), b0))
                            else:
                                pool.wait_ge(T[name], at(name, l, 4 * (br - 2) + 2 * t + n + 1))
                            pool.wait_ge(free[b], ev((k, "up", br), b))
                            m = u[:, t, n * 512:n * 512 + 512]
                            G.tensor_tensor(m, m, gates[:, t, br * 1024 + n * 512:br * 1024 + n * 512 + 512], ALU.add).then_inc(T[name], 1)

            for k, ready in zip(phases, XREADY):
                if k[0] == "norm" and k[2] == "mix2" and k[1] == 0:
                    for b, v in ready:
                        pool.wait_ge(free[b], v)
                    for l in range(L1):
                        load(wgrp[:, l], a["pool_w_2"][l].rearrange("g c d -> c g d"), True)
                    load(router[:, :, :], a["moe_router_2"][0].rearrange("(k p) n -> p k n", p=P), True)
                    load(poolw[:, :, :], a["poolw"], True)
                    load(onehot[:, :], a["onehot"], True)
                    load(tab[0:32, :], a["bias_table_2"], True)
                    load(tab[32:33, :], a["ones8"], True)
                    assert loads[1] == NPAR2, loads
                elif k[0] == "mix1":
                    mix1(k)
                    merge(k)
                elif k[0] == "mix2":
                    if k[1] == 0:
                        pool.wait_ge(free[X[0]], ev("bias_rows", X[0]))
                        pool.dma_start(scratch, tabT[0:8, :]).then_inc(rows_out, 16)
                        pool.wait_ge(rows_out, 16)
                        pool.dma_start(biasT[:, :, :], bass.AP(scratch.tensor, 0, [[1, P], [384, 8], [1, S]])).then_inc(bias_in, 16)
                    merge(k)
            for b, v in last_x:
                pool.wait_ge(free[b], v)
            pool.dma_start(fgain[:, :], a["final_norm_g_2"].partition_broadcast(P)).then_inc(fgain_in, 16)


FFJ = {"ffn1": FH1 // FB, "ffn2": FH1 // FB, "moe": FH2 // FB}
LAM_INIT = [0.8 - 0.6 * math.exp(-0.3 * i) for i in range(L1)]
LOG_GAMMA = [float(np.log(np.float32(1.0) - np.float32(2.0) ** np.float32(-5.0 - h))) for h in range(RH)]
TWO_PI_2 = float(np.float32(2 * math.pi - 6.28125))
TWO_PI_3 = 2 * math.pi - 6.28125 - TWO_PI_2
NPAR = 1 + L1 * (3 + 4 + 1 + 8 + 3 + 2) + 4 + L1 * (2 + 3 + 1 + 2) + 1
NPAR2 = L1 + 5

_INS = ["x", "positions", "ln1", "ln2", "w_in", "fox_bf", "fox_qn", "fox_kn", "gla_w2", "gla_b", "gla_norm", "ret_norm",
        "ssd_conv_w", "ssd_conv_b", "ssd_dt_bias", "ssd_a_log", "ssd_d", "ssd_norm", "w_up_a", "w_up_b", "w_up_c", "w_up_d",
        "w_out", "w_ffn_in", "w_ffn_out", "bias_table_2", "mix_norm_g_2", "w_in_2", "conv_w_2", "pool_w_2", "pool_scale_2",
        "diff_lambda_2", "diff_subln_g_2", "branch_proj_2", "w_out_2", "ffn_norm_g_2", "dense_w1_2", "dense_w3_2",
        "dense_w2_2", "moe_router_2", "moe_w1_2", "moe_w3_2", "moe_w2_2", "final_norm_g_2"]


def kernel(**inputs):
    import concourse.bacc as bacc
    from concourse.bass_utils import run_bass_kernel_spmd as run

    nc = bacc.Bacc("TRN2", target_bir_lowering=False, num_devices=1)
    arrays = {name: np.ascontiguousarray(inputs[name]) for name in _INS}
    arrays.update(cst=constants(), onehot=bias_buckets(), poolw=pool_matrices(), ones8=np.ones((1, 8), np.float32))
    a = {name: nc.dram_tensor(f"in_{name}", v.shape, mybir.dt.from_np(v.dtype), kind="ExternalInput").ap()
         for name, v in arrays.items()}
    out = nc.dram_tensor("out", (S, D), F32, kind="ExternalOutput").ap()
    program(nc, a, out)
    r = run(nc, [{f"in_{name}": v for name, v in arrays.items()}], core_ids=[0])
    return r.results[0]["out"].reshape(1, S, D)
```

```python
import math
from contextlib import ExitStack

import numpy as np
import concourse.bass as bass
from concourse import mybir

F32 = mybir.dt.float32
F32R = mybir.dt.float32r
I32 = mybir.dt.int32
U32 = mybir.dt.uint32
ALU = mybir.AluOpType
ACT = mybir.ActivationFunctionType
AX = mybir.AxisListType.X

P = 128
D = 1024
S = 256
KT = D // P
NT = S // P
L1 = 2
HD = 64
RH = 4
FH1 = 2816
FH2 = 3584
NE = 8
MORE = (2 * S) // (P + 1)
JOBS = NE + MORE + 1
FB = 256
BLK = 512
RAW = 6
HI = 3
BIG = 3.0e38
NEG = -1.0e30

U1 = dict(fq=0, fk=256, fv=512, gq=768, gk=1024, gv=1280, gr=1536, rq=1792, rk=2048, rv=2304, rg=2560, z=2816, xbc=3328)
W1RUNS = [[(0, 512)], [(512, 256), (772, 256)], [(1028, 512)]] + [[(1556 + 512 * i, 512)] for i in range(5)] \
    + [[(4124 + 512 * i, 512)] for i in range(8)]
W1SMALL = [(1540, 16), (768, 4), (4116, 8)]
U2 = dict(qa=0, ka=256, va=512, xb=768, bb=1024, cb=1280, pc=1536, qd=1792, kd=2048, vd=2304)
W2RUNS = [[(512 * i, 512)] for i in range(13)]

CST = {}


def constants():
    a = np.arange(P)
    j, t = a[:, None], a[None, :]
    parts = [
        ("ident", (j == t) * 1.0),
        ("triu", (j <= t) * 1.0),
        ("ones", np.ones((P, P))),
        ("after", (j > t) * 1.0),
        ("trimid", (j <= t) * 1.0 - (j <= 63) * 1.0),
        ("clamp", np.concatenate([(j <= t) * BIG, np.full((P, P), BIG), (j <= t) * BIG], 1)),
        ("negmask", (t > j) * NEG),
        ("rel", np.concatenate([np.where(t >= j, t - j, 1e30), P + t - j], 1)),
        ("flip", (j + t == P - 1) * 1.0),
        ("half", (j // 64 == np.arange(2)[None]) * 1.0),
        ("halfs", (j // 64 == np.arange(2)[None]) * 0.125),
        ("quarter", (j // 32 == np.arange(4)[None]) * 32 ** -0.5),
        ("experts", np.zeros((P, 1)) + np.arange(NE)[None]),
        ("countdown", np.zeros((P, 1)) + NE - np.arange(NE)[None]),
        ("slots", np.zeros((P, 1)) + np.arange(P)[None]),
        ("freq", np.zeros((P, 1)) + (np.float32(10000.0) ** (-np.arange(32, dtype=np.float32) / np.float32(32)))[None]),
    ]
    at = 0
    for name, m in parts:
        CST[name] = (at, m.shape[1])
        at += m.shape[1]
    return np.concatenate([m.astype(np.float32) for _, m in parts], 1)


def bias_buckets():
    d = 255 - np.arange(384)
    n = np.maximum(d, 0)
    nf = np.maximum(n, 16).astype(np.float32)
    large = 16 + (np.log(nf / np.float32(16)) / np.float32(math.log(8.0)) * np.float32(16)).astype(np.int32)
    bucket = np.where(n < 16, n, np.minimum(large, 31))
    return np.concatenate([(bucket[None] == np.arange(32)[:, None]) * 1.0, (d < 0)[None] * NEG], 0).astype(np.float32)


def pool_matrices():
    s, t = np.arange(S)[:, None], np.arange(S)[None]
    out = []
    for w in (2, 4, 8, 16):
        m = ((s <= t) & (s > t - w)) / np.minimum(t + 1, w) - (s == t)
        out.append(np.concatenate([m[:P, :], m[P:, P:]], 1))
    return np.stack(out, 1).astype(np.float32)


constants()


G1 = {
    0: [("small", [0])], 1: [("glrT", [1])], 2: [("zg", [2])],
    4: [("fqk", [0, 1])], 5: [("cum", [2, 3])],
    6: [("fs0", [0]), ("fs1", [1])], 7: [("fs2", [2]), ("fs3", [3])],
    8: [("ft0", [0]), ("ft1", [1])], 9: [("ft2", [2]), ("ft3", [3])],
    10: [("fy", [0])], 11: [("gt", [1, 2, 3])],
    13: [(f"gs{h}", [h]) for h in range(4)], 15: [("gy", [0])],
    16: [("rt", [1, 3])], 18: [(f"rs{h}", [h]) for h in range(4)], 20: [("ry", [0])],
    21: [("xt", [1, 2, 3])], 24: [("xs", [0, 1]), ("cb", [2, 3])],
    26: [(f"sg{h}", [h]) for h in range(4)], 28: [("sy0", [0])],
    29: [(f"sg{h + 4}", [h]) for h in range(4)], 31: [("sy1", [0])],
}
G2 = {
    2: [("aqk", [0, 1])], 3: [(f"as{h}", [h]) for h in range(4)], 5: [(f"at{h}", [h]) for h in range(4)],
    6: [("cx", [0, 1])], 7: [("ay", [2])], 8: [("pl", [0, 1])], 9: [("py", [2])],
    10: [("dqk", [0, 1])], 12: [(f"ds{i}", [i]) for i in range(4)], 14: [("dt0", [0]), ("dt1", [1])], 15: [("dy0", [2])],
    17: [(f"ds{i + 4}", [i]) for i in range(4)], 19: [("dt2", [0]), ("dt3", [1])], 20: [("dy1", [2])],
}


def program(nc, a, out, stop=99):
    ctx = ExitStack()
    with ctx:
        ctx.enter_context(nc.allow_non_contiguous_dma("small parameters"))

        room = nc.sbuf_bytes_remaining - 64 
        room -= room % 64
        base = nc.sbuf_base 
        ctx.enter_context(nc.sbuf_tensor("slab", [P, room // 4], F32))
        top = [base + (-base) % 64]

        def sb(name, shape, dtype=F32, at=None):
            size = int(np.prod(shape[1:])) * 4
            if at is None:
                at = top[0]
                top[0] += size + (-size) % 32
                assert top[0] <= base + room, (name, top[0] - base, room)
            return nc.alloc_sbuf_tensor_at(name, shape, dtype, offset=at)

        ring_at = top[0]
        raw = sb("raw", [P, RAW, 2048])
        lo = sb("w_lo", [P, RAW, 2048], F32R, at=ring_at)
        hi = sb("w_hi", [P, HI, 2048], F32R)
        xhi = sb("xhi", [P, 10, S], F32R)
        xlo = sb("xlo", [P, 10, S], F32R)
        x = sb("x", [P, NT, D])
        u_at = top[0]
        u = sb("u", [P, NT, 4096])
        g_at = top[0]
        gates = sb("gates", [P, NT, 4096])
        ghi = sb("ghi", [P, 2, NT, P], F32R, at=u_at)
        glo = sb("glo", [P, 2, NT, P], F32R, at=u_at + 2048)
        silu = sb("silu", [P, NT, FB], at=u_at + 4096)
        gprod = sb("gprod", [P, NT, FB], at=u_at + 6144)
        pick = sb("pick", [P, NT, P], at=u_at + 8192)
        pick_g = sb("pick_g", [P, NT, P], at=u_at + 9216)
        pick_t = sb("pick_t", [P, NT, P], at=u_at + 10240)
        y = sb("y", [P, D], at=u_at + 11264)
        hrow = sb("hrow", [P, NT, D], at=g_at)
        rope_t = sb("rope_t", [P, 3, NT, 8, 32], at=g_at + 8192)
        sq = sb("sq", [P, NT, 512], at=g_at + 16384)
        fgain = sb("fgain", [P, D], at=g_at + 16384)
        NC = max(v[0] + v[1] for v in CST.values())
        cst = sb("cst", [P, NC])

        def C(name, lo_=0, n=None):
            at, w = CST[name]
            return cst[:, at + lo_:at + (w if n is None else lo_ + n)]

        cols1 = sb("cols1", [P, L1, 60])
        cols2 = sb("cols2", [P, L1, 25])
        heads8 = sb("heads8", [P, L1, 16])
        lam_in = sb("lam_in", [P, L1, 4, 32])
        lam = sb("lam", [P, L1, 6])
        small = sb("small", [P, 64])
        epst = sb("epst", [P, 2])
        conv2 = sb("conv2", [P, L1, 6])
        nstat = sb("nstat", [P, 8])
        type1_at = top[0]
        brow = sb("brow", [1, L1, 28])
        wsm = sb("wsm", [P, L1, KT, 28])
        gw2 = sb("gw2", [17, L1, 256])
        rot = sb("rot", [P, 2, NT, 32])
        glrT = sb("glrT", [17, S])
        z = sb("z", [P, NT, 268])
        dtv = sb("dtv", [P, NT, 8])
        E_at = top[0]
        E = sb("E", [P, 6, 256])
        zlog = sb("zlog", [P, NT, 268], at=E_at)
        tg = sb("tg", [P, NT, 256], at=E_at)
        ysq = sb("ysq", [P, NT, 256], at=E_at + 2048)
        tgz = sb("tgz", [P, NT, 512], at=E_at)
        us = sb("us", [P, NT, P], at=top[0])
        Bld = sb("Bld", [P, 4, 384])
        Pm = sb("Pm", [P, 4, 384])
        kT = sb("kT", [P, 2, S])
        qM = sb("qM", [P, 2, 2, S])
        kE_at = top[0]
        kE = sb("kE", [P, 2, P])
        qD = sb("qD", [P, 2, 2, P])
        cbm = sb("cbm", [P, 2, 384], at=kE_at)
        type1_end = top[0]
        top[0] = type1_at
        router = sb("router", [P, KT, NE])
        wgrp = sb("wgrp", [64, L1, 4, 64])
        biasT = sb("biasT", [P, 8, S])
        poolw = sb("poolw", [P, 4, 384])
        tab = sb("tab", [33, 8])
        tabT = sb("tabT", [8, 384])
        p2_at = top[0]
        P2m = sb("P2m", [P, 4, 384])
        kT2 = sb("kT2", [P, 2, S])
        qM2 = sb("qM2", [P, 4, 2, S])
        mgain = sb("mgain", [P, D], at=p2_at)
        type2_end = top[0]
        top[0] = max(type1_end, type2_end)
        ybT = sb("ybT", [P, 2, S], at=u_at + 4 * 2560)
        plT = sb("plT", [64, 4, S], at=u_at + 4 * 2560 + 2048)
        onehot = sb("onehot", [33, 384], at=g_at + 24576)
        ang = sb("ang", [P, 4, NT, 32], at=g_at + 24576)
        posi = sb("posi", [P, NT], I32, at=g_at + 28672)
        posf = sb("posf", [P, NT], at=g_at + 28672 + 64)
        gate8 = sb("gate8", [P, NT, 8], at=u_at + 15360)
        m8 = sb("m8", [P, NT, 8], at=u_at + 15424)
        i8 = sb("i8", [P, NT, 8], U32, at=u_at + 15488)
        i8f = sb("i8f", [P, NT, 2], at=u_at + 15552)
        lg8 = sb("lg8", [P, NT, 8], at=u_at + 15616)
        top2 = sb("top2", [P, NT, 4], at=u_at + 15680)
        chosen = sb("chosen", [P, NT, 8], at=u_at + 15744)
        rank = sb("rank", [P, 3, 8], at=u_at + 15808)
        over = sb("over", [P, 4, 8], at=u_at + 15936)
        prod8 = sb("prod8", [P, NT, 8], at=u_at + 16064)
        jobpos = sb("jobpos", [P, NT, JOBS], at=u_at + 16128)
        jobgate = sb("jobgate", [P, NT, JOBS], at=u_at + 16256)
        jobs_f = sb("jobs_f", [P, 4], at=u_at + 16384)
        jobs_i = sb("jobs_i", [P, 4], I32, at=u_at + 16448)
        if top[0] > base + room:
            raise ValueError("SBUF")

        bank = [ctx.enter_context(nc.psum_tensor(f"bank{i}", [P, 512], F32)) for i in range(8)]
        X = [4, 5, 6, 7]
        scratch = nc.dram_tensor("bias_rows", (8, 384), F32, kind="Internal").ap()

        def sem(name):
            return ctx.enter_context(nc.semaphore(name))

        full = [sem(f"bank_full{i}") for i in range(8)]
        free = [sem(f"bank_free{i}") for i in range(8)]
        raw_full = [sem(f"raw_full{i}") for i in range(RAW)]
        hi_ready = sem("hi_ready")
        lo_ready = sem("lo_ready")
        w_used = sem("w_used")
        x_loaded, cst_loaded, par_loaded = sem("x_loaded"), sem("cst_loaded"), sem("par_loaded")
        par2_loaded, rows_out, bias_in, fgain_in, stored = (sem(n) for n in
            ("par2_loaded", "bias_rows_out", "bias_in", "final_gain_in", "stored"))
        setup_v, setup_s, setup2_v = sem("setup_vector"), sem("setup_scalar"), sem("setup2_vector")
        norm_ss, norm_rstd, norm_h, norm_hi = sem("norm_sumsq"), sem("norm_rstd"), sem("norm_rows"), sem("norm_hi")
        silu_done, ghi_done = sem("silu_done"), sem("gated_hi")
        route_m, route_e = sem("route_max"), sem("route_exp")
        chosen_ready, routed = sem("chosen_ready"), sem("routed")
        pick_ready = sem("pick_ready")
        gather_hi = sem("gather_hi")
        moe_gain_in = sem("moe_gain_in")
        dve_link, act_link, pool_link = sem("vector_link"), sem("scalar_link"), sem("pool_link")
        STEPS = dict(z_abs=1, z_log=1, decay=1, fox_ss=1, fox_rstd=1, fox_qn=1, builds=12, fox_max=4,
                     gla_prod=1, gla_p=4, gate_exp=2, br_ss=3, br_rstd=3, y_gla=1, y_ret=1, rope=1, ret_decay=4,
                     conv_out=3, conv_exp=3, xbc=3, ssd_c=1, ssd_x=1, cb=1, ssd_p=8, ssd_dx=2, z_exp=1, y_ssd=1,
                     gate_one=8, y_hi=5, merged=12, m_hi=4,
                     moba_max=4, conv_in=1, dif_max=8, dif_p=4, d_ss=1, d_rstd=1, y_dif=1, y_conv=1,
                     gate_one_b=8, y_hi_b=4, merged_b=12, m_hi_b=4)
        T = {name: sem(name) for name in STEPS}

        def at(name, l, n=1):
            return l * STEPS[name] + n

        uses, fulls = [0] * 8, [0] * 8
        USE, FULL, CH, FFB = {}, {}, {}, {}

        def claim(key, *banks, streamed=False):
            for b in banks:
                uses[b] += 1
                USE[key, b] = uses[b]
                if not streamed:
                    fulls[b] += 1
                    FULL[key, b] = fulls[b]

        phases = []
        for l in range(L1):
            phases += [("norm", l, "mix1"), ("mix1", l), ("norm", l, "ffn1"), ("ffn1", l)]
        for l in range(L1):
            f = "ffn2" if l == 0 else "moe"
            phases += [("norm", l, "mix2"), ("mix2", l), ("norm", l, f), (f, l)]
        phases = phases[:2 * stop]
        c = ffb = 0
        XREADY = []
        last_x = None
        for k in phases:
            XREADY.append(last_x)
            if k[0] == "norm":
                for i in range(4):
                    claim(k, X[i])
                continue
            CH[k] = c
            if k[0] in ("mix1", "mix2"):
                nb, groups, ny = (16, G1, 5) if k[0] == "mix1" else (13, G2, 4)
                if k[0] == "mix2" and k[1] == 0:
                    claim("bias_rows", X[0])
                for pos in range(2 * nb):
                    if pos % 2 == 0:
                        claim((k, "gemm", pos // 2), *(2 * (pos // 2 % 2) + t for t in range(NT)), streamed=True)
                    for g, bs in groups.get(pos, []):
                        claim((k, g), *(X[b] for b in bs))
                for i in range(ny):
                    claim((k, "yT", i), X[i % 4])
                for br in range(4):
                    claim((k, "up", br), *((0, 1, 2, 3) if br % 2 == 0 else X), streamed=True)
                for i in range(4):
                    claim((k, "mT", i), X[i])
                claim((k, "out"), 0, 1, 2, 3, streamed=True)
                c += 2 * nb + ny + 4
                last_x = [(b, USE[(k, "out"), b] + 1) for b in range(4)]
            else:
                J = FFJ[k[0]]
                FFB[k] = ffb
                if k[0] == "moe":
                    claim((k, "router"), X[0])
                    claim((k, "rank"), X[1])
                    claim((k, "gather"), 2, 3)
                    u0, f0 = list(uses), list(fulls)
                    for j in range(J):
                        claim((k, "U", j), j % 2, streamed=True)
                        if j == 0:
                            claim((k, "scatter"), X[2], X[3], 2, 3)
                            claim((k, "turned"), X[2])
                        if j == J - 1:
                            claim((k, "next"), 2, 3)
                        claim((k, "T", j), j % 2)
                    claim((k, "D"), X[0], X[1], streamed=True)
                    JU, JF = [m - n for m, n in zip(uses, u0)], [m - n for m, n in zip(fulls, f0)]
                    c += 2
                else:
                    for j in range(J):
                        for t in range(NT):
                            claim((k, "U", j), 2 * (j % 2) + t, streamed=True)
                            claim((k, "T", j), 2 * (j % 2) + t)
                    claim((k, "D"), *X, streamed=True)
                    c += 3 * J
                    ffb += 2 * J
                    last_x = [(b, USE[(k, "D"), b] + 1) for b in X]
        END = c

        def use(key, b):
            return USE[key, b]

        def ev(key, b):
            return USE[key, b] + 1

        def fl(key, b):
            return FULL[key, b]

        def gbank(n, t):
            return 2 * (n % 2) + t

        def walk(eng, J, u0, tr, u1, dn, early=lambda: None, late=lambda: None):
            u0(0, 0, 0)
            u1(0, 0, 1)
            early()
            u0(1, 0, 2)
            tr(0, 0)
            u1(1, 0, 3)
            dn(0, 0, 4)
            n = (J - 3) // 2
            with eng.Fori(0, n) as it:
                for j in (1, 2):
                    u0(j + 1, it, 2 + 3 * j)
                    tr(j, it)
                    u1(j + 1, it, 3 + 3 * j)
                    dn(j, it, 4 + 3 * j)
            for j in range(1 + 2 * n, J - 1):
                u0(j + 1, 0, 2 + 3 * j)
                tr(j, 0)
                u1(j + 1, 0, 3 + 3 * j)
                dn(j, 0, 4 + 3 * j)
            late()
            tr(J - 1, 0)
            dn(J - 1, 0, 3 * J - 1)

        def each_job(eng, job):
            with eng.Fori(0, NE) as e:
                job(e)
            nj = eng.value_load(jobs_i[0:1, MORE:MORE + 1], min_val=NE, max_val=NE + MORE)
            with eng.If(nj > NE):
                with eng.Fori(NE, nj) as e:
                    job(e)
            return nj

        block = ctx.enter_context(nc.Block())

        @block.sync
        def _(sp):
            def slot(c, it=0, eo=0, per=0):
                if c >= RAW:
                    sp.wait_ge(w_used, c - RAW + 1 + 6 * it + per * eo)
                return c % RAW

            def columns(c, w, k0, runs):
                s = slot(c)
                dst = raw[:, s, :].rearrange("p (k n) -> p k n", k=4)
                src = w.rearrange("(k p) n -> p k n", p=P)[:, k0:k0 + 4]
                if len(runs) == 1:
                    (f, n), = runs
                    sp.dma_start(dst[:, 0:2], src[:, 0:2, f:f + n]).then_inc(raw_full[s], 16)
                    sp.dma_start(dst[:, 2:4], src[:, 2:4, f:f + n]).then_inc(raw_full[s], 16)
                else:
                    for i, (f, n) in enumerate(runs):
                        sp.dma_start(dst[:, :, 256 * i:256 * i + n], src[:, :, f:f + n]).then_inc(raw_full[s], 16)

            def rows(c, w, k0):
                s = slot(c)
                for i in range(2):
                    sp.dma_start(raw[:, s, 1024 * i:1024 * i + 1024],
                                 w[(k0 + i) * P:(k0 + i + 1) * P, :]).then_inc(raw_full[s], 16)

            def feed_forward(c0, J, wa, wb, wd, eo=0, per=0):
                va, vb = (w.rearrange("(k p) n -> p k n", p=P) for w in (wa, wb))

                def up(j, it, c, k0):
                    s = slot(c0 + c, it, eo, per)
                    dst = raw[:, s, :].rearrange("p (k n) -> p k n", k=4)
                    f = j * FB + it * (2 * FB)
                    sp.dma_start(dst[:, :, 0:FB], va[:, k0:k0 + 4, bass.ds(f, FB)]).then_inc(raw_full[s], 16)
                    sp.dma_start(dst[:, :, FB:2 * FB], vb[:, k0:k0 + 4, bass.ds(f, FB)]).then_inc(raw_full[s], 16)

                def down(j, it, c):
                    s = slot(c0 + c, it, eo, per)
                    for i in range(2):
                        f = j * FB + i * P + it * (2 * FB)
                        sp.dma_start(raw[:, s, 1024 * i:1024 * i + 1024], wd[bass.ds(f, P), :]).then_inc(raw_full[s], 16)

                walk(sp, J, lambda j, it, c: up(j, it, c, 0), lambda j, it: None,
                     lambda j, it, c: up(j, it, c, 4), down)

            for k in phases:
                if k[0] == "norm":
                    continue
                c0, l = CH[k], k[1]
                if k[0] in ("mix1", "mix2"):
                    w, runs, ups, wo = ((a["w_in"][l], W1RUNS, [a["w_up_a"][l], a["w_up_b"][l], a["w_up_c"][l], a["w_up_d"][l]],
                                         a["w_out"][l]) if k[0] == "mix1" else
                                        (a["w_in_2"][l], W2RUNS, [a["branch_proj_2"][l, i] for i in range(4)], a["w_out_2"][l]))
                    for n, run in enumerate(runs):
                        columns(c0, w, 0, run)
                        columns(c0 + 1, w, 4, run)
                        c0 += 2
                    for wu in ups:
                        for k0 in range(0, wu.shape[0] // P, 2):
                            rows(c0, wu, k0)
                            c0 += 1
                    for k0 in range(0, KT, 2):
                        rows(c0, wo, k0)
                        c0 += 1
                elif k[0] == "ffn1":
                    feed_forward(c0, FFJ[k[0]], a["w_ffn_in"][l][:, 0:FH1], a["w_ffn_in"][l][:, FH1:2 * FH1], a["w_ffn_out"][l])
                elif k[0] == "ffn2":
                    feed_forward(c0, FFJ[k[0]], a["dense_w1_2"][0], a["dense_w3_2"][0], a["dense_w2_2"][0])
                else:
                    J = FFJ[k[0]]
                    wts = [a["moe_w1_2"][0], a["moe_w3_2"][0], a["moe_w2_2"][0]]

                    def job(e, expert):
                        feed_forward(c0, J, *(w[bass.ds(expert, 1)].rearrange("a k n -> (a k) n") for w in wts), e, 3 * J)

                    with sp.Fori(0, NE) as e:
                        job(e, e)
                    sp.wait_ge(routed, 1)
                    nj = sp.value_load(jobs_i[0:1, MORE:MORE + 1], min_val=NE, max_val=NE + MORE)
                    with sp.If(nj > NE):
                        with sp.Fori(NE, nj) as e:
                            job(e, sp.value_load(jobs_i[0:1, bass.ds(e - NE, 1)], min_val=0, max_val=NE - 1))
                    for i in range(2):
                        s = slot(c0 + i, 0, nj, 3 * J)
                        for h in range(2):
                            sp.dma_start(raw[:, s, 1024 * h:1024 * h + 1024], wts[2][0, 0:P, :]).then_inc(raw_full[s], 16)
            sp.wait_ge(norm_h, 2 * len([k for k in phases if k[0] == "norm"]) + 2)
            sp.dma_start(out.rearrange("(t p) n -> p t n", p=P), hrow[:, :, :]).then_inc(stored, 16)
            sp.wait_ge(stored, 16)

        @block.tensor
        def _(pe):
            mm = nc.tensor.matmul
            ident = C("ident")

            def tr(dst, src):
                return nc.tensor.transpose(dst, src, ident)

            def gemm_half(banks, c, k0, start, stop, it=0, eo=0, per=0):
                s, h = c % RAW, c % HI
                pe.wait_ge(lo_ready, c + 1 + 6 * it + per * eo)
                for k in range(4):
                    for t in range(NT):
                        tok = slice(t * P, t * P + P)
                        wh, wl = (w[:, i, k * 512:k * 512 + 512] for w, i in ((hi, h), (lo, s)))
                        mm(bank[banks[t]][:, :], xhi[:, k0 + k, tok], wh, start=start and k == 0, stop=False)
                        mm(bank[banks[t]][:, :], xlo[:, k0 + k, tok], wh, start=False, stop=False)
                        last = mm(bank[banks[t]][:, :], xhi[:, k0 + k, tok], wl, start=False, stop=stop and k == 3)
                last.then_inc(w_used, 1)

            def gemm_rows(banks, c, lhs, first, final, it=0, eo=0, per=0):
                s, h = c % RAW, c % HI
                pe.wait_ge(lo_ready, c + 1 + 6 * it + per * eo)
                for k in range(2):
                    for t in range(NT):
                        xh, xl = lhs(k, t)
                        for n in range(2):
                            b = bank[banks[2 * t + n]][:, :]
                            o = k * 1024 + n * 512
                            mm(b, xh, hi[:, h, o:o + 512], start=first and k == 0, stop=False)
                            mm(b, xl, hi[:, h, o:o + 512], start=False, stop=False)
                            last = mm(b, xh, lo[:, s, o:o + 512], start=False, stop=final and k == 1)
                last.then_inc(w_used, 1)

            def xt(kt):
                return lambda k, t: (xhi[:, kt + k, t * P:t * P + P], xlo[:, kt + k, t * P:t * P + P])

            def transposes_to(key, b, srcs):
                pe.wait_ge(free[b], use(key, b))
                for i, src in enumerate(srcs):
                    last = tr(bank[b][:, i * P:(i + 1) * P], src)
                last.then_inc(full[b], 1)

            def norm(k, n):
                pe.wait_ge(norm_h, 2 * n + 2)
                for i in range(4):
                    transposes_to(k, X[i], [hrow[:, t, (2 * i + kk) * P:(2 * i + kk + 1) * P] for kk in range(2) for t in range(NT)])

            def values(key, b, off, heads, pblk, v0):
                for h in range(heads):
                    v = [u[:, t, v0 + h * HD:v0 + h * HD + HD] for t in range(NT)]
                    mm(bank[b][:, h * HD:h * HD + HD], pblk(h)[:, 0:P], v[0], start=True, stop=True)
                    mm(bank[b][:, 256 + h * HD:256 + h * HD + HD], pblk(h)[:, P:2 * P], v[0], start=True, stop=False)
                    last = mm(bank[b][:, 256 + h * HD:256 + h * HD + HD], pblk(h)[:, 2 * P:3 * P], v[1], start=False, stop=True)
                last.then_inc(full[b], 1)

            def gemm_waits(k, n):
                for t in range(NT):
                    pe.wait_ge(free[gbank(n, t)], ev((k, "gemm", n), gbank(n, t)))

            def attend1(k, pos):
                l = k[1]
                if pos == 0:
                    b, key = X[0], (k, "small")
                    pe.wait_ge(free[b], use(key, b))
                    if l == 0:
                        pe.wait_ge(par_loaded, 16 * NPAR)
                        pe.wait_ge(setup_v, 1)
                    for t in range(NT):
                        o = bank[b][:, t * 32:t * 32 + 28]
                        for kt in range(KT):
                            for j, xx in enumerate((xhi, xlo)):
                                mm(o, xx[:, kt, t * P:t * P + P].bitcast(F32), wsm[:, l, kt, :], start=kt == 0 and j == 0, stop=False)
                        last = mm(o, C("ones")[0:1, :], brow[0:1, l, :], start=False, stop=True)
                    last.then_inc(full[b], 1)
                elif pos == 1:
                    pe.wait_ge(free[X[0]], ev((k, "small"), X[0]))
                    transposes_to((k, "glrT"), X[1], [us[:, t, :] for t in range(NT)])
                elif pos == 2:
                    b, key = X[2], (k, "zg")
                    pe.wait_ge(free[X[1]], ev((k, "glrT"), X[1]))
                    pe.wait_ge(free[b], use(key, b))
                    for t in range(NT):
                        last = mm(bank[b][:, t * 256:t * 256 + 256], glrT[0:17, t * P:t * P + P], gw2[0:17, l, :], start=True, stop=True)
                    last.then_inc(full[b], 1)
                elif pos == 4:
                    pe.wait_ge(T["fox_qn"], at("fox_qn", l))
                    for i, o in ((0, U1["fq"]), (1, U1["fk"])):
                        transposes_to((k, "fqk"), X[i], [u[:, t, o + p * P:o + p * P + P] for p in range(2) for t in range(NT)])
                elif pos == 5:
                    pe.wait_ge(T["decay"], at("decay", l))
                    for i, mats in ((0, ("after", "trimid")), (1, ("trimid", "triu"))):
                        b = X[2 + i]
                        pe.wait_ge(free[b], use((k, "cum"), b))
                        for j, m in enumerate(mats):
                            last = mm(bank[b][:, j * 256:j * 256 + 256], C(m), z[:, i, 0:256], start=True, stop=True)
                        last.then_inc(full[b], 1)
                elif pos in (6, 7):
                    for h in (0, 1) if pos == 6 else (2, 3):
                        key, b, o = (k, f"fs{h}"), X[h], bank[X[h]]
                        pe.wait_ge(free[b], use(key, b))
                        for i in range(2):
                            pe.wait_ge(free[X[i]], ev((k, "fqk"), X[i]))
                        pe.wait_ge(T["builds"], at("builds", l, h + 1))
                        q, kk = qM[:, h % 2, h // 2, :], kT[:, h // 2, :]
                        mm(o[:, 0:P], q[:, 0:P], kk[:, 0:P], start=True, stop=False)
                        mm(o[:, 0:P], C("triu"), Bld[:, h, 0:P], start=False, stop=False)
                        mm(o[:, 0:P], ident, C("negmask"), start=False, stop=True)
                        mm(o[:, P:3 * P], q[:, P:2 * P], kk, start=True, stop=False)
                        mm(o[:, P:3 * P], C("triu"), Bld[:, h, P:3 * P], start=False, stop=False)
                        mm(o[:, P:2 * P], C("ones"), Bld[:, h, 0:P], start=False, stop=False)
                        mm(o[:, 2 * P:3 * P], ident, C("negmask"), start=False, stop=True).then_inc(full[b], 1)
                elif pos in (8, 9):
                    for h in (0, 1) if pos == 8 else (2, 3):
                        pe.wait_ge(free[X[h]], ev((k, f"fs{h}"), X[h]))
                        transposes_to((k, f"ft{h}"), X[h], [Pm[:, h, i * P:i * P + P] for i in range(3)])
                elif pos == 10:
                    for h in range(4):
                        pe.wait_ge(free[X[h]], ev((k, f"ft{h}"), X[h]))
                    values((k, "fy"), X[0], 0, 4, lambda h: Pm[:, h, :], U1["fv"])
                elif pos == 11:
                    pe.wait_ge(T["gla_prod"], at("gla_prod", l))
                    for i, es in ((1, ((2, 0), (4, 0), (2, 1), (4, 1))), (2, ((0, 0), (0, 1), (5, 0), (5, 1))),
                                  (3, ((1, 0), (3, 0), (1, 1), (3, 1)))):
                        transposes_to((k, "gt"), X[i], [E[:, e, p * P:p * P + P] for e, p in es])
                elif pos == 13:
                    for i in (1, 2, 3):
                        pe.wait_ge(free[X[i]], ev((k, "gt"), X[i]))
                    for h in range(4):
                        key, b, o, p, m = (k, f"gs{h}"), X[h], bank[X[h]], h // 2, h % 2
                        pe.wait_ge(free[b], use(key, b))
                        mm(o[:, 0:P], kT[:, p, 0:P], qM[:, m, p, 0:P], start=True, stop=True)
                        mm(o[:, P:2 * P], kE[:, p, :], qD[:, m, p, :], start=True, stop=True)
                        mm(o[:, 2 * P:3 * P], kT[:, p, P:2 * P], qM[:, m, p, P:2 * P], start=True, stop=True).then_inc(full[b], 1)
                elif pos == 15:
                    pe.wait_ge(free[X[0]], use((k, "gy"), X[0]))
                    pe.wait_ge(T["gla_p"], at("gla_p", l, 4))
                    values((k, "gy"), X[0], 0, 4, lambda h: Pm[:, h, :], U1["gv"])
                elif pos == 16:
                    pe.wait_ge(T["rope"], at("rope", l))
                    for i, o in ((1, U1["rk"]), (3, U1["rq"])):
                        transposes_to((k, "rt"), X[i], [u[:, t, o + p * P:o + p * P + P] for p in range(2) for t in range(NT)])
                elif pos == 18:
                    for i in (1, 3):
                        pe.wait_ge(free[X[i]], ev((k, "rt"), X[i]))
                    for h in range(4):
                        key, b, o, p, m = (k, f"rs{h}"), X[h], bank[X[h]], h // 2, h % 2
                        pe.wait_ge(free[b], use(key, b))
                        mm(o[:, 0:2 * P], kT[:, p, 0:P], qM[:, m, p, :], start=True, stop=True)
                        mm(o[:, 2 * P:3 * P], kT[:, p, P:2 * P], qM[:, m, p, P:2 * P], start=True, stop=True).then_inc(full[b], 1)
                elif pos == 20:
                    for h in range(4):
                        pe.wait_ge(free[X[h]], ev((k, f"rs{h}"), X[h]))
                    values((k, "ry"), X[0], 0, 4, lambda h: Pm[:, h, :], U1["rv"])
                elif pos == 21:
                    gemm_waits(k, 6)
                    gemm_waits(k, 7)
                    for i in range(3):
                        transposes_to((k, "xt"), X[1 + i], [u[:, t, U1["xbc"] + (2 * i + j) * P:U1["xbc"] + (2 * i + j + 1) * P]
                                                            for j in range(2) for t in range(NT)])
                elif pos == 24:
                    pe.wait_ge(T["xbc"], at("xbc", l, 3))
                    for t in range(NT):
                        transposes_to((k, "xs"), X[t], [E[:, i, t * P:t * P + P] for i in range(4)])
                    pe.wait_ge(T["ssd_c"], at("ssd_c", l))
                    for g in range(2):
                        b, o = X[2 + g], bank[X[2 + g]]
                        pe.wait_ge(free[b], use((k, "cb"), b))
                        mm(o[:, 0:2 * P], E[:, 4, 0:P], kT[:, g, :], start=True, stop=True)
                        mm(o[:, 2 * P:3 * P], E[:, 4, P:2 * P], kT[:, g, P:2 * P], start=True, stop=True).then_inc(full[b], 1)
                elif pos in (26, 29):
                    for h in range(4) if pos == 26 else range(4, 8):
                        key, b = (k, f"sg{h}"), X[h % 4]
                        o, i = bank[b], h % 4
                        pe.wait_ge(free[b], use(key, b))
                        pe.wait_ge(T["builds"], at("builds", l, 5 + h))
                        mm(o[:, 0:2 * P], Bld[:, i, 0:P], C("triu", 0, 2 * P), start=True, stop=False)
                        mm(o[:, P:2 * P], Bld[:, i, P:2 * P], C("triu"), start=False, stop=True)
                        mm(o[:, 2 * P:3 * P], Bld[:, i, 2 * P:3 * P], C("triu"), start=True, stop=True).then_inc(full[b], 1)
                elif pos in (28, 31):
                    r = 0 if pos == 28 else 1
                    pe.wait_ge(free[X[0]], use((k, f"sy{r}"), X[0]))
                    pe.wait_ge(T["ssd_x"], at("ssd_x", l))
                    pe.wait_ge(T["ssd_p"], at("ssd_p", l, 4 * r + 4))
                    values((k, f"sy{r}"), X[0], 0, 4, lambda h: Pm[:, h, :], 256 + 256 * r)

            def softmax_scores(k, key, b, q, kk, head):
                o = bank[b]
                pe.wait_ge(free[b], use(key, b))
                mm(o[:, 0:P], q[:, 0:P], kk[:, 0:P], start=True, stop=False)
                mm(o[:, 0:P], C("flip"), biasT[:, head, P:2 * P], start=False, stop=True)
                mm(o[:, P:3 * P], q[:, P:2 * P], kk, start=True, stop=False)
                mm(o[:, P:3 * P], C("flip"), biasT[:, head, :], start=False, stop=True).then_inc(full[b], 1)

            def attend2(k, pos):
                l = k[1]
                if pos == 2:
                    gemm_waits(k, 0)
                    for i, o in ((0, U2["qa"]), (1, U2["ka"])):
                        transposes_to((k, "aqk"), X[i], [u[:, t, o + p * P:o + p * P + P] for p in range(2) for t in range(NT)])
                elif pos == 3:
                    for i in range(2):
                        pe.wait_ge(free[X[i]], ev((k, "aqk"), X[i]))
                    if l == 0:
                        pe.wait_ge(bias_in, 16)
                    for h in range(4):
                        softmax_scores(k, (k, f"as{h}"), X[h], qM2[:, h % 2, h // 2, :], kT2[:, h // 2, :], h)
                elif pos == 5:
                    for h in range(4):
                        pe.wait_ge(free[X[h]], ev((k, f"as{h}"), X[h]))
                        transposes_to((k, f"at{h}"), X[h], [P2m[:, h, i * P:i * P + P] for i in range(3)])
                elif pos == 6:
                    pe.wait_ge(T["conv_in"], at("conv_in", l))
                    for i, o in ((0, U2["cb"]), (1, U2["bb"])):
                        transposes_to((k, "cx"), X[i], [u[:, t, o + p * P:o + p * P + P] for p in range(2) for t in range(NT)])
                elif pos == 7:
                    pe.wait_ge(free[X[2]], use((k, "ay"), X[2]))
                    for h in range(4):
                        pe.wait_ge(free[X[h]], ev((k, f"at{h}"), X[h]))
                    values((k, "ay"), X[2], 0, 4, lambda h: P2m[:, h, :], U2["va"])
                elif pos == 8:
                    gemm_waits(k, 3)
                    if l == 0:
                        pe.wait_ge(par2_loaded, 16 * NPAR2)
                    for b_ in range(2):
                        b = X[b_]
                        pe.wait_ge(free[b], use((k, "pl"), b))
                        for gg in range(2):
                            g = 2 * b_ + gg
                            o = bank[b][0:64, gg * 256:gg * 256 + 256]
                            us_ = [u[:, t, U2["pc"] + g * 64:U2["pc"] + g * 64 + 64] for t in range(NT)]
                            mm(o, us_[0], poolw[:, g, 0:256], start=True, stop=False)
                            last = mm(o[:, P:2 * P], us_[1], poolw[:, g, 256:384], start=False, stop=True)
                        last.then_inc(full[b], 1)
                elif pos == 9:
                    b, key = X[2], (k, "py")
                    for i in range(2):
                        pe.wait_ge(free[X[i]], ev((k, "pl"), X[i]))
                    pe.wait_ge(free[b], use(key, b))
                    for t in range(NT):
                        for g in range(4):
                            last = mm(bank[b][:, t * 256 + g * 64:t * 256 + g * 64 + 64], plT[:, g, t * P:t * P + P],
                                      wgrp[:, l, g, :], start=True, stop=True)
                    last.then_inc(full[b], 1)
                elif pos == 10:
                    gemm_waits(k, 4)
                    for i, o in ((0, U2["qd"]), (1, U2["kd"])):
                        transposes_to((k, "dqk"), X[i], [u[:, t, o + p * P:o + p * P + P] for p in range(2) for t in range(NT)])
                elif pos in (12, 17):
                    r = 0 if pos == 12 else 1
                    for i in range(2):
                        pe.wait_ge(free[X[i]], ev((k, "dqk"), X[i]))
                    for i in range(4):
                        softmax_scores(k, (k, f"ds{4 * r + i}"), X[i], qM2[:, i, r, :], kT2[:, r, :], 4 + 2 * r + i // 2)
                elif pos in (14, 19):
                    r = 0 if pos == 14 else 1
                    for i in range(2):
                        pe.wait_ge(T["dif_p"], at("dif_p", l, 2 * r + i + 1))
                        transposes_to((k, f"dt{2 * r + i}"), X[i], [P2m[:, 2 * i, j * P:j * P + P] for j in range(3)])
                elif pos in (15, 20):
                    r = 0 if pos == 15 else 1
                    b = X[2]
                    pe.wait_ge(free[b], use((k, f"dy{r}"), b))
                    for i in range(2):
                        pe.wait_ge(free[X[i]], ev((k, f"dt{2 * r + i}"), X[i]))
                    values((k, f"dy{r}"), b, 0, 2, lambda h: P2m[:, 2 * h, :], U2["vd"] + 128 * r)

            def mixer(k):
                c0, l = CH[k], k[1]
                first = k[0] == "mix1"
                nb, attend, ny = (16, attend1, 5) if first else (13, attend2, 4)
                for i in range(4):
                    pe.wait_ge(free[X[i]], ev(("norm", l, k[0]), X[i]))
                if k == ("mix2", 0):
                    pe.wait_ge(par2_loaded, 16 * NPAR2)
                    pe.wait_ge(setup2_v, 1)
                    pe.wait_ge(free[X[0]], use("bias_rows", X[0]))
                    mm(bank[X[0]][0:8, 0:384], tab[0:33, :], onehot[0:33, :], start=True, stop=True).then_inc(full[X[0]], 1)
                for pos in range(2 * nb):
                    n, half = divmod(pos, 2)
                    banks = [gbank(n, t) for t in range(NT)]
                    if half == 0:
                        for b in banks:
                            pe.wait_ge(free[b], use((k, "gemm", n), b))
                    gemm_half(banks, c0 + pos, 4 * half, half == 0, half == 1)
                    attend(k, pos)
                if first:
                    ys = [U1["fq"] + i * P for i in range(2)] + [U1["gq"] + i * P for i in range(2)] \
                        + [U1["rq"] + i * P for i in range(2)] + [U1["xbc"] + i * P for i in range(4)]
                    pe.wait_ge(free[X[0]], ev((k, "fy"), X[0]))
                    pe.wait_ge(T["y_gla"], at("y_gla", l))
                    pe.wait_ge(T["y_ret"], at("y_ret", l))
                else:
                    ys = [U2["qa"] + i * P for i in range(2)] + [None, None] + [U2["pc"] + i * P for i in range(2)] \
                        + [U2["qd"] + i * P for i in range(2)]
                    pe.wait_ge(free[X[2]], ev((k, "ay"), X[2]))
                    pe.wait_ge(free[X[2]], ev((k, "py"), X[2]))
                    pe.wait_ge(T["y_dif"], at("y_dif", l))
                for i in range(ny):
                    if first and i == 3:
                        pe.wait_ge(T["y_ssd"], at("y_ssd", l))
                    if not first and i == 1:
                        b = X[i % 4]
                        pe.wait_ge(T["y_conv"], at("y_conv", l))
                        pe.wait_ge(free[b], use((k, "yT", i), b))
                        mm(bank[b][:, :], ident, ybT[:, :, :].rearrange("p a b -> p (a b)"), start=True, stop=True).then_inc(full[b], 1)
                    else:
                        transposes_to((k, "yT", i), X[i % 4], [u[:, t, ys[2 * i + j]:ys[2 * i + j] + P] for j in range(2) for t in range(NT)])
                c = c0 + 2 * nb
                kt = 0
                for br in range(4):
                    banks = (0, 1, 2, 3) if br % 2 == 0 else X
                    tiles = 4 if first and br == 3 else 2
                    for b in banks:
                        pe.wait_ge(free[b], use((k, "up", br), b))
                    for j in range(0, tiles, 2):
                        i = kt // 2
                        pe.wait_ge(free[X[i % 4]], ev((k, "yT", i), X[i % 4]))
                        gemm_rows(banks, c, xt(kt), j == 0, j == tiles - 2)
                        c += 1
                        kt += 2
                name = "merged" if first else "merged_b"
                pe.wait_ge(T[name], at(name, l, 12))
                for i in range(4):
                    transposes_to((k, "mT", i), X[i], [u[:, t, (2 * i + j) * P:(2 * i + j + 1) * P] for j in range(2) for t in range(NT)])
                for b in range(4):
                    pe.wait_ge(free[b], use((k, "out"), b))
                for i in range(4):
                    pe.wait_ge(free[X[i]], ev((k, "mT", i), X[i]))
                    gemm_rows((0, 1, 2, 3), c, xt(2 * i), i == 0, i == 3)
                    c += 1

            def feed_forward(k, J):
                c0 = CH[k]
                for i in range(4):
                    pe.wait_ge(free[X[i]], ev(("norm", k[1], k[0]), X[i]))

                def up(j, it, c, half):
                    banks = [gbank(j, t) for t in range(NT)]
                    if half == 0:
                        for b in banks:
                            pe.wait_ge(free[b], use((k, "U", j), b) + 2 * it)
                    gemm_half(banks, c0 + c, 4 * half, half == 0, half == 1, it)

                def turn(j, it):
                    for t in range(NT):
                        b = gbank(j, t)
                        pe.wait_ge(free[b], use((k, "T", j), b) + 2 * it)
                        tr(bank[b][:, 0:P], gprod[:, t, 0:P])
                        tr(bank[b][:, P:2 * P], gprod[:, t, P:2 * P]).then_inc(full[b], 1)

                def down(j, it, c):
                    if j == 0:
                        for b in X:
                            pe.wait_ge(free[b], use((k, "D"), b))
                    for t in range(NT):
                        b = gbank(j, t)
                        pe.wait_ge(free[b], ev((k, "T", j), b) + 2 * it)
                    gemm_rows(X, c0 + c, lambda kk, t: (ghi[:, kk, t, :], glo[:, kk, t, :]), j == 0, j == J - 1, it)

                walk(pe, J, lambda j, it, c: up(j, it, c, 0), turn, lambda j, it, c: up(j, it, c, 1), down)

            def gather(k, e):
                pe.wait_ge(pick_ready, e + 1)
                for i in range(2):
                    b = 2 + i
                    pe.wait_ge(free[b], use((k, "gather"), b) + JU[b] * e)
                    for m in range(4):
                        for t in range(NT):
                            last = mm(bank[b][:, m * P:m * P + P], hrow[:, t, (4 * i + m) * P:(4 * i + m + 1) * P],
                                      pick[:, t, :], start=t == 0, stop=t == NT - 1)
                    last.then_inc(full[b], 1)

            def scatter(k, e):
                for b in (X[0], X[1]):
                    pe.wait_ge(free[b], use((k, "D"), b) + JU[b] * e)
                for b, (t, n) in zip((X[2], X[3], 2, 3), ((0, 0), (0, 1), (1, 0), (1, 1))):
                    pe.wait_ge(free[b], use((k, "scatter"), b) + JU[b] * e)
                    mm(bank[b][:, :], pick_t[:, t, :], y[:, n * 512:n * 512 + 512], start=True, stop=True).then_inc(full[b], 1)

            def expert_job(k, J, e):
                c0, per = CH[k], 3 * J

                def up(j, it, c, half):
                    b = j % 2
                    if half == 0:
                        pe.wait_ge(free[b], use((k, "U", j), b) + 2 * it + JU[b] * e)
                    if j == 0:
                        pe.wait_ge(free[2 + half], ev((k, "gather"), 2 + half) + JU[2 + half] * e)
                    s, h = (c0 + c) % RAW, (c0 + c) % HI
                    pe.wait_ge(lo_ready, c0 + c + 1 + 6 * it + per * e)
                    for m in range(4):
                        kt, w = 4 * half + m, slice(m * 512, m * 512 + 512)
                        mm(bank[b][:, :], xhi[:, kt, 0:P], hi[:, h, w], start=kt == 0, stop=False)
                        mm(bank[b][:, :], xlo[:, kt, 0:P], hi[:, h, w], start=False, stop=False)
                        last = mm(bank[b][:, :], xhi[:, kt, 0:P], lo[:, s, w], start=False, stop=kt == KT - 1)
                    last.then_inc(w_used, 1)

                def early():
                    scatter(k, e)
                    b = X[2]
                    pe.wait_ge(free[b], use((k, "turned"), b) + JU[b] * e)
                    for t in range(NT):
                        last = tr(bank[b][:, t * P:t * P + P], pick_g[:, t, :])
                    last.then_inc(full[b], 1)

                def turn(j, it):
                    b = j % 2
                    pe.wait_ge(free[b], use((k, "T", j), b) + 2 * it + JU[b] * e)
                    tr(bank[b][:, 0:P], gprod[:, 0, 0:P])
                    tr(bank[b][:, P:2 * P], gprod[:, 0, P:2 * P]).then_inc(full[b], 1)

                def down(j, it, c):
                    if j == 0:
                        for b in (X[0], X[1]):
                            pe.wait_ge(free[b], use((k, "D"), b) + JU[b] * e)
                    pe.wait_ge(free[j % 2], ev((k, "T", j), j % 2) + 2 * it + JU[j % 2] * e)
                    s, h = (c0 + c) % RAW, (c0 + c) % HI
                    pe.wait_ge(lo_ready, c0 + c + 1 + 6 * it + per * e)
                    for m in range(2):
                        for n in range(2):
                            o, first, final = bank[X[n]][:, :], j == 0 and m == 0, j == J - 1 and m == 1
                            w = slice(m * 1024 + n * 512, m * 1024 + n * 512 + 512)
                            mm(o, ghi[:, m, 0, :], hi[:, h, w], start=first, stop=False)
                            mm(o, glo[:, m, 0, :], hi[:, h, w], start=False, stop=False)
                            last = mm(o, ghi[:, m, 0, :], lo[:, s, w], start=False, stop=final)
                    last.then_inc(w_used, 1)

                walk(pe, J, lambda j, it, c: up(j, it, c, 0), turn, lambda j, it, c: up(j, it, c, 1), down,
                     early, lambda: gather(k, e + 1))

            pe.wait_ge(cst_loaded, 16)
            n = 0
            for k in phases:
                if k[0] == "norm":
                    norm(k, n)
                    n += 1
                elif k[0] in ("mix1", "mix2"):
                    mixer(k)
                elif k[0] != "moe":
                    feed_forward(k, FFJ[k[0]])
                else:
                    b, key = X[0], (k, "router")
                    for i in range(4):
                        pe.wait_ge(free[X[i]], ev(("norm", k[1], "moe"), X[i]))
                    for t in range(NT):
                        for kt in range(KT):
                            for j, xx in enumerate((xhi, xlo)):
                                last = mm(bank[b][:, t * 8:t * 8 + 8], xx[:, kt, t * P:t * P + P].bitcast(F32), router[:, kt, :],
                                          start=kt == 0 and j == 0, stop=kt == KT - 1 and j == 1)
                    last.then_inc(full[b], 1)
                    b = X[1]
                    pe.wait_ge(free[b], use((k, "rank"), b))
                    pe.wait_ge(chosen_ready, 1)
                    mm(bank[b][:, 0:8], C("triu"), chosen[:, 0, :], start=True, stop=True)
                    for o, m in ((8, "triu"), (16, "ones")):
                        mm(bank[b][:, o:o + 8], C("ones"), chosen[:, 0, :], start=True, stop=False)
                        last = mm(bank[b][:, o:o + 8], C(m), chosen[:, 1, :], start=False, stop=True)
                    last.then_inc(full[b], 1)
                    gather(k, 0)
                    pe.wait_ge(routed, 1)
                    nj = each_job(pe, lambda e: expert_job(k, FFJ["moe"], e))
                    scatter(k, nj)

        @block.scalar
        def _(act):
            links = [0]

            def link(ins):
                links[0] += 1
                ins.then_inc(act_link, 1)
                act.wait_ge(act_link, links[0])

            def go(dst, src, f, **kw):
                return nc.scalar.activation(dst, src, f, **kw)

            def conv(c, it=0, eo=0, per=0):
                if c >= END and not per:
                    return
                act.wait_ge(raw_full[c % RAW], 32 * (c // RAW + 1) + 32 * it + 32 * (per // RAW) * eo)
                if c >= HI:
                    act.wait_ge(w_used, c - HI + 1 + 6 * it + per * eo)
                go(hi[:, c % HI, :], raw[:, c % RAW, :], ACT.Copy).then_inc(hi_ready, 1)

            def rsqrt(dst, src, n, eps, done):
                link(go(dst, src, ACT.Ln, scale=1.0 / n, bias=eps))
                go(dst, dst, ACT.Exp, scale=-0.5).then_inc(done, 1)

            def norm(k, n, ready):
                for b, v in ready or []:
                    act.wait_ge(free[b], v)
                for t in range(NT):
                    last = go(hrow[:, t, :], x[:, t, :], ACT.Square, accum_out=nstat[:, t:t + 1])
                link(last)
                rsqrt(nstat[:, 4:6], nstat[:, 0:2], D, eps1, norm_rstd)
                if k[2] is None:
                    return
                for i in range(4):
                    b = X[i]
                    act.wait_ge(full[b], fl(k, b))
                    for j in range(2):
                        kt = 2 * i + j
                        last = go(xhi[:, kt, :], bank[b][:, j * 256:j * 256 + 256], ACT.Copy, scale=gain_col(k, kt))
                    last.then_inc(norm_hi, 1)

            def gain_col(k, kt):
                l, f = k[1], k[2]
                return cols1[:, l, kt:kt + 1] if f == "mix1" else cols1[:, l, 8 + kt:9 + kt] if f == "ffn1" \
                    else cols2[:, l, kt:kt + 1] if f == "mix2" else cols2[:, l, 8 + kt:9 + kt] if f == "ffn2" else 1.0

            def softmax_exp(key, b, h, dst, max_sem, max_val):
                act.wait_ge(max_sem, max_val)
                go(dst[:, 0:P], bank[b][:, 0:P], ACT.Exp, bias=small[:, 16 + 2 * h:17 + 2 * h], accum_out=small[:, 32 + h:33 + h])
                go(dst[:, P:3 * P], bank[b][:, P:3 * P], ACT.Exp, bias=small[:, 17 + 2 * h:18 + 2 * h],
                   accum_out=small[:, 36 + h:37 + h]).then_inc(free[b], 1)

            def evac(key, b, dst, src, f=ACT.Copy, **kw):
                go(dst, src, f, **kw).then_inc(free[b], 1)

            def gemm_out(k, n):
                first = k[0] == "mix1"
                mixb = 8 if first else 5
                act.wait_ge(w_used, CH[k] + 2 * n + 2)
                for t in range(NT):
                    b = gbank(n, t)
                    if n < mixb:
                        evac((k, "gemm", n), b, u[:, t, n * 512:n * 512 + 512], bank[b][:, :])
                    else:
                        o = (n - mixb) * 512
                        evac((k, "gemm", n), b, gates[:, t, o:o + 512], bank[b][:, :], ACT.Exp, scale=-1.0)

            def wait_full(key, b):
                act.wait_ge(full[b], fl(key, b))

            def own_gemm(k, n):
                for t in range(NT):
                    act.wait_ge(free[gbank(n, t)], ev((k, "gemm", n), gbank(n, t)))

            def work1(k, pos):
                l = k[1]
                if pos % 2 == 1:
                    gemm_out(k, pos // 2)
                if pos == 0:
                    wait_full((k, "small"), X[0])
                    evac(0, X[0], us[:, :, 0:28], bank[X[0]][:, 0:64].rearrange("p (t n) -> p t n", t=2)[:, :, 0:28])
                elif pos == 1:
                    wait_full((k, "glrT"), X[1])
                    evac(0, X[1], glrT[0:16, :], bank[X[1]][0:16, 0:256])
                elif pos == 2:
                    act.wait_ge(T["z_abs"], at("z_abs", l))
                    link(go(zlog[:, :, :], zlog[:, :, :], ACT.Exp, scale=-1.0))
                    go(zlog[:, :, :], zlog[:, :, :], ACT.Ln, bias=1.0).then_inc(T["z_log"], 1)
                    act.wait_ge(T["fox_ss"], at("fox_ss", l))
                    rsqrt(small[:, 0:16], small[:, 0:16], HD, eps1, T["fox_rstd"])
                elif pos == 4:
                    wait_full((k, "fqk"), X[1])
                    evac(0, X[1], kT[:, :, :].rearrange("p a b -> p (a b)"), bank[X[1]][:, :], scale=cols1[:, l, 27:28])
                    wait_full((k, "fqk"), X[0])
                    for m in range(2):
                        last = go(qM[:, m].rearrange("p a b -> p (a b)"), bank[X[0]][:, :], ACT.Copy, scale=cols1[:, l, 58 + m:59 + m])
                    last.then_inc(free[X[0]], 1)
                elif pos == 5:
                    for i in range(2):
                        b = X[2 + i]
                        wait_full((k, "cum"), b)
                        for j, (e, o, sc) in enumerate([(0, 0, 1.0), (1, 256, 1.0), (2, 256, -1.0)] if i == 0 else
                                                       [(3, 0, 1.0), (4, 0, -1.0), (5, 256, 1.0)]):
                            last = go(E[:, e, :], bank[b][:, o:o + 256], ACT.Exp, scale=sc)
                        last.then_inc(free[b], 1)
                elif pos in (6, 7):
                    for h in (0, 1) if pos == 6 else (2, 3):
                        softmax_exp((k, f"fs{h}"), X[h], h, Pm[:, h, :], T["fox_max"], at("fox_max", l, h + 1))
                elif pos in (8, 9):
                    h = 1 if pos == 8 else 3
                    wait_full((k, f"ft{h}"), X[h])
                    evac(0, X[h], Pm[:, h, :], bank[X[h]][:, 0:384])
                elif pos == 11:
                    wait_full((k, "gt"), X[1])
                    evac(0, X[1], kT[:, :, :].rearrange("p a b -> p (a b)"), bank[X[1]][:, :])
                    wait_full((k, "gt"), X[3])
                    for m in range(2):
                        last = go(qM[:, m].rearrange("p a b -> p (a b)"), bank[X[3]][:, :], ACT.Copy, scale=C("halfs", m, 1))
                    last.then_inc(free[X[3]], 1)
                elif pos == 12:
                    own_gemm(k, 3)
                    wait_full((k, "gt"), X[2])
                    wait_full((k, "gt"), X[3])
                    go(tg[:, :, :], u[:, :, U1["gr"]:U1["gr"] + 256], ACT.Exp, scale=-1.0).then_inc(T["gate_exp"], 1)
                elif pos == 15:
                    act.wait_ge(T["br_ss"], at("br_ss", l, 1))
                    rsqrt(small[:, 48:56], small[:, 48:56], HD, eps1, T["br_rstd"])
                elif pos == 16:
                    wait_full((k, "rt"), X[1])
                    evac(0, X[1], kT[:, :, :].rearrange("p a b -> p (a b)"), bank[X[1]][:, :])
                    wait_full((k, "rt"), X[3])
                    for m in range(2):
                        last = go(qM[:, m].rearrange("p a b -> p (a b)"), bank[X[3]][:, :], ACT.Copy, scale=C("halfs", m, 1))
                    last.then_inc(free[X[3]], 1)
                elif pos == 17:
                    act.wait_ge(T["y_gla"], at("y_gla", l))
                    go(tg[:, :, :], u[:, :, U1["rg"]:U1["rg"] + 256], ACT.Exp, scale=-1.0).then_inc(T["gate_exp"], 1)
                    for h in (0, 1):
                        go(decay_tile(h), C("rel"), ACT.Exp, scale=LOG_GAMMA[h]).then_inc(T["ret_decay"], 1)
                elif pos == 18:
                    for h in (2, 3):
                        act.wait_ge(free[X[h - 2]], ev((k, f"rs{h - 2}"), X[h - 2]))
                        go(decay_tile(h), C("rel"), ACT.Exp, scale=LOG_GAMMA[h]).then_inc(T["ret_decay"], 1)
                elif pos == 20:
                    act.wait_ge(T["br_ss"], at("br_ss", l, 2))
                    rsqrt(small[:, 48:56], small[:, 48:56], HD, eps1, T["br_rstd"])
                elif pos in (21, 22, 23):
                    i = pos - 21
                    act.wait_ge(T["conv_out"], at("conv_out", l, i + 1))
                    go(qM[:, i % 2], E[:, 2 * i:2 * i + 2, :], ACT.Exp, scale=-1.0).then_inc(T["conv_exp"], 1)
                elif pos == 24:
                    for t in range(NT):
                        wait_full((k, "xs"), X[t])
                        evac(0, X[t], u[:, t, U1["xbc"]:U1["xbc"] + 512], bank[X[t]][:, :])
                elif pos == 25:
                    for g in range(2):
                        wait_full((k, "cb"), X[2 + g])
                    go(tgz[:, :, :], u[:, :, U1["z"]:U1["z"] + 512], ACT.Exp, scale=-1.0).then_inc(T["z_exp"], 1)
                elif pos in (26, 29):
                    for h in range(4) if pos == 26 else range(4, 8):
                        wait_full((k, f"sg{h}"), X[h % 4])
                        evac(0, X[h % 4], Pm[:, h % 4, :], bank[X[h % 4]][:, 0:384], ACT.Exp)
                elif pos == 31:
                    act.wait_ge(T["br_ss"], at("br_ss", l, 3))
                    rsqrt(small[:, 48:52], small[:, 48:52], 256, eps1, T["br_rstd"])

            def decay_tile(h):
                return qD[:, h % 2].rearrange("p a b -> p (a b)")

            def work2(k, pos):
                l = k[1]
                if pos % 2 == 1:
                    gemm_out(k, pos // 2)
                if pos in (2, 10):
                    key = (k, "aqk" if pos == 2 else "dqk")
                    wait_full(key, X[1])
                    evac(0, X[1], kT2[:, :, :].rearrange("p a b -> p (a b)"), bank[X[1]][:, :])
                    wait_full(key, X[0])
                    for m in range(2 if pos == 2 else 4):
                        last = go(qM2[:, m].rearrange("p a b -> p (a b)"), bank[X[0]][:, :], ACT.Copy,
                                  scale=C("halfs", m, 1) if pos == 2 else C("quarter", m, 1))
                    last.then_inc(free[X[0]], 1)
                elif pos == 3:
                    for h in range(4):
                        softmax_exp((k, f"as{h}"), X[h], h, P2m[:, h, :], T["moba_max"], at("moba_max", l, h + 1))
                elif pos == 5:
                    for h in (1, 3):
                        wait_full((k, f"at{h}"), X[h])
                        evac(0, X[h], P2m[:, h, :], bank[X[h]][:, 0:384])
                elif pos == 8:
                    for i in range(2):
                        wait_full((k, "pl"), X[i])
                        evac(0, X[i], plT[:, 2 * i:2 * i + 2, :].rearrange("p a b -> p (a b)"), bank[X[i]][0:64, :])
                elif pos == 9:
                    wait_full((k, "py"), X[2])
                    evac(0, X[2], u[:, :, U2["pc"]:U2["pc"] + 256], bank[X[2]][:, :].rearrange("p (t n) -> p t n", t=2))
                elif pos in (12, 17):
                    r = 0 if pos == 12 else 1
                    for i in range(4):
                        softmax_exp((k, f"ds{4 * r + i}"), X[i], i, P2m[:, i, :], T["dif_max"], at("dif_max", l, 4 * r + i + 1))
                elif pos in (14, 19):
                    r = 0 if pos == 14 else 1
                    i = 1
                    wait_full((k, f"dt{2 * r + i}"), X[i])
                    evac(0, X[i], P2m[:, 2 * i, :], bank[X[i]][:, 0:384])
                elif pos == 21:
                    act.wait_ge(T["d_ss"], at("d_ss", l))
                    rsqrt(small[:, 48:56], small[:, 48:56], HD, eps2, T["d_rstd"])

            def hi_tiles(k, what, i, name, l, ycol):
                b = X[i % 4]
                wait_full((k, what, i), b)
                for j in range(2):
                    kt = 2 * i + j
                    kw = dict(scale=ycol[:, kt:kt + 1]) if ycol is not None else {}
                    last = go(xhi[:, kt, :], bank[b][:, j * 256:j * 256 + 256], ACT.Copy, **kw)
                last.then_inc(T[name], 1)

            def mixer(k):
                c0, l = CH[k], k[1]
                first = k[0] == "mix1"
                nb, work, ny = (16, work1, 5) if first else (13, work2, 4)
                for pos in range(2 * nb):
                    conv(c0 + pos + 2)
                    work(k, pos)
                yc = cols1[:, l, 16:26] if first else cols2[:, l, 17:25]
                for i in range(ny):
                    hi_tiles(k, "yT", i, "y_hi" if first else "y_hi_b", l, yc)
                for pos in range(2 * nb, 2 * nb + ny):
                    conv(c0 + pos + 2)
                for i in range(4):
                    hi_tiles(k, "mT", i, "m_hi" if first else "m_hi_b", l, None)
                for pos in range(2 * nb + ny, 2 * nb + ny + 4):
                    conv(c0 + pos + 2)

            def feed_forward(k, J):
                c0 = CH[k]

                def up_done(j, it, c):
                    conv(c0 + c + 2, it)
                    for t in range(NT):
                        act.wait_ge(w_used, c0 + c + 1 + 6 * it)
                        go(silu[:, t, :], bank[gbank(j, t)][:, 0:FB], ACT.Silu).then_inc(silu_done, 1)

                def turn(j, it):
                    for t in range(NT):
                        b = gbank(j, t)
                        act.wait_ge(full[b], fl((k, "T", j), b) + it)
                        go(ghi[:, :, t, :], bank[b][:, 0:FB].rearrange("p (a b) -> p a b", a=2), ACT.Copy).then_inc(ghi_done, 1)

                walk(act, J, lambda j, it, c: conv(c0 + c + 2, it), turn, up_done, lambda j, it, c: conv(c0 + c + 2, it))

            def gathered(k, e):
                for i in range(2):
                    b = 2 + i
                    act.wait_ge(full[b], fl((k, "gather"), b) + JF[b] * e)
                    go(xhi[:, 4 * i:4 * i + 4, 0:P], bank[b][:, :].rearrange("p (m n) -> p m n", m=4), ACT.Copy).then_inc(gather_hi, 1)

            def expert_job(k, J, e):
                c0, per = CH[k], 3 * J

                def up_done(j, it, c):
                    conv(c0 + c + 2, it, e, per)
                    act.wait_ge(w_used, c0 + c + 1 + 6 * it + per * e)
                    go(silu[:, 0, :], bank[j % 2][:, 0:FB], ACT.Silu).then_inc(silu_done, 1)

                def turn(j, it):
                    b = j % 2
                    act.wait_ge(full[b], fl((k, "T", j), b) + it + JF[b] * e)
                    go(ghi[:, :, 0, :], bank[b][:, 0:FB].rearrange("p (a b) -> p a b", a=2), ACT.Copy).then_inc(ghi_done, 1)

                walk(act, J, lambda j, it, c: conv(c0 + c + 2, it, e, per), turn, up_done,
                     lambda j, it, c: conv(c0 + c + 2, it, e, per), late=lambda: gathered(k, e + 1))
                act.wait_ge(w_used, c0 + per + per * e)
                for n in range(2):
                    go(y[:, n * 512:n * 512 + 512], bank[X[n]][:, :], ACT.Copy).then_inc(free[X[n]], 1)

            eps1, eps2 = epst[:, 0:1], epst[:, 1:2]
            act.wait_ge(setup_v, 1)
            for i in range(2):
                last = go(rot[:, i], ang[:, i], ACT.Sin)
            for l in range(L1):
                last = go(heads8[:, l, 0:8], heads8[:, l, 0:8], ACT.Exp)
            last.then_inc(setup_s, 1)
            act.wait_ge(x_loaded, 16)
            conv(0)
            conv(1)
            n = 0
            for k, ready in zip(phases, XREADY):
                if k[0] == "norm":
                    norm(k, n, ready)
                    n += 1
                elif k[0] in ("mix1", "mix2"):
                    if k == ("mix2", 0):
                        act.wait_ge(setup2_v, 1)
                        go(lam[:, :, 0:2], lam[:, :, 0:2], ACT.Exp).then_inc(setup_s, 1)
                    mixer(k)
                elif k[0] != "moe":
                    feed_forward(k, FFJ[k[0]])
                else:
                    act.wait_ge(route_m, 1)
                    for t in range(NT):
                        last = go(top2[:, t, 0:1], m8[:, t, 1:2], ACT.Exp, bias=top2[:, t, 1:2])
                    last.then_inc(route_e, 1)
                    gathered(k, 0)
                    act.wait_ge(routed, 1)
                    nj = each_job(act, lambda e: expert_job(k, FFJ["moe"], e))
                    for b in (X[2], X[3], 2, 3):
                        act.wait_ge(free[b], ev((k, "scatter"), b) + JU[b] * nj)
            norm(("norm", 0, None), n, None if phases[-1][0] == "moe" else last_x)

        @block.vector
        def _(dve):
            links = [0]
            V = nc.vector

            def link(ins):
                links[0] += 1
                ins.then_inc(dve_link, 1)
                dve.wait_ge(dve_link, links[0])

            def conv(c, it=0, eo=0, per=0):
                if c >= END and not per:
                    return
                dve.wait_ge(hi_ready, c + 1 + 6 * it + per * eo)
                V.tensor_tensor(lo[:, c % RAW, :], raw[:, c % RAW, :], hi[:, c % HI, :].bitcast(F32),
                                ALU.subtract).then_inc(lo_ready, 1)

            def lo_tiles(b, hi_sem, hi_val, i, gain):
                dve.wait_ge(hi_sem, hi_val)
                for j in range(2):
                    kt = 2 * i + j
                    src = bank[b][:, j * 256:j * 256 + 256]
                    g = gain(kt)
                    last = V.scalar_tensor_tensor(out=xlo[:, kt, :], in0=src, scalar=g, in1=xhi[:, kt, :].bitcast(F32),
                                                  op0=ALU.mult, op1=ALU.subtract)
                last.then_inc(free[b], 1)

            def norm(k, n):
                l, f = k[1], k[2]
                dve.wait_ge(norm_rstd, n + 1)
                for t in range(NT):
                    if f is None:
                        if t == 0:
                            dve.wait_ge(fgain_in, 16)
                        V.scalar_tensor_tensor(out=hrow[:, t, :], in0=x[:, t, :], scalar=nstat[:, 4 + t:5 + t], in1=fgain[:, :],
                                               op0=ALU.mult, op1=ALU.mult).then_inc(norm_h, 1)
                    elif f == "moe":
                        if t == 0:
                            dve.wait_ge(moe_gain_in, 16)
                        V.scalar_tensor_tensor(out=hrow[:, t, :], in0=x[:, t, :], scalar=nstat[:, 4 + t:5 + t], in1=mgain[:, :],
                                               op0=ALU.mult, op1=ALU.mult).then_inc(norm_h, 1)
                    else:
                        V.tensor_scalar(hrow[:, t, :], x[:, t, :], nstat[:, 4 + t:5 + t], None, ALU.mult).then_inc(norm_h, 1)
                if f is None:
                    return
                col = (lambda kt: cols1[:, l, kt:kt + 1]) if f == "mix1" else (lambda kt: cols1[:, l, 8 + kt:9 + kt]) if f == "ffn1" \
                    else (lambda kt: cols2[:, l, kt:kt + 1]) if f == "mix2" else (lambda kt: cols2[:, l, 8 + kt:9 + kt]) \
                    if f == "ffn2" else (lambda kt: 1.0)
                for i in range(4):
                    lo_tiles(X[i], norm_hi, 4 * n + i + 1, i, col)

            def wait_full(key, b):
                dve.wait_ge(full[b], fl(key, b))

            def out_of(k, n):
                for t in range(NT):
                    dve.wait_ge(free[gbank(n, t)], ev((k, "gemm", n), gbank(n, t)))

            def maxima(key, b, h, name, l, n):
                wait_full(key, b)
                V.tensor_reduce(small[:, 16 + 2 * h:17 + 2 * h], bank[b][:, 0:P], AX, ALU.max, negate=True)
                V.tensor_reduce(small[:, 17 + 2 * h:18 + 2 * h], bank[b][:, P:3 * P], AX, ALU.max, negate=True).then_inc(T[name], 1)

            def gates_one(k, n, first):
                mixb = 8 if first else 5
                o = (n - mixb) * 512
                out_of(k, n)
                gg = gates[:, :, o:o + 512]
                link(V.tensor_scalar_add(gg, gg, 1.0))
                V.reciprocal(gg, gg).then_inc(T["gate_one" if first else "gate_one_b"], 1)

            def heads(ap, d=HD):
                return ap.rearrange("p t (h d) -> p t h d", d=d)

            def bc(ap, n):
                return ap.unsqueeze(3).to_broadcast([P, NT, ap.shape[2], n])

            def two(ap):
                return ap.rearrange("p (t n) -> p t n", t=2)

            def sumsq(yv, scr, d, stat, done):
                link(V.tensor_tensor(scr, yv, yv, ALU.mult))
                V.tensor_reduce(stat, heads(scr, d), AX, ALU.add).then_inc(done, 1)

            def gated_norm(k, key, yo, go, which, done):
                l = k[1]
                b = X[0]
                wait_full(key, b)
                yv = u[:, :, yo:yo + 256]
                V.tensor_copy(yv, two(bank[b][:, :])).then_inc(free[b], 1)
                dve.wait_ge(free[b], ev(key, b))
                sumsq(yv, ysq[:, :, :], HD, small[:, 48:56].rearrange("p (t h) -> p t h", t=2), T["br_ss"])
                dve.wait_ge(T["gate_exp"], at("gate_exp", l, which))
                link(V.tensor_scalar_add(tg[:, :, :], tg[:, :, :], 1.0))
                link(V.reciprocal(tg[:, :, :], tg[:, :, :]))
                link(V.tensor_tensor(tg[:, :, :], tg[:, :, :], u[:, :, go:go + 256], ALU.mult))
                dve.wait_ge(T["br_rstd"], at("br_rstd", l, which))
                link(V.tensor_tensor(heads(yv), heads(yv), bc(small[:, 48:56].rearrange("p (t h) -> p t h", t=2), HD), ALU.mult))
                V.tensor_tensor(yv, yv, tg[:, :, :], ALU.mult).then_inc(T[done], 1)

            def clamp_to(dst, b, key, done=None):
                wait_full(key, b)
                V.tensor_tensor(dst, bank[b][:, 0:384], C("clamp"), ALU.min).then_inc(free[b], 1)
                dve.wait_ge(free[b], ev(key, b))
                r = V.scalar_tensor_tensor(out=dst, in0=C("clamp"), scalar=-1.0, in1=dst, op0=ALU.mult, op1=ALU.max)
                if done is not None:
                    r.then_inc(done, 1)
                return r

            def work1(k, pos):
                l = k[1]
                if pos % 2 == 1 and pos >= 17:
                    gates_one(k, pos // 2, True)
                if pos == 1:
                    out_of(k, 0)
                    sumsq(u[:, :, 0:512], sq[:, :, :], HD, small[:, 0:16].rearrange("p (t h) -> p t h", t=2), T["fox_ss"])
                elif pos == 2:
                    wait_full((k, "zg"), X[2])
                    V.tensor_copy(z[:, :, 0:256], two(bank[X[2]][:, :])).then_inc(free[X[2]], 1)
                    dve.wait_ge(free[X[0]], ev((k, "small"), X[0]))
                    link(V.tensor_copy(z[:, :, 256:268], us[:, :, 16:28]))
                    V.scalar_tensor_tensor(out=zlog[:, :, :], in0=z[:, :, :], scalar=-1.0, in1=z[:, :, :], op0=ALU.mult,
                                           op1=ALU.max).then_inc(T["z_abs"], 1)
                elif pos == 3:
                    dve.wait_ge(T["z_log"], at("z_log", l))
                    V.scalar_tensor_tensor(out=dtv[:, :, :], in0=z[:, :, 260:268], scalar=0.0, in1=zlog[:, :, 260:268],
                                           op0=ALU.max, op1=ALU.add)
                    link(V.scalar_tensor_tensor(out=z[:, :, 0:260], in0=z[:, :, 0:260], scalar=0.0, in1=zlog[:, :, 0:260],
                                                op0=ALU.min, op1=ALU.subtract))
                    V.tensor_scalar(z[:, :, 0:256], z[:, :, 0:256], 1.0 / 16.0, None, ALU.mult)
                    if l == 0:
                        dve.wait_ge(setup_s, 1)
                    V.scalar_tensor_tensor(out=z[:, :, 260:268], in0=dtv[:, :, :], scalar=-1.0,
                                           in1=heads8[:, l, 0:8].unsqueeze(1).to_broadcast([P, NT, 8]), op0=ALU.mult,
                                           op1=ALU.mult).then_inc(T["decay"], 1)
                    dve.wait_ge(T["fox_rstd"], at("fox_rstd", l))
                    q = heads(u[:, :, 0:512])
                    V.tensor_tensor(q, q, bc(small[:, 0:16].rearrange("p (t h) -> p t h", t=2), HD), ALU.mult).then_inc(T["fox_qn"], 1)
                elif pos in (6, 7):
                    for h in (0, 1) if pos == 6 else (2, 3):
                        maxima((k, f"fs{h}"), X[h], h, "fox_max", l, h + 1)
                    if pos == 6:
                        for i in (2, 3):
                            dve.wait_ge(free[X[i]], ev((k, "cum"), X[i]))
                        out_of(k, 1)
                        out_of(k, 2)
                        for e, t, o in ((2, 0, "gk"), (0, 0, "gk"), (1, 0, "gq"), (4, 1, "gk"), (3, 1, "gq"), (5, 1, "gq")):
                            last = V.tensor_tensor(E[:, e, :], E[:, e, :], u[:, t, U1[o]:U1[o] + 256], ALU.mult)
                        last.then_inc(T["gla_prod"], 1)
                elif pos in (8, 9):
                    h = 0 if pos == 8 else 2
                    wait_full((k, f"ft{h}"), X[h])
                    V.tensor_copy(Pm[:, h, :], bank[X[h]][:, 0:384]).then_inc(free[X[h]], 1)
                elif pos == 10:
                    for h in range(4):
                        dve.wait_ge(free[X[h]], ev((k, f"fs{h}"), X[h]))
                    link(V.reciprocal(small[:, 40:48], small[:, 32:40]))
                    wait_full((k, "fy"), X[0])
                    V.tensor_tensor(heads(u[:, :, 0:256]), heads(two(bank[X[0]][:, :])),
                                    bc(small[:, 40:48].rearrange("p (t h) -> p t h", t=2), HD), ALU.mult).then_inc(free[X[0]], 1)
                elif pos == 11:
                    b = X[2]
                    wait_full((k, "gt"), b)
                    V.tensor_copy(kE[:, :, :].rearrange("p a b -> p (a b)"), bank[b][:, 0:256])
                    for m in range(2):
                        last = V.tensor_scalar(qD[:, m].rearrange("p a b -> p (a b)"), bank[b][:, 256:512], C("halfs", m, 1), None, ALU.mult)
                    last.then_inc(free[b], 1)
                elif pos == 13:
                    for h in range(4):
                        clamp_to(Pm[:, h, :], X[h], (k, f"gs{h}"), T["gla_p"])
                elif pos == 15:
                    gated_norm(k, (k, "gy"), U1["gq"], U1["gr"], 1, "y_gla")
                elif pos == 18:
                    for h in range(4):
                        b, r = X[h], qD[:, h % 2].rearrange("p a b -> p (a b)")
                        wait_full((k, f"rs{h}"), b)
                        dve.wait_ge(T["ret_decay"], at("ret_decay", l, h + 1))
                        V.tensor_tensor(Pm[:, h, 0:256], bank[b][:, 0:256], r, ALU.mult)
                        V.tensor_tensor(Pm[:, h, 256:384], bank[b][:, 256:384], r[:, 0:P], ALU.mult).then_inc(free[b], 1)
                elif pos == 20:
                    gated_norm(k, (k, "ry"), U1["rq"], U1["rg"], 2, "y_ret")
                elif pos in (21, 22, 23):
                    i = pos - 21
                    b = X[1 + i]
                    wait_full((k, "xt"), b)
                    cw = lambda tap, j: cols1[:, l, 28 + 6 * tap + j:29 + 6 * tap + j]
                    src = [bank[b][:, j * 256:j * 256 + 256] for j in range(2)]
                    for j in range(2):
                        last = V.tensor_scalar(E[:, 2 * i + j, :], src[j], cw(3, 2 * i + j), cols1[:, l, 52 + 2 * i + j:53 + 2 * i + j],
                                               ALU.mult, ALU.add)
                    link(last)
                    for sh in (1, 2, 3):
                        for j in range(2):
                            dst = E[:, 2 * i + j, sh:S]
                            last = V.scalar_tensor_tensor(out=dst, in0=src[j][:, 0:S - sh], scalar=cw(3 - sh, 2 * i + j), in1=dst,
                                                          op0=ALU.mult, op1=ALU.add)
                        if sh < 3:
                            link(last)
                    last.then_inc(free[b], 1)
                    dve.wait_ge(free[b], ev((k, "xt"), b))
                    V.memset(small[:, 60:61], 0.0).then_inc(T["conv_out"], 1)
                    dve.wait_ge(T["conv_exp"], at("conv_exp", l, i + 1))
                    e = qM[:, i % 2]
                    link(V.tensor_scalar_add(e, e, 1.0))
                    link(V.reciprocal(e, e))
                    xx = E[:, 2 * i:2 * i + 2, :]
                    V.tensor_tensor(xx, xx, e, ALU.mult).then_inc(T["xbc"], 1)
                    if pos == 23:
                        dve.wait_ge(T["xbc"], at("xbc", l, 3))
                        for g in range(2):
                            last = V.tensor_scalar(kT[:, g, :], E[:, 5, :], C("half", g, 1), None, ALU.mult)
                        last.then_inc(T["ssd_c"], 1)
                elif pos == 24:
                    for g in range(2):
                        link(clamp_to(cbm[:, g, :], X[2 + g], (k, "cb")))
                    for t in range(NT):
                        dve.wait_ge(free[X[t]], ev((k, "xs"), X[t]))
                    V.tensor_tensor(heads(u[:, :, 256:768]), heads(u[:, :, U1["xbc"]:U1["xbc"] + 512]), bc(dtv[:, :, :], HD),
                                    ALU.mult).then_inc(T["ssd_x"], 1)
                elif pos in (26, 29):
                    for h in range(4) if pos == 26 else range(4, 8):
                        dve.wait_ge(free[X[h % 4]], ev((k, f"sg{h}"), X[h % 4]))
                        V.tensor_tensor(Pm[:, h % 4, :], Pm[:, h % 4, :], cbm[:, h // 4, :], ALU.mult).then_inc(T["ssd_p"], 1)
                    if pos == 26:
                        dve.wait_ge(T["z_exp"], at("z_exp", l))
                        link(V.tensor_scalar_add(tgz[:, :, :], tgz[:, :, :], 1.0))
                        link(V.reciprocal(tgz[:, :, :], tgz[:, :, :]))
                        link(V.tensor_tensor(tgz[:, :, :], tgz[:, :, :], u[:, :, U1["z"]:U1["z"] + 512], ALU.mult))
                elif pos in (28, 31):
                    r = 0 if pos == 28 else 1
                    key, b = (k, f"sy{r}"), X[0]
                    wait_full(key, b)
                    dve.wait_ge(T["ssd_dx"], at("ssd_dx", l, r + 1))
                    V.tensor_tensor(u[:, :, U1["xbc"] + 256 * r:U1["xbc"] + 256 * r + 256], two(bank[b][:, :]), qM[:, r],
                                    ALU.add).then_inc(free[b], 1)
                    if r == 1:
                        dve.wait_ge(free[b], ev(key, b))
                        yv = u[:, :, U1["xbc"]:U1["xbc"] + 512]
                        link(V.tensor_tensor(yv, yv, tgz[:, :, :], ALU.mult))
                        scr = qM[:, :, :, :].rearrange("p a b c -> p (a b c)").rearrange("p (t n) -> p t n", t=2)
                        sumsq(yv, scr, 256, small[:, 48:52].rearrange("p (t h) -> p t h", t=2), T["br_ss"])
                        dve.wait_ge(T["br_rstd"], at("br_rstd", l, 3))
                        V.tensor_tensor(heads(yv, 256), heads(yv, 256), bc(small[:, 48:52].rearrange("p (t h) -> p t h", t=2), 256),
                                        ALU.mult).then_inc(T["y_ssd"], 1)

            def work2(k, pos):
                l = k[1]
                if pos % 2 == 1 and pos >= 11:
                    gates_one(k, pos // 2, False)
                if pos == 3:
                    for h in range(4):
                        maxima((k, f"as{h}"), X[h], h, "moba_max", l, h + 1)
                elif pos == 5:
                    for h in (0, 2):
                        wait_full((k, f"at{h}"), X[h])
                        V.tensor_copy(P2m[:, h, :], bank[X[h]][:, 0:384]).then_inc(free[X[h]], 1)
                    out_of(k, 1)
                    out_of(k, 2)
                    cx = u[:, :, U2["cb"]:U2["cb"] + 256]
                    V.tensor_tensor(cx, cx, u[:, :, U2["xb"]:U2["xb"] + 256], ALU.mult).then_inc(T["conv_in"], 1)
                elif pos == 6:
                    cw = lambda tap, j: conv2[:, l, 2 * tap + j:2 * tap + j + 1]
                    b = X[0]
                    wait_full((k, "cx"), b)
                    for j in range(2):
                        last = V.tensor_scalar(ybT[:, j, :], bank[b][:, j * 256:j * 256 + 256], cw(2, j), None, ALU.mult)
                    link(last)
                    for sh in (1, 2):
                        for j in range(2):
                            dst = ybT[:, j, sh:S]
                            last = V.scalar_tensor_tensor(out=dst, in0=bank[b][:, j * 256:j * 256 + S - sh], scalar=cw(2 - sh, j), in1=dst,
                                                          op0=ALU.mult, op1=ALU.add)
                        if sh == 1:
                            link(last)
                    last.then_inc(free[b], 1)
                    dve.wait_ge(free[b], ev((k, "cx"), b))
                    b = X[1]
                    wait_full((k, "cx"), b)
                    yb = ybT[:, :, :].rearrange("p a b -> p (a b)")
                    V.tensor_tensor(yb, yb, bank[b][:, :], ALU.mult).then_inc(free[b], 1)
                    dve.wait_ge(free[b], ev((k, "cx"), b))
                    V.memset(small[:, 60:61], 0.0).then_inc(T["y_conv"], 1)
                elif pos == 7:
                    for h in range(4):
                        dve.wait_ge(free[X[h]], ev((k, f"as{h}"), X[h]))
                    link(V.reciprocal(small[:, 40:48], small[:, 32:40]))
                    wait_full((k, "ay"), X[2])
                    V.tensor_tensor(heads(u[:, :, 0:256]), heads(two(bank[X[2]][:, :])),
                                    bc(small[:, 40:48].rearrange("p (t h) -> p t h", t=2), HD), ALU.mult).then_inc(free[X[2]], 1)
                elif pos in (12, 17):
                    r = 0 if pos == 12 else 1
                    for i in range(4):
                        maxima((k, f"ds{4 * r + i}"), X[i], i, "dif_max", l, 0)
                    for i in range(4):
                        dve.wait_ge(free[X[i]], ev((k, f"ds{4 * r + i}"), X[i]))
                    link(V.reciprocal(small[:, 40:48], small[:, 32:40]))
                    for t in range(NT):
                        for i in (1, 3):
                            cc = 40 + 4 * t + i
                            last = V.tensor_scalar(small[:, cc:cc + 1], small[:, cc:cc + 1], lam[:, l, 2:3], None, ALU.mult)
                    link(last)
                    for i in range(2):
                        for t, s in ((0, slice(0, P)), (1, slice(P, 3 * P))):
                            cc = 40 + 4 * t + 2 * i + 1
                            last = V.tensor_scalar(P2m[:, 2 * i + 1, s], P2m[:, 2 * i + 1, s], small[:, cc:cc + 1], None, ALU.mult)
                        link(last)
                        for t, s in ((0, slice(0, P)), (1, slice(P, 3 * P))):
                            cc = 40 + 4 * t + 2 * i
                            last = V.scalar_tensor_tensor(out=P2m[:, 2 * i, s], in0=P2m[:, 2 * i, s], scalar=small[:, cc:cc + 1],
                                                          in1=P2m[:, 2 * i + 1, s], op0=ALU.mult, op1=ALU.add)
                        last.then_inc(T["dif_p"], 1)
                elif pos in (14, 19):
                    r = 0 if pos == 14 else 1
                    wait_full((k, f"dt{2 * r}"), X[0])
                    V.tensor_copy(P2m[:, 0, :], bank[X[0]][:, 0:384]).then_inc(free[X[0]], 1)
                elif pos in (15, 20):
                    r = 0 if pos == 15 else 1
                    b, key = X[2], (k, f"dy{r}")
                    wait_full(key, b)
                    V.tensor_copy(u[:, :, U2["qd"] + 128 * r:U2["qd"] + 128 * r + 128], two(bank[b][:, :])[:, :, 0:128]).then_inc(free[b], 1)
                    if r == 1:
                        dve.wait_ge(free[b], ev(key, b))
                        yv = u[:, :, U2["qd"]:U2["qd"] + 256]
                        sumsq(yv, qM2[:, 0], HD, small[:, 48:56].rearrange("p (t h) -> p t h", t=2), T["d_ss"])
                elif pos == 21:
                    dve.wait_ge(T["d_rstd"], at("d_rstd", l))
                    yv = heads(u[:, :, U2["qd"]:U2["qd"] + 256])
                    V.tensor_tensor(yv, yv, bc(small[:, 48:56].rearrange("p (t h) -> p t h", t=2), HD), ALU.mult).then_inc(T["y_dif"], 1)

            def mixer(k):
                c0, l = CH[k], k[1]
                first = k[0] == "mix1"
                nb, work, ny = (16, work1, 5) if first else (13, work2, 4)
                for pos in range(2 * nb):
                    conv(c0 + pos + 2)
                    work(k, pos)
                yc = cols1[:, l, 16:26] if first else cols2[:, l, 17:25]
                for i in range(ny):
                    lo_tiles(X[i % 4], T["y_hi" if first else "y_hi_b"], at("y_hi" if first else "y_hi_b", l, i + 1), i,
                             lambda kt: yc[:, kt:kt + 1])
                pos = 2 * nb
                one = "gate_one" if first else "gate_one_b"
                for br in range(4):
                    banks = (0, 1, 2, 3) if br % 2 == 0 else X
                    for j in range(2 if first and br == 3 else 1):
                        conv(c0 + pos + 2)
                        pos += 1
                    dve.wait_ge(w_used, c0 + pos)
                    dve.wait_ge(T[one], at(one, l, 2 * br + 2))
                    for t in range(NT):
                        for n in range(2):
                            b = banks[2 * t + n]
                            gg = gates[:, t, br * 1024 + n * 512:br * 1024 + n * 512 + 512]
                            dst = u[:, t, n * 512:n * 512 + 512] if br == 0 else gg
                            V.tensor_tensor(dst, bank[b][:, :], gg, ALU.mult).then_inc(free[b], 1)
                for i in range(4):
                    lo_tiles(X[i], T["m_hi" if first else "m_hi_b"], at("m_hi" if first else "m_hi_b", l, i + 1), i, lambda kt: 1.0)
                for j in range(4):
                    conv(c0 + pos + 2)
                    pos += 1
                dve.wait_ge(w_used, c0 + pos)
                for t in range(NT):
                    for n in range(2):
                        b = 2 * t + n
                        xx = x[:, t, n * 512:n * 512 + 512]
                        V.tensor_tensor(xx, bank[b][:, :], xx, ALU.add).then_inc(free[b], 1)

            def feed_forward(k, J):
                c0, f0 = CH[k], FFB[k]

                def up_done(j, it, c):
                    conv(c0 + c + 2, it)
                    for t in range(NT):
                        b = gbank(j, t)
                        dve.wait_ge(silu_done, f0 + 2 * j + t + 1 + 4 * it)
                        V.tensor_tensor(gprod[:, t, :], bank[b][:, FB:2 * FB], silu[:, t, :], ALU.mult).then_inc(free[b], 1)

                def turn(j, it):
                    for t in range(NT):
                        b = gbank(j, t)
                        dve.wait_ge(ghi_done, f0 + 2 * j + t + 1 + 4 * it)
                        V.tensor_tensor(glo[:, :, t, :], bank[b][:, 0:FB].rearrange("p (a b) -> p a b", a=2),
                                        ghi[:, :, t, :].bitcast(F32), ALU.subtract).then_inc(free[b], 1)

                walk(dve, J, lambda j, it, c: conv(c0 + c + 2, it), turn, up_done, lambda j, it, c: conv(c0 + c + 2, it))
                dve.wait_ge(w_used, c0 + 3 * J)
                for t in range(NT):
                    for n in range(2):
                        b = X[2 * t + n]
                        xx = x[:, t, n * 512:n * 512 + 512]
                        V.tensor_tensor(xx, bank[b][:, :], xx, ALU.add).then_inc(free[b], 1)

            def pick_tokens(e):
                for t in range(NT):
                    where = jobpos[:, t, bass.ds(e, 1)]
                    V.tensor_scalar(pick[:, t, :], C("slots"), where, None, ALU.is_equal)
                    last = V.tensor_scalar(pick_g[:, t, :], C("slots"), where, jobgate[:, t, bass.ds(e, 1)], ALU.is_equal, ALU.mult)
                last.then_inc(pick_ready, 1)

            def gathered(k, e):
                for i in range(2):
                    b, rows = 2 + i, slice(4 * i, 4 * i + 4)
                    dve.wait_ge(gather_hi, 2 * e + i + 1)
                    V.tensor_tensor(xlo[:, rows, 0:P], bank[b][:, :].rearrange("p (m n) -> p m n", m=4),
                                    xhi[:, rows, 0:P].bitcast(F32), ALU.subtract).then_inc(free[b], 1)

            def scattered(k, e):
                for b, (t, n) in zip((X[2], X[3], 2, 3), ((0, 0), (0, 1), (1, 0), (1, 1))):
                    xx = x[:, t, n * 512:n * 512 + 512]
                    dve.wait_ge(full[b], fl((k, "scatter"), b) + JF[b] * e)
                    V.tensor_tensor(xx, bank[b][:, :], xx, ALU.add).then_inc(free[b], 1)

            def expert_job(k, J, e):
                c0, per, f0 = CH[k], 3 * J, FFB[k]

                def up_done(j, it, c):
                    conv(c0 + c + 2, it, e, per)
                    dve.wait_ge(silu_done, f0 + j + 1 + 2 * it + J * e)
                    V.tensor_tensor(gprod[:, 0, :], bank[j % 2][:, FB:2 * FB], silu[:, 0, :], ALU.mult).then_inc(free[j % 2], 1)

                def turn(j, it):
                    dve.wait_ge(ghi_done, f0 + j + 1 + 2 * it + J * e)
                    V.tensor_tensor(glo[:, :, 0, :], bank[j % 2][:, 0:FB].rearrange("p (a b) -> p a b", a=2),
                                    ghi[:, :, 0, :].bitcast(F32), ALU.subtract).then_inc(free[j % 2], 1)

                def early():
                    scattered(k, e)
                    b = X[2]
                    dve.wait_ge(full[b], fl((k, "turned"), b) + JF[b] * e)
                    V.tensor_copy(pick_t[:, :, :].rearrange("p t n -> p (t n)"), bank[b][:, 0:NT * P]).then_inc(free[b], 1)
                    pick_tokens(e + 1)

                walk(dve, J, lambda j, it, c: conv(c0 + c + 2, it, e, per), turn, up_done,
                     lambda j, it, c: conv(c0 + c + 2, it, e, per), early, lambda: gathered(k, e + 1))

            def route(k):
                b, key = X[0], (k, "router")
                V.memset(pick_t[:, :, :], 0.0)
                V.memset(y[:, :], 0.0)
                V.memset(jobpos[:, :, :], -1.0)
                V.memset(jobgate[:, :, :], 0.0)
                wait_full(key, b)
                V.tensor_copy(lg8[:, :, :], two(bank[b][:, 0:16])).then_inc(free[b], 1)
                dve.wait_ge(free[b], ev(key, b))
                for t in range(NT):
                    last = V.max(m8[:, t, :], lg8[:, t, :])
                link(last)
                for t in range(NT):
                    V.max_index(i8[:, t, :], m8[:, t, :], lg8[:, t, :])
                    last = V.tensor_scalar(top2[:, t, 1:2], m8[:, t, 0:1], -1.0, None, ALU.mult)
                last.then_inc(route_m, 1)
                dve.wait_ge(route_m, 1)
                link(V.tensor_copy(i8f[:, :, :], i8[:, :, 0:2]))
                for t in range(NT):
                    last = V.tensor_scalar(chosen[:, t, :], C("experts"), i8f[:, t, 0:1], None, ALU.is_equal)
                link(last)
                for t in range(NT):
                    last = V.scalar_tensor_tensor(out=chosen[:, t, :], in0=C("experts"), scalar=i8f[:, t, 1:2], in1=chosen[:, t, :],
                                                  op0=ALU.is_equal, op1=ALU.add)
                last.then_inc(chosen_ready, 1)
                dve.wait_ge(route_e, 1)
                link(V.tensor_scalar_add(top2[:, :, 2:3], top2[:, :, 0:1], 1.0))
                link(V.reciprocal(top2[:, :, 2:3], top2[:, :, 2:3]))
                link(V.tensor_tensor(top2[:, :, 3:4], top2[:, :, 2:3], top2[:, :, 0:1], ALU.mult))
                for t in range(NT):
                    V.tensor_scalar(gate8[:, t, :], C("experts"), i8f[:, t, 0:1], top2[:, t, 2:3], ALU.is_equal, ALU.mult)
                    last = V.tensor_scalar(lg8[:, t, :], C("experts"), i8f[:, t, 1:2], top2[:, t, 3:4], ALU.is_equal, ALU.mult)
                link(last)
                V.tensor_tensor(jobgate[:, :, 0:NE], gate8[:, :, :], lg8[:, :, :], ALU.add)
                b, key = X[1], (k, "rank")
                wait_full(key, b)
                V.tensor_copy(rank[:, :, :].rearrange("p t n -> p (t n)"), bank[b][:, 0:24]).then_inc(free[b], 1)
                dve.wait_ge(free[b], ev(key, b))
                link(V.scalar_tensor_tensor(out=rank[:, 0:NT, :], in0=chosen[:, :, :], scalar=1e6, in1=rank[:, 0:NT, :],
                                            op0=ALU.mult, op1=ALU.add))
                link(V.tensor_scalar(jobpos[:, :, 0:NE], rank[:, 0:NT, :], 1000001.0, None, ALU.subtract))
                pick_tokens(0)
                link(V.tensor_scalar(over[:, 0, :], rank[:, 2, :], float(P), None, ALU.is_gt))
                V.tensor_reduce(jobs_f[:, MORE:MORE + 1], over[:, 0, :], AX, ALU.add)
                link(V.tensor_tensor(over[:, 1, :], over[:, 0, :], C("countdown"), ALU.mult))
                link(V.max(over[:, 2, :], over[:, 1, :]))
                for i in range(MORE):
                    link(V.tensor_scalar(over[:, 3, :], over[:, 1, :], over[:, 2, i:i + 1], None, ALU.is_equal))
                    for src, dst in ((jobpos, jobpos), (jobgate, jobgate)):
                        for t in range(NT):
                            last = V.tensor_tensor(prod8[:, t, :], src[:, t, 0:NE], over[:, 3, :], ALU.mult)
                        link(last)
                        link(V.tensor_reduce(dst[:, :, NE + i:NE + i + 1], prod8[:, :, :], AX, ALU.add))
                V.tensor_scalar(jobpos[:, :, NE:NE + MORE], jobpos[:, :, NE:NE + MORE], float(P), None, ALU.subtract)
                link(V.tensor_scalar(jobs_f[:, 0:MORE], over[:, 2, 0:MORE], -1.0, float(NE), ALU.mult, ALU.add))
                link(V.tensor_scalar(jobs_f[:, 0:MORE], jobs_f[:, 0:MORE], float(NE - 1), None, ALU.min))
                link(V.tensor_scalar_add(jobs_f[:, MORE:MORE + 1], jobs_f[:, MORE:MORE + 1], float(NE)))
                V.tensor_copy(jobs_i[:, :], jobs_f[:, :]).then_inc(routed, 1)
                dve.wait_ge(routed, 1)

            for b in range(8):
                V.memset(small[:, 56 + b:57 + b], 0.0).then_inc(free[b], 1)
            V.memset(epst[:, 0:1], 1e-6)
            V.memset(epst[:, 1:2], 1e-5)
            V.memset(us[:, :, :], 0.0)
            V.memset(glrT[:, :], 1.0)
            V.memset(cols1[:, :, 16:18], 1.0)
            V.memset(cols2[:, :, 17:21], 1.0)
            link(V.memset(brow[:, :, 0:16], 0.0))
            dve.wait_ge(cst_loaded, 16)
            dve.wait_ge(par_loaded, 16 * NPAR)
            link(V.tensor_copy(posf[:, :], posi[:, :]))
            for t in range(NT):
                last = V.tensor_scalar(ang[:, 0, t, :], C("freq"), posf[:, t:t + 1], None, ALU.mult)
            link(last)
            A, Kt_, R = ang[:, 0], ang[:, 2], ang[:, 3]
            link(V.tensor_scalar(Kt_, A, 1.0 / (2 * math.pi), 12582912.0, ALU.mult, ALU.add))
            link(V.tensor_scalar(Kt_, Kt_, 12582912.0, None, ALU.subtract))
            link(V.scalar_tensor_tensor(out=A, in0=Kt_, scalar=-6.28125, in1=A, op0=ALU.mult, op1=ALU.add))
            link(V.scalar_tensor_tensor(out=A, in0=Kt_, scalar=-TWO_PI_2, in1=A, op0=ALU.mult, op1=ALU.add))
            link(V.scalar_tensor_tensor(out=A, in0=Kt_, scalar=-TWO_PI_3, in1=A, op0=ALU.mult, op1=ALU.add))
            link(V.tensor_scalar(A, A, 3.1415925, -3.1415925, ALU.min, ALU.max))
            link(V.tensor_scalar(ang[:, 1], A, math.pi / 2, None, ALU.add))
            link(V.tensor_scalar(R, ang[:, 1], math.pi, -2 * math.pi, ALU.is_gt, ALU.mult))
            link(V.tensor_tensor(ang[:, 1], ang[:, 1], R, ALU.add))
            link(V.tensor_scalar(ang[:, 1], ang[:, 1], 3.1415925, -3.1415925, ALU.min, ALU.max))
            for l in range(L1):
                for m in range(2):
                    V.tensor_scalar(cols1[:, l, 58 + m:59 + m], cols1[:, l, 26:27], C("halfs", m, 1), None, ALU.mult)
                V.tensor_copy(cols1[:, l, 19:20], cols1[:, l, 18:19])
                last = V.tensor_copy(cols1[:, l, 21:22], cols1[:, l, 20:21])
            last.then_inc(setup_v, 1)
            conv(0)
            conv(1)
            n = 0
            for k in phases:
                if k[0] == "norm":
                    norm(k, n)
                    n += 1
                elif k[0] in ("mix1", "mix2"):
                    if k == ("mix2", 0):
                        for i in range(2):
                            last = V.tensor_tensor(lam_in[:, :, 2 * i], lam_in[:, :, 2 * i], lam_in[:, :, 2 * i + 1], ALU.mult)
                        link(last)
                        for i in range(2):
                            last = V.tensor_reduce(lam[:, :, i:i + 1], lam_in[:, :, 2 * i], AX, ALU.add)
                        for l in range(L1):
                            s = 1.0 - LAM_INIT[l]
                            last = V.tensor_scalar(cols2[:, l, 23:24], cols2[:, l, 23:24], s, None, ALU.mult)
                        link(last)
                        for l in range(L1):
                            last = V.tensor_copy(cols2[:, l, 24:25], cols2[:, l, 23:24])
                        last.then_inc(setup2_v, 1)
                        dve.wait_ge(setup_s, 2)
                        link(V.tensor_tensor(lam[:, :, 2:3], lam[:, :, 1:2], lam[:, :, 0:1], ALU.subtract))
                        for l in range(L1):
                            last = V.tensor_scalar(lam[:, l, 2:3], lam[:, l, 2:3], LAM_INIT[l], None, ALU.subtract)
                        link(last)
                        b = X[0]
                        wait_full("bias_rows", b)
                        V.tensor_copy(tabT[0:8, :], bank[b][0:8, 0:384]).then_inc(free[b], 1)
                    mixer(k)
                elif k[0] != "moe":
                    feed_forward(k, FFJ[k[0]])
                else:
                    route(k)
                    gathered(k, 0)
                    nj = each_job(dve, lambda e: expert_job(k, FFJ["moe"], e))
                    scattered(k, nj)
            norm(("norm", 0, None), n)

        @block.gpsimd
        def _(pool):
            G = nc.gpsimd
            links = [0]
            loads = [0, 0]

            def link(ins):
                links[0] += 1
                ins.then_inc(pool_link, 1)
                pool.wait_ge(pool_link, links[0])

            def load(dst, src, second=False):
                loads[second] += 1
                pool.dma_start(dst, src).then_inc(par2_loaded if second else par_loaded, 16)

            pool.dma_start(x[:, :, :], a["x"][0].rearrange("(t p) d -> p t d", p=P)).then_inc(x_loaded, 16)
            pool.dma_start(cst[:, :], a["cst"]).then_inc(cst_loaded, 16)
            load(posi[:, :], a["positions"][0].rearrange("(t p) -> p t", p=P))
            for l in range(L1):
                load(cols1[:, l, 0:8], a["ln1"][l].rearrange("(k p) -> p k", p=P))
                load(cols1[:, l, 8:16], a["ln2"][l].rearrange("(k p) -> p k", p=P))
                load(cols1[:, l, 22:26], a["ssd_norm"][l].rearrange("(k p) -> p k", p=P))
                for tap in range(4):
                    load(cols1[:, l, 28 + 6 * tap:34 + 6 * tap], a["ssd_conv_w"][l, tap].rearrange("(k p) -> p k", p=P))
                load(cols1[:, l, 52:58], a["ssd_conv_b"][l].rearrange("(k p) -> p k", p=P))
                for name, cc in (("gla_norm", 18), ("ret_norm", 20), ("fox_qn", 26), ("fox_kn", 27)):
                    for h in range(2):
                        load(cols1[64 * h:64 * h + 64, l, cc:cc + 1], a[name][l].rearrange("(p o) -> p o", o=1))
                o = 0
                for f, w in W1SMALL:
                    load(wsm[:, l, :, o:o + w], a["w_in"][l].rearrange("(k p) n -> p k n", p=P)[:, :, f:f + w])
                    o += w
                load(gw2[0:16, l, :], a["gla_w2"][l])
                load(gw2[16:17, l, :], a["gla_b"][l:l + 1])
            load(brow[0:1, :, 16:20], a["fox_bf"].unsqueeze(0))
            load(brow[0:1, :, 20:28], a["ssd_dt_bias"].unsqueeze(0))
            load(heads8[:, :, 0:8], a["ssd_a_log"].partition_broadcast(P))
            load(heads8[:, :, 8:16], a["ssd_d"].partition_broadcast(P))
            for l in range(L1):
                load(cols2[:, l, 0:8], a["mix_norm_g_2"][l].rearrange("(k p) -> p k", p=P))
                load(cols2[:, l, 8:16], a["ffn_norm_g_2"][l].rearrange("(k p) -> p k", p=P))
                for tap in range(3):
                    load(conv2[:, l, 2 * tap:2 * tap + 2], a["conv_w_2"][l, tap].rearrange("(k p) -> p k", p=P))
                load(cols2[:, l, 21:23], a["pool_scale_2"][l].rearrange("(k p) -> p k", p=P))
                for h in range(2):
                    load(cols2[64 * h:64 * h + 64, l, 23:24], a["diff_subln_g_2"][l].rearrange("(p o) -> p o", o=1))
            load(lam_in[:, :, :, :], a["diff_lambda_2"].partition_broadcast(P))
            assert loads[0] == NPAR, loads

            def build(k, h, col, slot):
                for j, (m, t) in enumerate((("after", 0), ("ones", 1), ("after", 1))):
                    last = G.tensor_scalar(Bld[:, slot, j * P:j * P + P], C(m), z[:, t, col:col + 1], None, ALU.mult)
                last.then_inc(T["builds"], 1)

            def mix1(k):
                l, c0 = k[1], CH[k]
                pool.wait_ge(T["decay"], at("decay", l))
                for h in range(4):
                    build(k, h, 256 + h, h)
                for n in (3, 4):
                    for t in range(NT):
                        pool.wait_ge(free[gbank(n, t)], ev((k, "gemm", n), gbank(n, t)))
                if l == 0:
                    pool.wait_ge(setup_s, 1)
                for t in range(NT):
                    v = u[:, t, U1["rq"]:U1["rq"] + 512].rearrange("p (h j d) -> p h j d", j=2, d=32)
                    x1, x2 = v[:, :, 0, :], v[:, :, 1, :]
                    sn, cs = (rot[:, i, t, :].unsqueeze(1).to_broadcast([P, 8, 32]) for i in range(2))
                    t0, t1, t2 = (rope_t[:, i, t] for i in range(3))
                    G.tensor_tensor(t0, x1, cs, ALU.mult)
                    G.tensor_tensor(t1, x2, sn, ALU.mult)
                    link(G.tensor_tensor(t2, x1, sn, ALU.mult))
                    link(G.tensor_tensor(x1, t0, t1, ALU.subtract))
                    link(G.tensor_tensor(t0, x2, cs, ALU.mult))
                    last = G.tensor_tensor(x2, t2, t0, ALU.add)
                last.then_inc(T["rope"], 1)
                for h in range(4):
                    pool.wait_ge(full[X[h]], fl((k, f"fs{h}"), X[h]))
                    build(k, h, 260 + h, h)
                pool.wait_ge(T["xbc"], at("xbc", l, 3))
                for t in range(NT):
                    pool.wait_ge(free[X[t]], ev((k, "xs"), X[t]))
                for r in range(2):
                    for t in range(NT):
                        xs = u[:, t, U1["xbc"] + 256 * r:U1["xbc"] + 256 * r + 256].rearrange("p (h d) -> p h d", d=HD)
                        last = G.tensor_tensor(qM[:, r, t, :].rearrange("p (h d) -> p h d", d=HD), xs,
                                               heads8[:, l, 8 + 4 * r:12 + 4 * r].unsqueeze(2).to_broadcast([P, 4, HD]), ALU.mult)
                    last.then_inc(T["ssd_dx"], 1)
                for h in range(4, 8):
                    pool.wait_ge(full[X[h % 4]], fl((k, f"sg{h - 4}"), X[h % 4]))
                    build(k, h, 260 + h, h % 4)

            def merge(k):
                l, name = k[1], "merged" if k[0] == "mix1" else "merged_b"
                for br in range(1, 4):
                    banks = (0, 1, 2, 3) if br % 2 == 0 else X
                    for t in range(NT):
                        for n in range(2):
                            b0, b = 2 * t + n, banks[2 * t + n]
                            if br == 1:
                                pool.wait_ge(free[b0], ev((k, "up", 0), b0))
                            else:
                                pool.wait_ge(T[name], at(name, l, 4 * (br - 2) + 2 * t + n + 1))
                            pool.wait_ge(free[b], ev((k, "up", br), b))
                            m = u[:, t, n * 512:n * 512 + 512]
                            G.tensor_tensor(m, m, gates[:, t, br * 1024 + n * 512:br * 1024 + n * 512 + 512], ALU.add).then_inc(T[name], 1)

            for k, ready in zip(phases, XREADY):
                if k[0] == "norm" and k[2] == "mix2" and k[1] == 0:
                    for b, v in ready:
                        pool.wait_ge(free[b], v)
                    for l in range(L1):
                        load(wgrp[:, l], a["pool_w_2"][l].rearrange("g c d -> c g d"), True)
                    load(router[:, :, :], a["moe_router_2"][0].rearrange("(k p) n -> p k n", p=P), True)
                    load(poolw[:, :, :], a["poolw"], True)
                    load(onehot[:, :], a["onehot"], True)
                    load(tab[0:32, :], a["bias_table_2"], True)
                    load(tab[32:33, :], a["ones8"], True)
                    assert loads[1] == NPAR2, loads
                elif k[0] == "mix1":
                    mix1(k)
                    merge(k)
                elif k[0] == "mix2":
                    if k[1] == 0:
                        pool.wait_ge(free[X[0]], ev("bias_rows", X[0]))
                        pool.dma_start(scratch, tabT[0:8, :]).then_inc(rows_out, 16)
                        pool.wait_ge(rows_out, 16)
                        pool.dma_start(biasT[:, :, :], bass.AP(scratch.tensor, 0, [[1, P], [384, 8], [1, S]])).then_inc(bias_in, 16)
                    merge(k)
                    if k[1] == L1 - 1 and ("moe", k[1]) in phases:
                        pool.wait_ge(full[X[2]], fl((k, "dy1"), X[2]))
                        pool.dma_start(mgain[:, :], a["ffn_norm_g_2"][k[1]].partition_broadcast(P)).then_inc(moe_gain_in, 16)
            for b, v in last_x:
                pool.wait_ge(free[b], v)
            pool.dma_start(fgain[:, :], a["final_norm_g_2"].partition_broadcast(P)).then_inc(fgain_in, 16)


FFJ = {"ffn1": FH1 // FB, "ffn2": FH1 // FB, "moe": FH2 // FB}
LAM_INIT = [0.8 - 0.6 * math.exp(-0.3 * i) for i in range(L1)]
LOG_GAMMA = [float(np.log(np.float32(1.0) - np.float32(2.0) ** np.float32(-5.0 - h))) for h in range(RH)]
TWO_PI_2 = float(np.float32(2 * math.pi - 6.28125))
TWO_PI_3 = 2 * math.pi - 6.28125 - TWO_PI_2
NPAR = 1 + L1 * (3 + 4 + 1 + 8 + 3 + 2) + 4 + L1 * (2 + 3 + 1 + 2) + 1
NPAR2 = L1 + 5

_INS = ["x", "positions", "ln1", "ln2", "w_in", "fox_bf", "fox_qn", "fox_kn", "gla_w2", "gla_b", "gla_norm", "ret_norm",
        "ssd_conv_w", "ssd_conv_b", "ssd_dt_bias", "ssd_a_log", "ssd_d", "ssd_norm", "w_up_a", "w_up_b", "w_up_c", "w_up_d",
        "w_out", "w_ffn_in", "w_ffn_out", "bias_table_2", "mix_norm_g_2", "w_in_2", "conv_w_2", "pool_w_2", "pool_scale_2",
        "diff_lambda_2", "diff_subln_g_2", "branch_proj_2", "w_out_2", "ffn_norm_g_2", "dense_w1_2", "dense_w3_2",
        "dense_w2_2", "moe_router_2", "moe_w1_2", "moe_w3_2", "moe_w2_2", "final_norm_g_2"]


def kernel(**inputs):
    import concourse.bacc as bacc
    from concourse.bass_utils import run_bass_kernel_spmd as run

    nc = bacc.Bacc("TRN2", target_bir_lowering=False, num_devices=1)
    arrays = {name: np.ascontiguousarray(inputs[name]) for name in _INS}
    arrays.update(cst=constants(), onehot=bias_buckets(), poolw=pool_matrices(), ones8=np.ones((1, 8), np.float32))
    a = {name: nc.dram_tensor(f"in_{name}", v.shape, mybir.dt.from_np(v.dtype), kind="ExternalInput").ap()
         for name, v in arrays.items()}
    out = nc.dram_tensor("out", (S, D), F32, kind="ExternalOutput").ap()
    program(nc, a, out)
    r = run(nc, [{f"in_{name}": v for name, v in arrays.items()}], core_ids=[0])
    return r.results[0]["out"].reshape(1, S, D)
```

```python
import math
from contextlib import ExitStack

import numpy as np
import concourse.bass as bass
from concourse import mybir

F32 = mybir.dt.float32
F32R = mybir.dt.float32r
I32 = mybir.dt.int32
U32 = mybir.dt.uint32
ALU = mybir.AluOpType
ACT = mybir.ActivationFunctionType
AX = mybir.AxisListType.X

P = 128
D = 1024
S = 256
KT = D // P
NT = S // P
L1 = 2
HD = 64
RH = 4
FH1 = 2816
FH2 = 3584
NE = 8
MORE = (2 * S) // (P + 1)
JOBS = NE + MORE + 1
FB = 256
RAW = 6
HI = 3
BIG = 3.0e38
NEG = -1.0e30

U1 = dict(fq=0, fk=256, fv=512, gq=768, gk=1024, gv=1280, gr=1536, rq=1792, rk=2048, rv=2304, rg=2560, z=2816, xbc=3328)
W1RUNS = [[(0, 512)], [(512, 256), (772, 256)], [(1028, 512)]] + [[(1556 + 512 * i, 512)] for i in range(5)] \
    + [[(4124 + 512 * i, 512)] for i in range(8)]
W1SMALL = [(1540, 16), (768, 4), (4116, 8)]
U2 = dict(qa=0, ka=256, va=512, xb=768, bb=1024, cb=1280, pc=1536, qd=1792, kd=2048, vd=2304)
W2RUNS = [[(512 * i, 512)] for i in range(13)]

CST = {}


def constants():
    a = np.arange(P)
    j, t = a[:, None], a[None, :]
    parts = [
        ("triu", (j <= t) * 1.0),
        ("ones", np.ones((P, P))),
        ("after", (j > t) * 1.0),
        ("trimid", (j <= t) * 1.0 - (j <= 63) * 1.0),
        ("clamp", np.concatenate([(j <= t) * BIG, np.full((P, P), BIG), (j <= t) * BIG], 1)),
        ("negmask", (t > j) * NEG),
        ("rel", np.concatenate([np.where(t >= j, t - j, 1e30), P + t - j], 1)),
        ("flip", (j + t == P - 1) * 1.0),
        ("half", (j // 64 == np.arange(2)[None]) * 1.0),
        ("halfs", (j // 64 == np.arange(2)[None]) * 0.125),
        ("quarter", (j // 32 == np.arange(4)[None]) * 32 ** -0.5),
        ("experts", np.zeros((P, 1)) + np.arange(NE)[None]),
        ("countdown", np.zeros((P, 1)) + NE - np.arange(NE)[None]),
        ("slots", np.zeros((P, 1)) + np.arange(P)[None]),
        ("freq", np.zeros((P, 1)) + (np.float32(10000.0) ** (-np.arange(32, dtype=np.float32) / np.float32(32)))[None]),
    ]
    at = 0
    for name, m in parts:
        CST[name] = (at, m.shape[1])
        at += m.shape[1]
    return np.concatenate([m.astype(np.float32) for _, m in parts], 1)


def identity():
    return np.eye(P, dtype=np.float32)


def bias_buckets():
    d = 255 - np.arange(384)
    n = np.maximum(d, 0)
    nf = np.maximum(n, 16).astype(np.float32)
    large = 16 + (np.log(nf / np.float32(16)) / np.float32(math.log(8.0)) * np.float32(16)).astype(np.int32)
    bucket = np.where(n < 16, n, np.minimum(large, 31))
    return np.concatenate([(bucket[None] == np.arange(32)[:, None]) * 1.0, (d < 0)[None] * NEG], 0).astype(np.float32)


def pool_matrices():
    s, t = np.arange(S)[:, None], np.arange(S)[None]
    out = []
    for w in (2, 4, 8, 16):
        m = ((s <= t) & (s > t - w)) / np.minimum(t + 1, w) - (s == t)
        out.append(np.concatenate([m[:P, :], m[P:, P:]], 1))
    return np.stack(out, 1).astype(np.float32)


constants()


G1 = {
    0: [("narrow", [0])], 1: [("nt", [1]), ("zg", [2])],
    4: [("fqk", [0, 1])], 5: [("cum", [2, 3])],
    6: [("fs0", [0]), ("fs1", [1])], 7: [("fs2", [2]), ("fs3", [3])],
    8: [("ft0", [0]), ("ft1", [1])], 9: [("ft2", [2]), ("ft3", [3])],
    10: [("fy", [0])], 11: [("gt", [1, 2, 3])],
    13: [(f"gs{h}", [h]) for h in range(4)], 14: [("xt0", [2])], 15: [("gy", [0])],
    16: [("rt", [1, 3]), ("xt1", [2])], 18: [(f"rs{h}", [h]) for h in range(4)], 19: [("xt2", [1])], 20: [("ry", [0])],
    22: [("xs", [0, 1]), ("cb", [2, 3])],
    24: [(f"sg{h}", [h]) for h in range(4)], 26: [("sy0", [0])],
    27: [(f"sg{h + 4}", [h]) for h in range(4)], 29: [("sy1", [0])],
}
G2 = {
    2: [("aqk", [0, 1])], 3: [(f"as{h}", [h]) for h in range(4)], 5: [(f"at{h}", [h]) for h in range(4)],
    6: [("cx", [0, 1])], 7: [("ay", [2])], 8: [("pl", [0, 1])], 9: [("py", [2])],
    10: [("dqk", [0, 1])], 12: [(f"ds{i}", [i]) for i in range(4)], 14: [("dt0", [0]), ("dt1", [1])], 15: [("dy0", [2])],
    17: [(f"ds{i + 4}", [i]) for i in range(4)], 19: [("dt2", [0]), ("dt3", [1])], 20: [("dy1", [2])],
}


def program(nc, a, out, stop=99):
    ctx = ExitStack()
    with ctx:
        ctx.enter_context(nc.allow_non_contiguous_dma("small parameters"))

        room = nc.sbuf_bytes_remaining - 64
        room -= room % 64
        base = nc.sbuf_base
        ctx.enter_context(nc.sbuf_tensor("slab", [P, room // 4], F32))
        top = [base + (-base) % 64]

        def sb(name, shape, dtype=F32, at=None):
            size = int(np.prod(shape[1:])) * 4
            if at is None:
                at = top[0]
                top[0] += size + (-size) % 32
                assert top[0] <= base + room, (name, top[0] - base, room)
            return nc.alloc_sbuf_tensor_at(name, shape, dtype, offset=at)

        ring_at = top[0]
        raw = sb("raw", [P, RAW, 2048])
        lo = sb("w_lo", [P, RAW, 2048], F32R, at=ring_at)
        hi = sb("w_hi", [P, HI, 2048], F32R)
        xhi = sb("xhi", [P, 10, S], F32R)
        xlo = sb("xlo", [P, 10, S], F32R)
        x = sb("x", [P, NT, D])
        u_at = top[0]
        u = sb("u", [P, NT, 4096])
        g_at = top[0]
        gates = sb("gates", [P, NT, 4096])
        ghi = sb("ghi", [P, 2, NT, P], F32R, at=u_at)
        glo = sb("glo", [P, 2, NT, P], F32R, at=u_at + 2048)
        silu = sb("silu", [P, NT, FB], at=u_at + 4096)
        gprod = sb("gprod", [P, NT, FB], at=u_at + 6144)
        pick = sb("pick", [P, NT, P], at=u_at + 8192)
        pick_g = sb("pick_g", [P, NT, P], at=u_at + 9216)
        pick_t = sb("pick_t", [P, NT, P], at=u_at + 10240)
        y = sb("y", [P, D], at=u_at + 11264)
        hrow = sb("hrow", [P, NT, D], at=g_at)
        rope_t = sb("rope_t", [P, 3, NT, 8, 32], at=g_at + 8192)
        sq = sb("sq", [P, NT, 512], at=g_at + 16384)
        fgain = sb("fgain", [P, D], at=g_at + 16384)
        NC = max(v[0] + v[1] for v in CST.values())
        cst = sb("cst", [P, NC])

        def C(name, lo_=0, n=None):
            at, w = CST[name]
            return cst[:, at + lo_:at + (w if n is None else lo_ + n)]

        ident_t = sb("ident_t", [P, P])
        cols1 = sb("cols1", [P, L1, 60])
        cols2 = sb("cols2", [P, L1, 25])
        heads8 = sb("heads8", [P, L1, 16])
        lam_in = sb("lam_in", [P, L1, 4, 32])
        lam = sb("lam", [P, L1, 6])
        small = sb("small", [P, 64])
        epst = sb("epst", [P, 2])
        conv2 = sb("conv2", [P, L1, 6])
        nstat = sb("nstat", [P, 8])
        type1_at = top[0]
        brow = sb("brow", [P, L1, 12])
        nar_at = top[0]
        wsm = sb("wsm", [P, L1, KT, 28])
        wsm_lo = sb("wsm_lo", [P, L1, KT, 28], F32R, at=nar_at)
        gw2 = sb("gw2", [16, L1, 256])
        rot = sb("rot", [P, 2, NT, 32])
        narT = sb("narT", [28, S])
        z = sb("z", [P, NT, 268])
        dtv = sb("dtv", [P, NT, 8])
        E_at = top[0]
        E = sb("E", [P, 6, 256])
        zlog = sb("zlog", [P, NT, 268], at=E_at)
        tg = sb("tg", [P, NT, 256], at=g_at + 28672)
        ysq = sb("ysq", [P, NT, 256], at=g_at + 30720)
        ctanh = sb("ctanh", [P, 2, S], at=g_at + 14336)
        tgz = sb("tgz", [P, NT, 512], at=E_at)
        Bld = sb("Bld", [P, 4, 384])
        Pm = sb("Pm", [P, 4, 384])
        kT = sb("kT", [P, 2, S])
        qM = sb("qM", [P, 2, 2, S])
        kE_at = top[0]
        kE = sb("kE", [P, 2, P])
        qD = sb("qD", [P, 2, 2, P])
        cbm = sb("cbm", [P, 2, 384], at=kE_at)
        type1_end = top[0]
        top[0] = type1_at
        router = sb("router", [P, KT, NE])
        router_hi = sb("router_hi", [P, KT, NE], F32R)
        router_lo = sb("router_lo", [P, KT, NE], F32R)
        wgrp = sb("wgrp", [64, L1, 4, 64])
        biasT = sb("biasT", [P, 8, S])
        poolw = sb("poolw", [P, 4, 384])
        p2_at = top[0]
        P2m = sb("P2m", [P, 4, 384])
        kT2 = sb("kT2", [P, 2, S])
        qM2 = sb("qM2", [P, 4, 2, S])
        mgain = sb("mgain", [P, D], at=p2_at)
        type2_end = top[0]
        top[0] = max(type1_end, type2_end)
        ybT = sb("ybT", [P, 2, S], at=u_at + 4 * 2560)
        plT = sb("plT", [64, 4, S], at=u_at + 4 * 2560 + 2048)
        onehot = sb("onehot", [33, 384], at=g_at + 20480)
        tabT = sb("tabT", [8, 384], at=g_at + 22016)
        tab = sb("tab", [33, 8], at=g_at + 23552)
        ang = sb("ang", [P, 4, NT, 32], at=g_at + 24576)
        posi = sb("posi", [P, NT], I32, at=g_at + 25600)
        posf = sb("posf", [P, NT], at=g_at + 25600 + 64)
        wsm_hi = sb("wsm_hi", [P, KT, 28], F32R, at=g_at + 26624)
        glab = sb("glab", [P, 256], at=g_at + 27648)
        gate8 = sb("gate8", [P, NT, 8], at=u_at + 15360)
        m8 = sb("m8", [P, NT, 8], at=u_at + 15424)
        i8 = sb("i8", [P, NT, 8], U32, at=u_at + 15488)
        i8f = sb("i8f", [P, NT, 2], at=u_at + 15552)
        lgT = sb("lgT", [NE, S], at=u_at + 20480)
        lg8 = sb("lg8", [P, NT, 8], at=u_at + 15616)
        top2 = sb("top2", [P, NT, 4], at=u_at + 15680)
        chosen = sb("chosen", [P, NT, 8], at=u_at + 15744)
        rank = sb("rank", [P, 3, 8], at=u_at + 15808)
        over = sb("over", [P, 4, 8], at=u_at + 15936)
        prod8 = sb("prod8", [P, 2 * NT, 8], at=u_at + 24576)
        jobtab = sb("jobtab", [P, 2 * NT, JOBS], at=u_at + 24576 + 128)
        jobpos, jobgate = jobtab[:, 0:NT], jobtab[:, NT:2 * NT]
        moe_sq = sb("moe_sq", [P, NT, D], at=g_at + 20480)
        jobs_f = sb("jobs_f", [P, 4], at=u_at + 16384)
        jobs_i = sb("jobs_i", [P, 4], I32, at=u_at + 16448)
        if top[0] > base + room:
            raise ValueError("SBUF")

        bank = [ctx.enter_context(nc.psum_tensor(f"bank{i}", [P, 512], F32)) for i in range(8)]
        X = [4, 5, 6, 7]
        scratch = nc.dram_tensor("bias_rows", (8, 384), F32, kind="Internal").ap()

        def sem(name):
            return ctx.enter_context(nc.semaphore(name))

        full = [sem(f"bank_full{i}") for i in range(8)]
        free = [sem(f"bank_free{i}") for i in range(8)]
        raw_full = [sem(f"raw_full{i}") for i in range(RAW)]
        hi_ready = sem("hi_ready")
        lo_ready = sem("lo_ready")
        w_used = sem("w_used")
        half_done = sem("half_done")
        x_loaded, cst_loaded, par_loaded = sem("x_loaded"), sem("cst_loaded"), sem("par_loaded")
        par_sp_loaded = sem("par_sp_loaded")
        narrow_rounded, narrow_split, glab_loaded = sem("narrow_rounded"), sem("narrow_split"), sem("glab_loaded")
        ident_loaded, bias_loaded = sem("ident_loaded"), sem("bias_loaded")
        par2_loaded, rows_out, bias_in, fgain_in, stored = (sem(n) for n in
            ("par2_loaded", "bias_rows_out", "bias_in", "final_gain_in", "stored"))
        gain1_loaded, narrow_loaded, tiles_set = sem("gain1_loaded"), sem("narrow_loaded"), sem("constant_tiles_set")
        setup_v, setup_s = sem("setup_vector"), sem("setup_scalar")
        norm_rstd, norm_h, norm_hi = sem("norm_rstd"), sem("norm_rows"), sem("norm_hi")
        silu_done, ghi_done = sem("silu_done"), sem("gated_hi")
        route_m, route_e = sem("route_max"), sem("route_exp")
        chosen_ready, routed = sem("chosen_ready"), sem("routed")
        router_rounded, router_split = sem("router_rounded"), sem("router_split")
        rows_gained = sem("rows_gained")
        pick_ready = sem("pick_ready")
        gather_hi = sem("gather_hi")
        moe_gain_in = sem("moe_gain_in")
        dve_link, act_link, pool_link = sem("vector_link"), sem("scalar_link"), sem("pool_link")
        STEPS = dict(z_abs=1, z_log=1, decay=1, fox_ss=1, fox_rstd=1, fox_qn=1, builds=12, fox_max=4,
                     gla_prod=1, gla_p=4, gate_tanh=2, br_ss=3, br_rstd=3, y_gla=1, y_ret=1, rope=1, ret_decay=4,
                     conv_out=3, conv_tanh=3, xbc=3, ssd_c=1, ssd_x=1, ssd_p=8, ssd_dx=2, z_tanh=1, y_ssd=1,
                     y_hi=5, merged=8, whole=4, m_hi=4,
                     moba_max=4, conv_in=1, dif_max=8, dif_p=4, d_ss=1, d_rstd=1, y_dif=1, y_conv=1,
                     y_hi_b=4, merged_b=8, whole_b=4, m_hi_b=4)
        T = {name: sem(name) for name in STEPS}

        def at(name, l, n=1):
            return l * STEPS[name] + n

        uses, fulls = [0] * 8, [0] * 8
        USE, FULL, CH, FFB, HALF = {}, {}, {}, {}, {}

        def claim(key, *banks, streamed=False):
            for b in banks:
                uses[b] += 1
                USE[key, b] = uses[b]
                if not streamed:
                    fulls[b] += 1
                    FULL[key, b] = fulls[b]

        phases = []
        for l in range(L1):
            phases += [("norm", l, "mix1"), ("mix1", l), ("norm", l, "ffn1"), ("ffn1", l)]
        for l in range(L1):
            f = "ffn2" if l == 0 else "moe"
            phases += [("norm", l, "mix2"), ("mix2", l), ("norm", l, f), (f, l)]
        phases = phases[:2 * stop]
        c = ffb = 0
        XREADY = []
        last_x = None
        for k in phases:
            XREADY.append(last_x)
            if k[0] == "norm":
                for i in range(4):
                    claim(k, X[i])
                continue
            CH[k] = c
            if k[0] in ("mix1", "mix2"):
                nb, groups, ny = (16, G1, 5) if k[0] == "mix1" else (13, G2, 4)
                for pos in range(2 * nb):
                    if pos % 2 == 0:
                        claim((k, "gemm", pos // 2), *(2 * (pos // 2 % 2) + t for t in range(NT)), streamed=True)
                    if k == ("mix1", 0) and pos == 1:
                        claim("bias_rows", X[3])
                    for g, bs in groups.get(pos, []):
                        claim((k, g), *(X[b] for b in bs))
                for i in range(ny):
                    claim((k, "yT", i), X[i % 4])
                for br in range(4):
                    claim((k, "up", br), *((0, 1, 2, 3) if br % 2 == 0 else X), streamed=True)
                for i in range(4):
                    claim((k, "mT", i), X[i])
                claim((k, "out"), 0, 1, 2, 3, streamed=True)
                HALF[k, "up"], HALF[k, "out"] = len(HALF) + 1, len(HALF) + 2
                c += 2 * nb + ny + 4
                last_x = [(b, USE[(k, "out"), b] + 1) for b in range(4)]
            else:
                J = FFJ[k[0]]
                FFB[k] = ffb
                if k[0] == "moe":
                    claim((k, "logits"), X[0])
                    claim((k, "router"), X[0])
                    claim((k, "rank"), X[1])
                    claim((k, "gather"), 2, 3)
                    u0, f0 = list(uses), list(fulls)
                    for j in range(J):
                        claim((k, "U", j), j % 2, streamed=True)
                        if j == 0:
                            claim((k, "scatter"), X[2], X[3], 2, 3)
                            claim((k, "turned"), X[2])
                        if j == J - 1:
                            claim((k, "next"), 2, 3)
                        claim((k, "T", j), j % 2)
                    claim((k, "D"), X[0], X[1], streamed=True)
                    JU, JF = [m - n for m, n in zip(uses, u0)], [m - n for m, n in zip(fulls, f0)]
                    c += 2
                else:
                    for j in range(J):
                        for t in range(NT):
                            claim((k, "U", j), 2 * (j % 2) + t, streamed=True)
                            claim((k, "T", j), 2 * (j % 2) + t)
                    claim((k, "D"), *X, streamed=True)
                    HALF[k, "D"] = len(HALF) + 1
                    c += 3 * J
                    ffb += 2 * J
                    last_x = [(b, USE[(k, "D"), b] + 1) for b in X]
        END = c

        def use(key, b):
            return USE[key, b]

        def ev(key, b):
            return USE[key, b] + 1

        def fl(key, b):
            return FULL[key, b]

        def gbank(n, t):
            return 2 * (n % 2) + t

        def walk(eng, J, u0, tr, u1, dn, middle=None, late=lambda: None):
            u0(0, 0, 0)
            u1(0, 0, 1)
            u0(1, 0, 2)
            tr(0, 0)
            u1(1, 0, 3)
            dn(0, 0, 4)
            n = (J - 3) // 2

            def blocks(first, end):
                with eng.Fori(first, end) as it:
                    for j in (1, 2):
                        u0(j + 1, it, 2 + 3 * j)
                        tr(j, it)
                        u1(j + 1, it, 3 + 3 * j)
                        dn(j, it, 4 + 3 * j)

            if middle is None:
                blocks(0, n)
            else:
                blocks(0, n // 2)
                middle()
                blocks(n // 2, n)
            for j in range(1 + 2 * n, J - 1):
                u0(j + 1, 0, 2 + 3 * j)
                tr(j, 0)
                u1(j + 1, 0, 3 + 3 * j)
                dn(j, 0, 4 + 3 * j)
            late()
            tr(J - 1, 0)
            dn(J - 1, 0, 3 * J - 1)

        def each_job(eng, job):
            with eng.Fori(0, NE) as e:
                job(e)
            nj = eng.value_load(jobs_i[0:1, MORE:MORE + 1], min_val=NE, max_val=NE + MORE)
            with eng.If(nj > NE):
                with eng.Fori(NE, nj) as e:
                    job(e)
            return nj

        block = ctx.enter_context(nc.Block())

        @block.sync
        def _(sp):
            def slot(c, it=0, eo=0, per=0):
                if c >= RAW:
                    sp.wait_ge(w_used, c - RAW + 1 + 6 * it + per * eo)
                return c % RAW

            def columns(c, w, k0, runs):
                s = slot(c)
                dst = raw[:, s, :].rearrange("p (k n) -> p k n", k=4)
                src = w.rearrange("(k p) n -> p k n", p=P)[:, k0:k0 + 4]
                if len(runs) == 1:
                    (f, n), = runs
                    sp.dma_start(dst[:, 0:2], src[:, 0:2, f:f + n]).then_inc(raw_full[s], 16)
                    sp.dma_start(dst[:, 2:4], src[:, 2:4, f:f + n]).then_inc(raw_full[s], 16)
                else:
                    for i, (f, n) in enumerate(runs):
                        sp.dma_start(dst[:, :, 256 * i:256 * i + n], src[:, :, f:f + n]).then_inc(raw_full[s], 16)

            def rows(c, w, k0):
                s = slot(c)
                for i in range(2):
                    sp.dma_start(raw[:, s, 1024 * i:1024 * i + 1024],
                                 w[(k0 + i) * P:(k0 + i + 1) * P, :]).then_inc(raw_full[s], 16)

            def feed_forward(c0, J, wa, wb, wd, eo=0, per=0):
                va, vb = (w.rearrange("(k p) n -> p k n", p=P) for w in (wa, wb))

                def up(j, it, c, k0):
                    s = slot(c0 + c, it, eo, per)
                    dst = raw[:, s, :].rearrange("p (k n) -> p k n", k=4)
                    f = j * FB + it * (2 * FB)
                    sp.dma_start(dst[:, :, 0:FB], va[:, k0:k0 + 4, bass.ds(f, FB)]).then_inc(raw_full[s], 16)
                    sp.dma_start(dst[:, :, FB:2 * FB], vb[:, k0:k0 + 4, bass.ds(f, FB)]).then_inc(raw_full[s], 16)

                def down(j, it, c):
                    s = slot(c0 + c, it, eo, per)
                    for i in range(2):
                        f = j * FB + i * P + it * (2 * FB)
                        sp.dma_start(raw[:, s, 1024 * i:1024 * i + 1024], wd[bass.ds(f, P), :]).then_inc(raw_full[s], 16)

                walk(sp, J, lambda j, it, c: up(j, it, c, 0), lambda j, it: None,
                     lambda j, it, c: up(j, it, c, 4), down)

            def load(dst, src):
                sp.dma_start(dst, src).then_inc(par_sp_loaded, 16)

            def by_tile(name, dst, taps=False):
                for l in range(L1):
                    load(dst[:, l], a[name][l].rearrange("w (k p) -> p (w k)" if taps else "(k p) -> p k", p=P))

            def parameters():
                for name, cc in (("gla_norm", 18), ("ret_norm", 20)):
                    for h in range(2):
                        load(cols1[64 * h:64 * h + 64, :, cc], a[name].rearrange("l p -> p l"))
                by_tile("ln2", cols1[:, :, 8:16])
                by_tile("ssd_norm", cols1[:, :, 22:26])
                by_tile("ssd_conv_w", cols1[:, :, 28:52], True)
                by_tile("ssd_conv_b", cols1[:, :, 52:58])
                by_tile("mix_norm_g_2", cols2[:, :, 0:8])
                by_tile("ffn_norm_g_2", cols2[:, :, 8:16])
                by_tile("conv_w_2", conv2[:, :, :], True)
                by_tile("pool_scale_2", cols2[:, :, 21:23])
                for h in range(2):
                    load(cols2[64 * h:64 * h + 64, :, 23], a["diff_subln_g_2"].rearrange("l p -> p l"))
                load(lam_in[:, :, :, :], a["diff_lambda_2"].partition_broadcast(P))

            for t in range(NT):
                sp.dma_start(x[:, t, :], a["x"][0, t * P:t * P + P, :]).then_inc(x_loaded, 16)
            for k in phases:
                if k[0] == "norm":
                    continue
                c0, l = CH[k], k[1]
                if k[0] in ("mix1", "mix2"):
                    w, runs, ups, wo = ((a["w_in"][l], W1RUNS, [a["w_up_a"][l], a["w_up_b"][l], a["w_up_c"][l], a["w_up_d"][l]],
                                         a["w_out"][l]) if k[0] == "mix1" else
                                        (a["w_in_2"][l], W2RUNS, [a["branch_proj_2"][l, i] for i in range(4)], a["w_out_2"][l]))
                    for n, run in enumerate(runs):
                        if c0 == RAW:
                            parameters()
                        columns(c0, w, 0, run)
                        columns(c0 + 1, w, 4, run)
                        c0 += 2
                    for wu in ups:
                        for k0 in range(0, wu.shape[0] // P, 2):
                            rows(c0, wu, k0)
                            c0 += 1
                    for k0 in range(0, KT, 2):
                        rows(c0, wo, k0)
                        c0 += 1
                elif k[0] == "ffn1":
                    feed_forward(c0, FFJ[k[0]], a["w_ffn_in"][l][:, 0:FH1], a["w_ffn_in"][l][:, FH1:2 * FH1], a["w_ffn_out"][l])
                elif k[0] == "ffn2":
                    feed_forward(c0, FFJ[k[0]], a["dense_w1_2"][0], a["dense_w3_2"][0], a["dense_w2_2"][0])
                else:
                    J = FFJ[k[0]]
                    wts = [a["moe_w1_2"][0], a["moe_w3_2"][0], a["moe_w2_2"][0]]

                    def job(e, expert):
                        feed_forward(c0, J, *(w[bass.ds(expert, 1)].rearrange("a k n -> (a k) n") for w in wts), e, 3 * J)

                    with sp.Fori(0, NE) as e:
                        job(e, e)
                    sp.wait_ge(routed, 1)
                    nj = sp.value_load(jobs_i[0:1, MORE:MORE + 1], min_val=NE, max_val=NE + MORE)
                    with sp.If(nj > NE):
                        with sp.Fori(NE, nj) as e:
                            job(e, sp.value_load(jobs_i[0:1, bass.ds(e - NE, 1)], min_val=0, max_val=NE - 1))
                    for i in range(2):
                        s = slot(c0 + i, 0, nj, 3 * J)
                        for h in range(2):
                            sp.dma_start(raw[:, s, 1024 * h:1024 * h + 1024], wts[2][0, 0:P, :]).then_inc(raw_full[s], 16)
            for t in range(NT):
                sp.wait_ge(norm_h, NT * len([k for k in phases if k[0] == "moe"]) + t + 1)
                sp.dma_start(out[t * P:t * P + P, :], hrow[:, t, :]).then_inc(stored, 16)
            sp.wait_ge(stored, 16 * NT)

        @block.tensor
        def _(pe):
            mm = nc.tensor.matmul
            ident = ident_t[:, :]

            def tr(dst, src):
                return nc.tensor.transpose(dst, src, ident)

            def gemm_half(banks, c, k0, start, stop, it=0):
                s, h = c % RAW, c % HI
                pe.wait_ge(lo_ready, c + 1 + 6 * it)
                for k in range(4):
                    for t in range(NT):
                        tok = slice(t * P, t * P + P)
                        wh, wl = (w[:, i, k * 512:k * 512 + 512] for w, i in ((hi, h), (lo, s)))
                        mm(bank[banks[t]][:, :], xhi[:, k0 + k, tok], wh, start=start and k == 0, stop=False)
                        mm(bank[banks[t]][:, :], xlo[:, k0 + k, tok], wh, start=False, stop=False)
                        last = mm(bank[banks[t]][:, :], xhi[:, k0 + k, tok], wl, start=False, stop=stop and k == 3)
                last.then_inc(w_used, 1)

            def gemm_rows(banks, c, lhs, first, final, it=0, by_half=False):
                s, h = c % RAW, c % HI
                pe.wait_ge(lo_ready, c + 1 + 6 * it)

                def part(k, t, n):
                    xh, xl = lhs(k, t)
                    b = bank[banks[2 * t + n]][:, :]
                    o = k * 1024 + n * 512
                    mm(b, xh, hi[:, h, o:o + 512], start=first and k == 0, stop=False)
                    mm(b, xl, hi[:, h, o:o + 512], start=False, stop=False)
                    return mm(b, xh, lo[:, s, o:o + 512], start=False, stop=final and k == 1)

                if by_half:
                    for n in range(2):
                        for k in range(2):
                            for t in range(NT):
                                last = part(k, t, n)
                        last.then_inc(half_done if n == 0 else w_used, 1)
                else:
                    for k in range(2):
                        for t in range(NT):
                            for n in range(2):
                                last = part(k, t, n)
                    last.then_inc(w_used, 1)

            def xt(kt):
                return lambda k, t: (xhi[:, kt + k, t * P:t * P + P], xlo[:, kt + k, t * P:t * P + P])

            def transposes_to(key, b, srcs):
                pe.wait_ge(free[b], use(key, b))
                for i, src in enumerate(srcs):
                    last = tr(bank[b][:, i * P:(i + 1) * P], src)
                last.then_inc(full[b], 1)

            def norm(k, ready):
                for i in range(4):
                    if ready is None:
                        pe.wait_ge(x_loaded, 16 * NT)
                    else:
                        for t in range(NT):
                            pe.wait_ge(free[ready[2 * t + i // 2][0]], ready[2 * t + i // 2][1])
                    transposes_to(k, X[i], [x[:, t, (2 * i + kk) * P:(2 * i + kk + 1) * P] for kk in range(2) for t in range(NT)])

            def values(key, b, heads, pblk, v0):
                for h in range(heads):
                    v = [u[:, t, v0 + h * HD:v0 + h * HD + HD] for t in range(NT)]
                    mm(bank[b][:, h * HD:h * HD + HD], pblk(h)[:, 0:P], v[0], start=True, stop=True)
                    mm(bank[b][:, 256 + h * HD:256 + h * HD + HD], pblk(h)[:, P:2 * P], v[0], start=True, stop=False)
                    last = mm(bank[b][:, 256 + h * HD:256 + h * HD + HD], pblk(h)[:, 2 * P:3 * P], v[1], start=False, stop=True)
                last.then_inc(full[b], 1)

            def gemm_waits(k, n):
                for t in range(NT):
                    pe.wait_ge(free[gbank(n, t)], ev((k, "gemm", n), gbank(n, t)))

            def conv_columns(k, i):
                gemm_waits(k, 6 if i == 0 else 7)
                transposes_to((k, f"xt{i}"), X[2 if i < 2 else 1],
                              [u[:, t, U1["xbc"] + (2 * i + j) * P:U1["xbc"] + (2 * i + j + 1) * P] for j in range(2) for t in range(NT)])

            def attend1(k, pos):
                l = k[1]
                if pos == 0:
                    b, key = X[0], (k, "narrow")
                    pe.wait_ge(free[b], use(key, b))
                    pe.wait_ge(narrow_split, l + 1)
                    o = bank[b][0:28, 0:S]
                    for kt in range(KT):
                        mm(o, wsm_hi[:, kt, :], xhi[:, kt, :], start=kt == 0, stop=False)
                        mm(o, wsm_hi[:, kt, :], xlo[:, kt, :], start=False, stop=False)
                        last = mm(o, wsm_lo[:, l, kt, :], xhi[:, kt, :], start=False, stop=kt == KT - 1)
                    last.then_inc(full[b], 1)
                elif pos == 1:
                    pe.wait_ge(free[X[0]], ev((k, "narrow"), X[0]))
                    b = X[1]
                    pe.wait_ge(free[b], use((k, "nt"), b))
                    for t in range(NT):
                        last = nc.tensor.transpose(bank[b][:, t * 28:t * 28 + 28], narT[0:28, t * P:t * P + P], ident_t[0:28, 0:28])
                    last.then_inc(full[b], 1)
                    b = X[2]
                    pe.wait_ge(free[b], use((k, "zg"), b))
                    for t in range(NT):
                        last = mm(bank[b][:, t * 256:t * 256 + 256], narT[0:16, t * P:t * P + P], gw2[0:16, l, :], start=True, stop=True)
                    last.then_inc(full[b], 1)
                elif pos == 4:
                    pe.wait_ge(T["fox_qn"], at("fox_qn", l))
                    for i, o in ((0, U1["fq"]), (1, U1["fk"])):
                        transposes_to((k, "fqk"), X[i], [u[:, t, o + p * P:o + p * P + P] for p in range(2) for t in range(NT)])
                elif pos == 5:
                    pe.wait_ge(T["decay"], at("decay", l))
                    for i, mats in ((0, ("after", "trimid")), (1, ("trimid", "triu"))):
                        b = X[2 + i]
                        pe.wait_ge(free[b], use((k, "cum"), b))
                        for j, m in enumerate(mats):
                            last = mm(bank[b][:, j * 256:j * 256 + 256], C(m), z[:, i, 0:256], start=True, stop=True)
                        last.then_inc(full[b], 1)
                elif pos in (6, 7):
                    for h in (0, 1) if pos == 6 else (2, 3):
                        key, b, o = (k, f"fs{h}"), X[h], bank[X[h]]
                        pe.wait_ge(free[b], use(key, b))
                        for i in range(2):
                            pe.wait_ge(free[X[i]], ev((k, "fqk"), X[i]))
                        pe.wait_ge(T["builds"], at("builds", l, h + 1))
                        q, kk = qM[:, h % 2, h // 2, :], kT[:, h // 2, :]
                        mm(o[:, 0:P], q[:, 0:P], kk[:, 0:P], start=True, stop=False)
                        mm(o[:, 0:P], C("triu"), Bld[:, h, 0:P], start=False, stop=False)
                        mm(o[:, 0:P], ident, C("negmask"), start=False, stop=True)
                        mm(o[:, P:3 * P], q[:, P:2 * P], kk, start=True, stop=False)
                        mm(o[:, P:3 * P], C("triu"), Bld[:, h, P:3 * P], start=False, stop=False)
                        mm(o[:, P:2 * P], C("ones"), Bld[:, h, 0:P], start=False, stop=False)
                        mm(o[:, 2 * P:3 * P], ident, C("negmask"), start=False, stop=True).then_inc(full[b], 1)
                elif pos in (8, 9):
                    for h in (0, 1) if pos == 8 else (2, 3):
                        pe.wait_ge(free[X[h]], ev((k, f"fs{h}"), X[h]))
                        transposes_to((k, f"ft{h}"), X[h], [Pm[:, h, i * P:i * P + P] for i in range(3)])
                elif pos == 10:
                    for h in range(4):
                        pe.wait_ge(free[X[h]], ev((k, f"ft{h}"), X[h]))
                    values((k, "fy"), X[0], 4, lambda h: Pm[:, h, :], U1["fv"])
                elif pos == 11:
                    pe.wait_ge(T["gla_prod"], at("gla_prod", l))
                    for i, es in ((1, ((2, 0), (4, 0), (2, 1), (4, 1))), (2, ((0, 0), (0, 1), (5, 0), (5, 1))),
                                  (3, ((1, 0), (3, 0), (1, 1), (3, 1)))):
                        transposes_to((k, "gt"), X[i], [E[:, e, p * P:p * P + P] for e, p in es])
                elif pos == 13:
                    for i in (1, 2, 3):
                        pe.wait_ge(free[X[i]], ev((k, "gt"), X[i]))
                    for h in range(4):
                        key, b, o, p, m = (k, f"gs{h}"), X[h], bank[X[h]], h // 2, h % 2
                        pe.wait_ge(free[b], use(key, b))
                        mm(o[:, 0:P], kT[:, p, 0:P], qM[:, m, p, 0:P], start=True, stop=True)
                        mm(o[:, P:2 * P], kE[:, p, :], qD[:, m, p, :], start=True, stop=True)
                        mm(o[:, 2 * P:3 * P], kT[:, p, P:2 * P], qM[:, m, p, P:2 * P], start=True, stop=True).then_inc(full[b], 1)
                elif pos == 14:
                    conv_columns(k, 0)
                elif pos == 15:
                    pe.wait_ge(free[X[0]], use((k, "gy"), X[0]))
                    pe.wait_ge(T["gla_p"], at("gla_p", l, 4))
                    values((k, "gy"), X[0], 4, lambda h: Pm[:, h, :], U1["gv"])
                elif pos == 16:
                    pe.wait_ge(T["rope"], at("rope", l))
                    for i, o in ((1, U1["rk"]), (3, U1["rq"])):
                        transposes_to((k, "rt"), X[i], [u[:, t, o + p * P:o + p * P + P] for p in range(2) for t in range(NT)])
                    conv_columns(k, 1)
                elif pos == 19:
                    conv_columns(k, 2)
                elif pos == 18:
                    for i in (1, 3):
                        pe.wait_ge(free[X[i]], ev((k, "rt"), X[i]))
                    for h in range(4):
                        key, b, o, p, m = (k, f"rs{h}"), X[h], bank[X[h]], h // 2, h % 2
                        pe.wait_ge(free[b], use(key, b))
                        mm(o[:, 0:2 * P], kT[:, p, 0:P], qM[:, m, p, :], start=True, stop=True)
                        mm(o[:, 2 * P:3 * P], kT[:, p, P:2 * P], qM[:, m, p, P:2 * P], start=True, stop=True).then_inc(full[b], 1)
                elif pos == 20:
                    for h in range(4):
                        pe.wait_ge(free[X[h]], ev((k, f"rs{h}"), X[h]))
                    values((k, "ry"), X[0], 4, lambda h: Pm[:, h, :], U1["rv"])
                elif pos == 22:
                    pe.wait_ge(T["xbc"], at("xbc", l, 3))
                    for t in range(NT):
                        transposes_to((k, "xs"), X[t], [E[:, i, t * P:t * P + P] for i in range(4)])
                    pe.wait_ge(T["ssd_c"], at("ssd_c", l))
                    for g in range(2):
                        b, o = X[2 + g], bank[X[2 + g]]
                        pe.wait_ge(free[b], use((k, "cb"), b))
                        mm(o[:, 0:2 * P], E[:, 4, 0:P], kT[:, g, :], start=True, stop=True)
                        mm(o[:, 2 * P:3 * P], E[:, 4, P:2 * P], kT[:, g, P:2 * P], start=True, stop=True).then_inc(full[b], 1)
                elif pos in (24, 27):
                    for h in range(4) if pos == 24 else range(4, 8):
                        key, b = (k, f"sg{h}"), X[h % 4]
                        o, i = bank[b], h % 4
                        pe.wait_ge(free[b], use(key, b))
                        pe.wait_ge(T["builds"], at("builds", l, 5 + h))
                        mm(o[:, 0:2 * P], Bld[:, i, 0:P], C("triu", 0, 2 * P), start=True, stop=False)
                        mm(o[:, P:2 * P], Bld[:, i, P:2 * P], C("triu"), start=False, stop=True)
                        mm(o[:, 2 * P:3 * P], Bld[:, i, 2 * P:3 * P], C("triu"), start=True, stop=True).then_inc(full[b], 1)
                elif pos in (26, 29):
                    r = 0 if pos == 26 else 1
                    pe.wait_ge(free[X[0]], use((k, f"sy{r}"), X[0]))
                    pe.wait_ge(T["ssd_x"], at("ssd_x", l))
                    pe.wait_ge(T["ssd_p"], at("ssd_p", l, 4 * r + 4))
                    values((k, f"sy{r}"), X[0], 4, lambda h: Pm[:, h, :], 256 + 256 * r)

            def softmax_scores(k, key, b, q, kk, head):
                o = bank[b]
                pe.wait_ge(free[b], use(key, b))
                mm(o[:, 0:P], q[:, 0:P], kk[:, 0:P], start=True, stop=False)
                mm(o[:, 0:P], C("flip"), biasT[:, head, P:2 * P], start=False, stop=True)
                mm(o[:, P:3 * P], q[:, P:2 * P], kk, start=True, stop=False)
                mm(o[:, P:3 * P], C("flip"), biasT[:, head, :], start=False, stop=True).then_inc(full[b], 1)

            def attend2(k, pos):
                l = k[1]
                if pos == 2:
                    gemm_waits(k, 0)
                    for i, o in ((0, U2["qa"]), (1, U2["ka"])):
                        transposes_to((k, "aqk"), X[i], [u[:, t, o + p * P:o + p * P + P] for p in range(2) for t in range(NT)])
                elif pos == 3:
                    for i in range(2):
                        pe.wait_ge(free[X[i]], ev((k, "aqk"), X[i]))
                    if l == 0:
                        pe.wait_ge(bias_in, 16)
                    for h in range(4):
                        softmax_scores(k, (k, f"as{h}"), X[h], qM2[:, h % 2, h // 2, :], kT2[:, h // 2, :], h)
                elif pos == 5:
                    for h in range(4):
                        pe.wait_ge(free[X[h]], ev((k, f"as{h}"), X[h]))
                        transposes_to((k, f"at{h}"), X[h], [P2m[:, h, i * P:i * P + P] for i in range(3)])
                elif pos == 6:
                    pe.wait_ge(T["conv_in"], at("conv_in", l))
                    for i, o in ((0, U2["cb"]), (1, U2["bb"])):
                        transposes_to((k, "cx"), X[i], [u[:, t, o + p * P:o + p * P + P] for p in range(2) for t in range(NT)])
                elif pos == 7:
                    pe.wait_ge(free[X[2]], use((k, "ay"), X[2]))
                    for h in range(4):
                        pe.wait_ge(free[X[h]], ev((k, f"at{h}"), X[h]))
                    values((k, "ay"), X[2], 4, lambda h: P2m[:, h, :], U2["va"])
                elif pos == 8:
                    gemm_waits(k, 3)
                    if l == 0:
                        pe.wait_ge(par2_loaded, 16 * NPAR2)
                    for b_ in range(2):
                        b = X[b_]
                        pe.wait_ge(free[b], use((k, "pl"), b))
                        for gg in range(2):
                            g = 2 * b_ + gg
                            o = bank[b][0:64, gg * 256:gg * 256 + 256]
                            us_ = [u[:, t, U2["pc"] + g * 64:U2["pc"] + g * 64 + 64] for t in range(NT)]
                            mm(o, us_[0], poolw[:, g, 0:256], start=True, stop=False)
                            last = mm(o[:, P:2 * P], us_[1], poolw[:, g, 256:384], start=False, stop=True)
                        last.then_inc(full[b], 1)
                elif pos == 9:
                    b, key = X[2], (k, "py")
                    for i in range(2):
                        pe.wait_ge(free[X[i]], ev((k, "pl"), X[i]))
                    pe.wait_ge(free[b], use(key, b))
                    for t in range(NT):
                        for g in range(4):
                            last = mm(bank[b][:, t * 256 + g * 64:t * 256 + g * 64 + 64], plT[:, g, t * P:t * P + P],
                                      wgrp[:, l, g, :], start=True, stop=True)
                    last.then_inc(full[b], 1)
                elif pos == 10:
                    gemm_waits(k, 4)
                    for i, o in ((0, U2["qd"]), (1, U2["kd"])):
                        transposes_to((k, "dqk"), X[i], [u[:, t, o + p * P:o + p * P + P] for p in range(2) for t in range(NT)])
                elif pos in (12, 17):
                    r = 0 if pos == 12 else 1
                    for i in range(2):
                        pe.wait_ge(free[X[i]], ev((k, "dqk"), X[i]))
                    for i in range(4):
                        softmax_scores(k, (k, f"ds{4 * r + i}"), X[i], qM2[:, i, r, :], kT2[:, r, :], 4 + 2 * r + i // 2)
                elif pos in (14, 19):
                    r = 0 if pos == 14 else 1
                    for i in range(2):
                        pe.wait_ge(T["dif_p"], at("dif_p", l, 2 * r + i + 1))
                        transposes_to((k, f"dt{2 * r + i}"), X[i], [P2m[:, 2 * i, j * P:j * P + P] for j in range(3)])
                elif pos in (15, 20):
                    r = 0 if pos == 15 else 1
                    b = X[2]
                    pe.wait_ge(free[b], use((k, f"dy{r}"), b))
                    for i in range(2):
                        pe.wait_ge(free[X[i]], ev((k, f"dt{2 * r + i}"), X[i]))
                    values((k, f"dy{r}"), b, 2, lambda h: P2m[:, 2 * h, :], U2["vd"] + 128 * r)

            def mixer(k):
                c0, l = CH[k], k[1]
                first = k[0] == "mix1"
                nb, attend, ny = (16, attend1, 5) if first else (13, attend2, 4)
                for i in range(2):
                    pe.wait_ge(free[X[i]], ev(("norm", l, k[0]), X[i]))
                for pos in range(2 * nb):
                    n, half = divmod(pos, 2)
                    banks = [gbank(n, t) for t in range(NT)]
                    if half == 0:
                        for b in banks:
                            pe.wait_ge(free[b], use((k, "gemm", n), b))
                    gemm_half(banks, c0 + pos, 4 * half, half == 0, half == 1)
                    if pos == 0:
                        for i in (2, 3):
                            pe.wait_ge(free[X[i]], ev(("norm", l, k[0]), X[i]))
                        if k == phases[1]:
                            pe.wait_ge(cst_loaded, 16)
                    if pos == 1 and k == phases[1]:
                        b = X[3]
                        pe.wait_ge(bias_loaded, 16 * 3)
                        pe.wait_ge(free[b], use("bias_rows", b))
                        mm(bank[b][0:8, 0:384], tab[0:33, :], onehot[0:33, :], start=True, stop=True).then_inc(full[b], 1)
                    attend(k, pos)
                if first:
                    ys = [U1["fq"] + i * P for i in range(2)] + [U1["gq"] + i * P for i in range(2)] \
                        + [U1["rq"] + i * P for i in range(2)] + [U1["xbc"] + i * P for i in range(4)]
                    pe.wait_ge(free[X[0]], ev((k, "fy"), X[0]))
                    pe.wait_ge(T["y_gla"], at("y_gla", l))
                    pe.wait_ge(T["y_ret"], at("y_ret", l))
                else:
                    ys = [U2["qa"] + i * P for i in range(2)] + [None, None] + [U2["pc"] + i * P for i in range(2)] \
                        + [U2["qd"] + i * P for i in range(2)]
                    pe.wait_ge(free[X[2]], ev((k, "ay"), X[2]))
                    pe.wait_ge(free[X[2]], ev((k, "py"), X[2]))
                    pe.wait_ge(T["y_dif"], at("y_dif", l))
                for i in range(ny):
                    if first and i == 3:
                        pe.wait_ge(T["y_ssd"], at("y_ssd", l))
                    if not first and i == 1:
                        b = X[i % 4]
                        pe.wait_ge(T["y_conv"], at("y_conv", l))
                        pe.wait_ge(free[b], use((k, "yT", i), b))
                        mm(bank[b][:, :], ident, ybT[:, :, :].rearrange("p a b -> p (a b)"), start=True, stop=True).then_inc(full[b], 1)
                    else:
                        transposes_to((k, "yT", i), X[i % 4], [u[:, t, ys[2 * i + j]:ys[2 * i + j] + P] for j in range(2) for t in range(NT)])
                c = c0 + 2 * nb
                kt = 0
                for br in range(4):
                    banks = (0, 1, 2, 3) if br % 2 == 0 else X
                    tiles = 4 if first and br == 3 else 2
                    for b in banks:
                        pe.wait_ge(free[b], use((k, "up", br), b))
                    for j in range(0, tiles, 2):
                        i = kt // 2
                        pe.wait_ge(free[X[i % 4]], ev((k, "yT", i), X[i % 4]))
                        gemm_rows(banks, c, xt(kt), j == 0, j == tiles - 2, by_half=br == 3 and j == tiles - 2)
                        c += 1
                        kt += 2
                name = "whole" if first else "whole_b"

                def merged_columns(half):
                    pe.wait_ge(T[name], at(name, l, 2 * half + 2))
                    for i in (2 * half, 2 * half + 1):
                        transposes_to((k, "mT", i), X[i], [u[:, t, (2 * i + j) * P:(2 * i + j + 1) * P] for j in range(2) for t in range(NT)])

                merged_columns(0)
                for b in range(4):
                    pe.wait_ge(free[b], use((k, "out"), b))
                for i in range(4):
                    pe.wait_ge(free[X[i]], ev((k, "mT", i), X[i]))
                    gemm_rows((0, 1, 2, 3), c, xt(2 * i), i == 0, i == 3, by_half=i == 3)
                    c += 1
                    if i == 0:
                        merged_columns(1)

            def feed_forward(k, J):
                c0 = CH[k]

                def up(j, it, c, half):
                    if j == 0:
                        for i in (2 * half, 2 * half + 1):
                            pe.wait_ge(free[X[i]], ev(("norm", k[1], k[0]), X[i]))
                    banks = [gbank(j, t) for t in range(NT)]
                    if half == 0:
                        for b in banks:
                            pe.wait_ge(free[b], use((k, "U", j), b) + 2 * it)
                    gemm_half(banks, c0 + c, 4 * half, half == 0, half == 1, it)

                def turn(j, it):
                    for t in range(NT):
                        b = gbank(j, t)
                        pe.wait_ge(free[b], use((k, "T", j), b) + 2 * it)
                        tr(bank[b][:, 0:P], gprod[:, t, 0:P])
                        tr(bank[b][:, P:2 * P], gprod[:, t, P:2 * P]).then_inc(full[b], 1)

                def down(j, it, c):
                    if j == 0:
                        for b in X:
                            pe.wait_ge(free[b], use((k, "D"), b))
                    for t in range(NT):
                        b = gbank(j, t)
                        pe.wait_ge(free[b], ev((k, "T", j), b) + 2 * it)
                    gemm_rows(X, c0 + c, lambda kk, t: (ghi[:, kk, t, :], glo[:, kk, t, :]), j == 0, j == J - 1, it,
                              by_half=j == J - 1)

                walk(pe, J, lambda j, it, c: up(j, it, c, 0), turn, lambda j, it, c: up(j, it, c, 1), down)

            def gather(k, e):
                pe.wait_ge(norm_h, NT)
                pe.wait_ge(pick_ready, e + 1)
                for i in range(2):
                    b = 2 + i
                    pe.wait_ge(free[b], use((k, "gather"), b) + JU[b] * e)
                    for m in range(4):
                        for t in range(NT):
                            last = mm(bank[b][:, m * P:m * P + P], hrow[:, t, (4 * i + m) * P:(4 * i + m + 1) * P],
                                      pick[:, t, :], start=t == 0, stop=t == NT - 1)
                    last.then_inc(full[b], 1)

            def scatter(k, e):
                for b in (X[0], X[1]):
                    pe.wait_ge(free[b], use((k, "D"), b) + JU[b] * e)
                for b, (t, n) in zip((X[2], X[3], 2, 3), ((0, 0), (0, 1), (1, 0), (1, 1))):
                    pe.wait_ge(free[b], use((k, "scatter"), b) + JU[b] * e)
                    mm(bank[b][:, :], pick_t[:, t, :], y[:, n * 512:n * 512 + 512], start=True, stop=True).then_inc(full[b], 1)

            def expert_job(k, J, e):
                c0, per = CH[k], 3 * J

                def up(j, it, c, half):
                    b = j % 2
                    if half == 0:
                        pe.wait_ge(free[b], use((k, "U", j), b) + 2 * it + JU[b] * e)
                    if j == 0:
                        pe.wait_ge(free[2 + half], ev((k, "gather"), 2 + half) + JU[2 + half] * e)
                    s, h = (c0 + c) % RAW, (c0 + c) % HI
                    pe.wait_ge(lo_ready, c0 + c + 1 + 6 * it + per * e)
                    for m in range(4):
                        kt, w = 4 * half + m, slice(m * 512, m * 512 + 512)
                        mm(bank[b][:, :], xhi[:, kt, 0:P], hi[:, h, w], start=kt == 0, stop=False)
                        mm(bank[b][:, :], xlo[:, kt, 0:P], hi[:, h, w], start=False, stop=False)
                        last = mm(bank[b][:, :], xhi[:, kt, 0:P], lo[:, s, w], start=False, stop=kt == KT - 1)
                    last.then_inc(w_used, 1)

                def middle():
                    scatter(k, e)
                    b = X[2]
                    pe.wait_ge(free[b], use((k, "turned"), b) + JU[b] * e)
                    for t in range(NT):
                        last = tr(bank[b][:, t * P:t * P + P], pick_g[:, t, :])
                    last.then_inc(full[b], 1)

                def turn(j, it):
                    b = j % 2
                    pe.wait_ge(free[b], use((k, "T", j), b) + 2 * it + JU[b] * e)
                    tr(bank[b][:, 0:P], gprod[:, 0, 0:P])
                    tr(bank[b][:, P:2 * P], gprod[:, 0, P:2 * P]).then_inc(full[b], 1)

                def down(j, it, c):
                    if j == 0:
                        for b in (X[0], X[1]):
                            pe.wait_ge(free[b], use((k, "D"), b) + JU[b] * e)
                    pe.wait_ge(free[j % 2], ev((k, "T", j), j % 2) + 2 * it + JU[j % 2] * e)
                    s, h = (c0 + c) % RAW, (c0 + c) % HI
                    pe.wait_ge(lo_ready, c0 + c + 1 + 6 * it + per * e)
                    for m in range(2):
                        for n in range(2):
                            o, first, final = bank[X[n]][:, :], j == 0 and m == 0, j == J - 1 and m == 1
                            w = slice(m * 1024 + n * 512, m * 1024 + n * 512 + 512)
                            mm(o, ghi[:, m, 0, :], hi[:, h, w], start=first, stop=False)
                            mm(o, glo[:, m, 0, :], hi[:, h, w], start=False, stop=False)
                            last = mm(o, ghi[:, m, 0, :], lo[:, s, w], start=False, stop=final)
                    last.then_inc(w_used, 1)

                walk(pe, J, lambda j, it, c: up(j, it, c, 0), turn, lambda j, it, c: up(j, it, c, 1), down,
                     middle, lambda: gather(k, e + 1))

            pe.wait_ge(ident_loaded, 16)
            for k, ready in zip(phases, XREADY):
                if k[0] == "norm":
                    norm(k, ready)
                elif k[0] in ("mix1", "mix2"):
                    mixer(k)
                elif k[0] != "moe":
                    feed_forward(k, FFJ[k[0]])
                else:
                    b = X[0]
                    for i in range(4):
                        pe.wait_ge(free[X[i]], ev(("norm", k[1], "moe"), X[i]))
                    pe.wait_ge(router_split, 1)
                    for kt in range(KT):
                        o = bank[b][0:NE, 0:S]
                        mm(o, router_hi[:, kt, :], xhi[:, kt, :], start=kt == 0, stop=False)
                        mm(o, router_hi[:, kt, :], xlo[:, kt, :], start=False, stop=False)
                        last = mm(o, router_lo[:, kt, :], xhi[:, kt, :], start=False, stop=kt == KT - 1)
                    last.then_inc(full[b], 1)
                    pe.wait_ge(free[b], use((k, "router"), b))
                    for t in range(NT):
                        last = nc.tensor.transpose(bank[b][:, t * NE:t * NE + NE], lgT[0:NE, t * P:t * P + P], ident_t[0:NE, 0:NE])
                    last.then_inc(full[b], 1)
                    b = X[1]
                    pe.wait_ge(free[b], use((k, "rank"), b))
                    pe.wait_ge(chosen_ready, 1)
                    mm(bank[b][:, 0:8], C("triu"), chosen[:, 0, :], start=True, stop=True)
                    for o, m in ((8, "triu"), (16, "ones")):
                        mm(bank[b][:, o:o + 8], C("ones"), chosen[:, 0, :], start=True, stop=False)
                        last = mm(bank[b][:, o:o + 8], C(m), chosen[:, 1, :], start=False, stop=True)
                    last.then_inc(full[b], 1)
                    gather(k, 0)
                    pe.wait_ge(routed, 1)
                    nj = each_job(pe, lambda e: expert_job(k, FFJ["moe"], e))
                    scatter(k, nj)

        @block.scalar
        def _(act):
            links = [0]

            def link(ins):
                links[0] += 1
                ins.then_inc(act_link, 1)
                act.wait_ge(act_link, links[0])

            def go(dst, src, f, **kw):
                return nc.scalar.activation(dst, src, f, **kw)

            def conv(c, it=0, eo=0, per=0):
                if c >= END and not per:
                    return
                act.wait_ge(raw_full[c % RAW], 32 * (c // RAW + 1) + 32 * it + 32 * (per // RAW) * eo)
                if c >= HI:
                    act.wait_ge(w_used, c - HI + 1 + 6 * it + per * eo)
                go(hi[:, c % HI, :], raw[:, c % RAW, :], ACT.Copy).then_inc(hi_ready, 1)

            def rsqrt(dst, src, n, eps, done):
                link(go(dst, src, ACT.Ln, scale=1.0 / n, bias=eps))
                go(dst, dst, ACT.Exp, scale=-0.5).then_inc(done, 1)

            def norm(k, n, ready, before=lambda t: None):
                def statistics():
                    if n == 0:
                        act.wait_ge(x_loaded, 16 * NT)
                    for b, v in ready or []:
                        act.wait_ge(free[b], v)
                    for t in range(NT):
                        before(t)
                        last = go(moe_sq[:, t, :] if k[2] == "moe" else hrow[:, t, :], x[:, t, :], ACT.Square,
                                  accum_out=nstat[:, t:t + 1])
                    link(last)
                    rsqrt(nstat[:, 4:6], nstat[:, 0:2], D, eps1, norm_rstd)
                    act.wait_ge(norm_rstd, n + 1)
                    link(go(nstat[:, 6:8], nstat[:, 4:6], ACT.Copy, scale=0.5))

                if k[2] is None:
                    statistics()
                    return
                if k[2] == "moe":
                    act.wait_ge(par2_loaded, 16 * NPAR2)
                    go(router_hi[:, :, :], router[:, :, :], ACT.Copy).then_inc(router_rounded, 1)
                if n == 0:
                    act.wait_ge(gain1_loaded, 16 * L1)
                for i in range(4):
                    b = X[i]
                    act.wait_ge(full[b], fl(k, b))
                    for j in range(2):
                        kt = 2 * i + j
                        last = go(xhi[:, kt, :], bank[b][:, j * 256:j * 256 + 256], ACT.Copy, scale=gain_col(k, kt))
                    last.then_inc(norm_hi, 1)
                if n == 0:
                    conv(0)
                    conv(1)
                statistics()
                if k[2] == "mix1":
                    if k[1] == 0:
                        act.wait_ge(narrow_loaded, 16 * NNARROW)
                    go(wsm_hi[:, :, :], wsm[:, k[1]], ACT.Copy).then_inc(narrow_rounded, 1)

            def gain_col(k, kt):
                l, f = k[1], k[2]
                return cols1[:, l, kt:kt + 1] if f == "mix1" else cols1[:, l, 8 + kt:9 + kt] if f == "ffn1" \
                    else cols2[:, l, kt:kt + 1] if f == "mix2" else cols2[:, l, 8 + kt:9 + kt]

            def softmax_exp(key, b, h, dst, max_sem, max_val):
                act.wait_ge(max_sem, max_val)
                go(dst[:, 0:P], bank[b][:, 0:P], ACT.Exp, bias=small[:, 16 + 2 * h:17 + 2 * h], accum_out=small[:, 32 + h:33 + h])
                go(dst[:, P:3 * P], bank[b][:, P:3 * P], ACT.Exp, bias=small[:, 17 + 2 * h:18 + 2 * h],
                   accum_out=small[:, 36 + h:37 + h]).then_inc(free[b], 1)

            def evac(key, b, dst, src, f=ACT.Copy, **kw):
                go(dst, src, f, **kw).then_inc(free[b], 1)

            def gemm_out(k, n):
                first = k[0] == "mix1"
                mixb = 8 if first else 5
                act.wait_ge(w_used, CH[k] + 2 * n + 2)
                for t in range(NT):
                    b = gbank(n, t)
                    if n < mixb:
                        evac((k, "gemm", n), b, u[:, t, n * 512:n * 512 + 512], bank[b][:, :], scale=nstat[:, 4 + t:5 + t])
                    else:
                        o = (n - mixb) * 512
                        evac((k, "gemm", n), b, gates[:, t, o:o + 512], bank[b][:, :], ACT.Tanh,
                             scale=nstat[:, 6 + t:7 + t])

            def wait_full(key, b):
                act.wait_ge(full[b], fl(key, b))

            def own_gemm(k, n):
                for t in range(NT):
                    act.wait_ge(free[gbank(n, t)], ev((k, "gemm", n), gbank(n, t)))

            def conv_gate(l, i):
                if i > 0:
                    act.wait_ge(T["xbc"], at("xbc", l, i))
                act.wait_ge(T["conv_out"], at("conv_out", l, i + 1))
                go(ctanh[:, :, :], E[:, 2 * i:2 * i + 2, :], ACT.Tanh).then_inc(T["conv_tanh"], 1)

            def work1(k, pos):
                l = k[1]
                if pos % 2 == 1:
                    gemm_out(k, pos // 2)
                if pos == 16 and l == 0:
                    act.wait_ge(rows_out, 16)
                if pos in (14, 16, 19):
                    conv_gate(l, (14, 16, 19).index(pos))
                if pos == 0:
                    wait_full((k, "narrow"), X[0])
                    evac(0, X[0], narT[:, :], bank[X[0]][0:28, 0:S])
                elif pos == 2:
                    act.wait_ge(T["z_abs"], at("z_abs", l))
                    link(go(zlog[:, :, :], zlog[:, :, :], ACT.Exp, scale=-1.0))
                    go(zlog[:, :, :], zlog[:, :, :], ACT.Ln, bias=1.0).then_inc(T["z_log"], 1)
                    act.wait_ge(T["fox_ss"], at("fox_ss", l))
                    rsqrt(small[:, 0:16], small[:, 0:16], HD, eps1, T["fox_rstd"])
                elif pos == 4:
                    wait_full((k, "fqk"), X[1])
                    evac(0, X[1], kT[:, :, :].rearrange("p a b -> p (a b)"), bank[X[1]][:, :], scale=cols1[:, l, 27:28])
                    wait_full((k, "fqk"), X[0])
                    for m in range(2):
                        last = go(qM[:, m].rearrange("p a b -> p (a b)"), bank[X[0]][:, :], ACT.Copy, scale=cols1[:, l, 58 + m:59 + m])
                    last.then_inc(free[X[0]], 1)
                elif pos == 5:
                    for i in range(2):
                        b = X[2 + i]
                        wait_full((k, "cum"), b)
                        for j, (e, o, sc) in enumerate([(0, 0, 1.0), (1, 256, 1.0), (2, 256, -1.0)] if i == 0 else
                                                       [(3, 0, 1.0), (4, 0, -1.0), (5, 256, 1.0)]):
                            last = go(E[:, e, :], bank[b][:, o:o + 256], ACT.Exp, scale=sc)
                        last.then_inc(free[b], 1)
                elif pos in (6, 7):
                    for h in (0, 1) if pos == 6 else (2, 3):
                        softmax_exp((k, f"fs{h}"), X[h], h, Pm[:, h, :], T["fox_max"], at("fox_max", l, h + 1))
                elif pos in (8, 9):
                    h = 1 if pos == 8 else 3
                    wait_full((k, f"ft{h}"), X[h])
                    evac(0, X[h], Pm[:, h, :], bank[X[h]][:, 0:384])
                elif pos == 11:
                    wait_full((k, "gt"), X[1])
                    evac(0, X[1], kT[:, :, :].rearrange("p a b -> p (a b)"), bank[X[1]][:, :])
                    wait_full((k, "gt"), X[3])
                    for m in range(2):
                        last = go(qM[:, m].rearrange("p a b -> p (a b)"), bank[X[3]][:, :], ACT.Copy, scale=C("halfs", m, 1))
                    last.then_inc(free[X[3]], 1)
                elif pos == 12:
                    own_gemm(k, 3)
                    wait_full((k, "gt"), X[2])
                    wait_full((k, "gt"), X[3])
                    go(tg[:, :, :], u[:, :, U1["gr"]:U1["gr"] + 256], ACT.Tanh, scale=0.5).then_inc(T["gate_tanh"], 1)
                elif pos == 15:
                    act.wait_ge(T["br_ss"], at("br_ss", l, 1))
                    rsqrt(small[:, 48:56], small[:, 48:56], HD, eps1, T["br_rstd"])
                elif pos == 16:
                    wait_full((k, "rt"), X[1])
                    evac(0, X[1], kT[:, :, :].rearrange("p a b -> p (a b)"), bank[X[1]][:, :])
                    wait_full((k, "rt"), X[3])
                    for m in range(2):
                        last = go(qM[:, m].rearrange("p a b -> p (a b)"), bank[X[3]][:, :], ACT.Copy, scale=C("halfs", m, 1))
                    last.then_inc(free[X[3]], 1)
                elif pos == 17:
                    act.wait_ge(T["y_gla"], at("y_gla", l))
                    go(tg[:, :, :], u[:, :, U1["rg"]:U1["rg"] + 256], ACT.Tanh, scale=0.5).then_inc(T["gate_tanh"], 1)
                    for h in (0, 1):
                        go(decay_tile(h), C("rel"), ACT.Exp, scale=LOG_GAMMA[h]).then_inc(T["ret_decay"], 1)
                elif pos == 18:
                    for h in (2, 3):
                        act.wait_ge(free[X[h - 2]], ev((k, f"rs{h - 2}"), X[h - 2]))
                        go(decay_tile(h), C("rel"), ACT.Exp, scale=LOG_GAMMA[h]).then_inc(T["ret_decay"], 1)
                elif pos == 20:
                    act.wait_ge(T["br_ss"], at("br_ss", l, 2))
                    rsqrt(small[:, 48:56], small[:, 48:56], HD, eps1, T["br_rstd"])
                elif pos == 22:
                    for t in range(NT):
                        wait_full((k, "xs"), X[t])
                        evac(0, X[t], u[:, t, U1["xbc"]:U1["xbc"] + 512], bank[X[t]][:, :])
                elif pos == 23:
                    for g in range(2):
                        wait_full((k, "cb"), X[2 + g])
                    go(tgz[:, :, :], u[:, :, U1["z"]:U1["z"] + 512], ACT.Tanh, scale=0.5).then_inc(T["z_tanh"], 1)
                elif pos in (24, 27):
                    for h in range(4) if pos == 24 else range(4, 8):
                        wait_full((k, f"sg{h}"), X[h % 4])
                        evac(0, X[h % 4], Pm[:, h % 4, :], bank[X[h % 4]][:, 0:384], ACT.Exp)
                elif pos == 29:
                    act.wait_ge(T["br_ss"], at("br_ss", l, 3))
                    rsqrt(small[:, 48:52], small[:, 48:52], 4 * 256, eps1, T["br_rstd"])

            def decay_tile(h):
                return qD[:, h % 2].rearrange("p a b -> p (a b)")

            def work2(k, pos):
                l = k[1]
                if pos % 2 == 1:
                    gemm_out(k, pos // 2)
                if pos in (2, 10):
                    key = (k, "aqk" if pos == 2 else "dqk")
                    wait_full(key, X[1])
                    evac(0, X[1], kT2[:, :, :].rearrange("p a b -> p (a b)"), bank[X[1]][:, :])
                    wait_full(key, X[0])
                    for m in range(2 if pos == 2 else 4):
                        last = go(qM2[:, m].rearrange("p a b -> p (a b)"), bank[X[0]][:, :], ACT.Copy,
                                  scale=C("halfs", m, 1) if pos == 2 else C("quarter", m, 1))
                    last.then_inc(free[X[0]], 1)
                elif pos == 3:
                    for h in range(4):
                        softmax_exp((k, f"as{h}"), X[h], h, P2m[:, h, :], T["moba_max"], at("moba_max", l, h + 1))
                elif pos == 5:
                    for h in (1, 3):
                        wait_full((k, f"at{h}"), X[h])
                        evac(0, X[h], P2m[:, h, :], bank[X[h]][:, 0:384])
                elif pos == 8:
                    for i in range(2):
                        wait_full((k, "pl"), X[i])
                        evac(0, X[i], plT[:, 2 * i:2 * i + 2, :].rearrange("p a b -> p (a b)"), bank[X[i]][0:64, :])
                elif pos == 9:
                    wait_full((k, "py"), X[2])
                    evac(0, X[2], u[:, :, U2["pc"]:U2["pc"] + 256], bank[X[2]][:, :].rearrange("p (t n) -> p t n", t=2))
                elif pos in (12, 17):
                    r = 0 if pos == 12 else 1
                    for i in range(4):
                        softmax_exp((k, f"ds{4 * r + i}"), X[i], i, P2m[:, i, :], T["dif_max"], at("dif_max", l, 4 * r + i + 1))
                elif pos in (14, 19):
                    r = 0 if pos == 14 else 1
                    i = 1
                    wait_full((k, f"dt{2 * r + i}"), X[i])
                    evac(0, X[i], P2m[:, 2 * i, :], bank[X[i]][:, 0:384])
                elif pos == 21:
                    act.wait_ge(T["d_ss"], at("d_ss", l))
                    rsqrt(small[:, 48:56], small[:, 48:56], HD, eps2, T["d_rstd"])

            def hi_tiles(k, what, i, name, l, ycol):
                b = X[i % 4]
                wait_full((k, what, i), b)
                for j in range(2):
                    kt = 2 * i + j
                    last = go(xhi[:, kt, :], bank[b][:, j * 256:j * 256 + 256], ACT.Copy,
                              scale=0.5 if ycol is None else ycol[:, kt:kt + 1])
                last.then_inc(T[name], 1)

            def mixer(k):
                c0, l = CH[k], k[1]
                first = k[0] == "mix1"
                nb, work, ny = (16, work1, 5) if first else (13, work2, 4)
                for pos in range(2 * nb):
                    conv(c0 + pos + 2)
                    work(k, pos)
                    if c0 + pos == 1:
                        setup()
                yc = cols1[:, l, 16:26] if first else cols2[:, l, 17:25]
                for i in range(ny):
                    hi_tiles(k, "yT", i, "y_hi" if first else "y_hi_b", l, yc)
                for pos in range(2 * nb, 2 * nb + ny):
                    conv(c0 + pos + 2)
                for i in range(4):
                    hi_tiles(k, "mT", i, "m_hi" if first else "m_hi_b", l, None)
                for pos in range(2 * nb + ny, 2 * nb + ny + 4):
                    conv(c0 + pos + 2)

            def feed_forward(k, J):
                c0 = CH[k]

                def up_done(j, it, c):
                    conv(c0 + c + 2, it)
                    for t in range(NT):
                        act.wait_ge(w_used, c0 + c + 1 + 6 * it)
                        go(silu[:, t, :], bank[gbank(j, t)][:, 0:FB], ACT.Silu, scale=nstat[:, 4 + t:5 + t]).then_inc(silu_done, 1)

                def turn(j, it):
                    for t in range(NT):
                        b = gbank(j, t)
                        act.wait_ge(full[b], fl((k, "T", j), b) + it)
                        go(ghi[:, :, t, :], bank[b][:, 0:FB].rearrange("p (a b) -> p a b", a=2), ACT.Copy).then_inc(ghi_done, 1)

                walk(act, J, lambda j, it, c: conv(c0 + c + 2, it), turn, up_done, lambda j, it, c: conv(c0 + c + 2, it))

            def gathered(k, e):
                for i in range(2):
                    b = 2 + i
                    act.wait_ge(full[b], fl((k, "gather"), b) + JF[b] * e)
                    go(xhi[:, 4 * i:4 * i + 4, 0:P], bank[b][:, :].rearrange("p (m n) -> p m n", m=4), ACT.Copy).then_inc(gather_hi, 1)

            def expert_job(k, J, e):
                c0, per = CH[k], 3 * J

                def up_done(j, it, c):
                    conv(c0 + c + 2, it, e, per)
                    act.wait_ge(w_used, c0 + c + 1 + 6 * it + per * e)
                    go(silu[:, 0, :], bank[j % 2][:, 0:FB], ACT.Silu).then_inc(silu_done, 1)

                def turn(j, it):
                    b = j % 2
                    act.wait_ge(full[b], fl((k, "T", j), b) + it + JF[b] * e)
                    go(ghi[:, :, 0, :], bank[b][:, 0:FB].rearrange("p (a b) -> p a b", a=2), ACT.Copy).then_inc(ghi_done, 1)

                walk(act, J, lambda j, it, c: conv(c0 + c + 2, it, e, per), turn, up_done,
                     lambda j, it, c: conv(c0 + c + 2, it, e, per), late=lambda: gathered(k, e + 1))
                act.wait_ge(w_used, c0 + per + per * e)
                for n in range(2):
                    go(y[:, n * 512:n * 512 + 512], bank[X[n]][:, :], ACT.Copy).then_inc(free[X[n]], 1)

            def setup():
                act.wait_ge(setup_v, 1)
                for i in range(2):
                    last = go(rot[:, i], ang[:, i], ACT.Sin)
                for l in range(L1):
                    go(heads8[:, l, 0:8], heads8[:, l, 0:8], ACT.Exp)
                go(lam[:, :, 0:2], lam[:, :, 0:2], ACT.Exp).then_inc(setup_s, 1)

            eps1, eps2 = epst[:, 0:1], epst[:, 1:2]

            def gain(dst, src):
                act.dma_start(dst, src).then_inc(gain1_loaded, 16)

            def narrow(dst, src):
                act.dma_start(dst, src).then_inc(narrow_loaded, 16)

            act.dma_start(ident_t[:, :], a["ident"]).then_inc(ident_loaded, 16)
            for l in range(L1):
                gain(cols1[:, l, 0:8], a["ln1"][l].rearrange("(k p) -> p k", p=P))
            act.wait_ge(tiles_set, 1)
            link(go(nstat[:, 0:1], epst[:, 0:1], ACT.Exp))
            o = 0
            for f, w in W1SMALL:
                narrow(wsm[:, :, :, o:o + w].rearrange("p l k n -> p (l k) n"),
                       a["w_in"].rearrange("l (k p) n -> p (l k) n", p=P)[:, :, f:f + w])
                o += w
            narrow(brow[:, :, 0:4], a["fox_bf"].partition_broadcast(P))
            narrow(brow[:, :, 4:12], a["ssd_dt_bias"].partition_broadcast(P))
            narrow(gw2[0:16, :, :], a["gla_w2"].rearrange("l r n -> r l n"))
            act.dma_start(cst[:, :], a["cst"]).then_inc(cst_loaded, 16)
            n = 0
            for k, ready in zip(phases, XREADY):
                if k[0] == "norm":
                    norm(k, n, ready)
                    n += 1
                elif k[0] in ("mix1", "mix2"):
                    mixer(k)
                elif k[0] != "moe":
                    feed_forward(k, FFJ[k[0]])
                else:
                    def normalised(t):
                        act.wait_ge(rows_gained, t + 1)
                        go(hrow[:, t, :], hrow[:, t, :], ACT.Copy, scale=nstat[:, 4 + t:5 + t]).then_inc(norm_h, 1)

                    normalised(0)
                    act.wait_ge(route_m, 1)
                    for t in range(NT):
                        last = go(top2[:, t, 0:1], m8[:, t, 1:2], ACT.Exp, bias=top2[:, t, 1:2])
                    last.then_inc(route_e, 1)
                    normalised(1)
                    gathered(k, 0)
                    act.wait_ge(routed, 1)
                    nj = each_job(act, lambda e: expert_job(k, FFJ["moe"], e))

                    def last_job(t):
                        for b in ((X[2], X[3]), (2, 3))[t]:
                            act.wait_ge(free[b], ev((k, "scatter"), b) + JU[b] * nj)

                    norm(("norm", 0, None), n, None, last_job)
            if phases[-1][0] != "moe":
                norm(("norm", 0, None), n, last_x)

        @block.vector
        def _(dve):
            links = [0]
            V = nc.vector

            def link(ins):
                links[0] += 1
                ins.then_inc(dve_link, 1)
                dve.wait_ge(dve_link, links[0])

            def conv(c, it=0, eo=0, per=0):
                if c >= END and not per:
                    return
                dve.wait_ge(hi_ready, c + 1 + 6 * it + per * eo)
                V.tensor_tensor(lo[:, c % RAW, :], raw[:, c % RAW, :], hi[:, c % HI, :].bitcast(F32),
                                ALU.subtract).then_inc(lo_ready, 1)

            def lo_tiles(b, hi_sem, hi_val, i, gain):
                dve.wait_ge(hi_sem, hi_val)
                for j in range(2):
                    kt = 2 * i + j
                    src = bank[b][:, j * 256:j * 256 + 256]
                    g = gain(kt)
                    last = V.scalar_tensor_tensor(out=xlo[:, kt, :], in0=src, scalar=g, in1=xhi[:, kt, :].bitcast(F32),
                                                  op0=ALU.mult, op1=ALU.subtract)
                last.then_inc(free[b], 1)

            def norm(k, n):
                l, f = k[1], k[2]
                if n == 0:
                    dve.wait_ge(gain1_loaded, 16 * L1)
                if f is None:
                    dve.wait_ge(norm_rstd, n + 1)
                    dve.wait_ge(fgain_in, 16)
                    for t in range(NT):
                        V.scalar_tensor_tensor(out=hrow[:, t, :], in0=x[:, t, :], scalar=nstat[:, 4 + t:5 + t], in1=fgain[:, :],
                                               op0=ALU.mult, op1=ALU.mult).then_inc(norm_h, 1)
                    return
                if f == "moe":
                    dve.wait_ge(router_rounded, 1)
                    V.tensor_tensor(router_lo[:, :, :], router[:, :, :], router_hi[:, :, :].bitcast(F32), ALU.subtract).then_inc(router_split, 1)
                col = (lambda kt: cols1[:, l, kt:kt + 1]) if f == "mix1" else (lambda kt: cols1[:, l, 8 + kt:9 + kt]) if f == "ffn1" \
                    else (lambda kt: cols2[:, l, kt:kt + 1]) if f == "mix2" else (lambda kt: cols2[:, l, 8 + kt:9 + kt])
                for i in range(4):
                    lo_tiles(X[i], norm_hi, 4 * n + i + 1, i, col)
                if n == 0:
                    conv(0)
                    conv(1)
                if f == "mix1":
                    dve.wait_ge(narrow_rounded, l + 1)
                    V.tensor_tensor(wsm_lo[:, l], wsm[:, l], wsm_hi[:, :, :].bitcast(F32), ALU.subtract).then_inc(narrow_split, 1)

            def wait_full(key, b):
                dve.wait_ge(full[b], fl(key, b))

            def out_of(k, n):
                for t in range(NT):
                    dve.wait_ge(free[gbank(n, t)], ev((k, "gemm", n), gbank(n, t)))

            def maxima(key, b, h, name, l, n):
                wait_full(key, b)
                V.tensor_reduce(small[:, 16 + 2 * h:17 + 2 * h], bank[b][:, 0:P], AX, ALU.max, negate=True)
                V.tensor_reduce(small[:, 17 + 2 * h:18 + 2 * h], bank[b][:, P:3 * P], AX, ALU.max, negate=True).then_inc(T[name], 1)

            def heads(ap, d=HD):
                return ap.rearrange("p t (h d) -> p t h d", d=d)

            def bc(ap, n):
                return ap.unsqueeze(3).to_broadcast([P, NT, ap.shape[2], n])

            def two(ap):
                return ap.rearrange("p (t n) -> p t n", t=2)

            def sumsq(yv, scr, d, stat, done):
                link(V.tensor_tensor(scr, yv, yv, ALU.mult))
                V.tensor_reduce(stat, heads(scr, d), AX, ALU.add).then_inc(done, 1)

            def gated_norm(k, key, yo, go, which, done):
                l = k[1]
                b = X[0]
                wait_full(key, b)
                yv = u[:, :, yo:yo + 256]
                V.tensor_copy(yv, two(bank[b][:, :])).then_inc(free[b], 1)
                dve.wait_ge(free[b], ev(key, b))
                sumsq(yv, ysq[:, :, :], HD, small[:, 48:56].rearrange("p (t h) -> p t h", t=2), T["br_ss"])
                dve.wait_ge(T["gate_tanh"], at("gate_tanh", l, which))
                link(V.scalar_tensor_tensor(out=tg[:, :, :], in0=tg[:, :, :], scalar=1.0, in1=u[:, :, go:go + 256],
                                            op0=ALU.add, op1=ALU.mult))
                dve.wait_ge(T["br_rstd"], at("br_rstd", l, which))
                link(V.tensor_tensor(heads(yv), heads(yv), bc(small[:, 48:56].rearrange("p (t h) -> p t h", t=2), HD), ALU.mult))
                V.tensor_tensor(yv, yv, tg[:, :, :], ALU.mult).then_inc(T[done], 1)

            def convolve(k, i):
                l, b, key = k[1], X[2 if i < 2 else 1], (k, f"xt{i}")
                wait_full(key, b)
                cw = lambda tap, j: cols1[:, l, 28 + 6 * tap + j:29 + 6 * tap + j]
                src = [bank[b][:, j * 256:j * 256 + 256] for j in range(2)]
                for j in range(2):
                    last = V.tensor_scalar(E[:, 2 * i + j, :], src[j], cw(3, 2 * i + j), cols1[:, l, 52 + 2 * i + j:53 + 2 * i + j],
                                           ALU.mult, ALU.add)
                link(last)
                for sh in (1, 2, 3):
                    for j in range(2):
                        dst = E[:, 2 * i + j, sh:S]
                        last = V.scalar_tensor_tensor(out=dst, in0=src[j][:, 0:S - sh], scalar=cw(3 - sh, 2 * i + j), in1=dst,
                                                      op0=ALU.mult, op1=ALU.add)
                    if sh < 3:
                        link(last)
                last.then_inc(free[b], 1)
                dve.wait_ge(free[b], ev(key, b))
                V.memset(small[:, 60:61], 0.0).then_inc(T["conv_out"], 1)

            def convolved(k, i):
                l = k[1]
                dve.wait_ge(T["conv_tanh"], at("conv_tanh", l, i + 1))
                xx = E[:, 2 * i:2 * i + 2, :]
                V.scalar_tensor_tensor(out=xx, in0=ctanh[:, :, :], scalar=1.0, in1=xx, op0=ALU.add, op1=ALU.mult).then_inc(T["xbc"], 1)
                if i == 2:
                    dve.wait_ge(T["xbc"], at("xbc", l, 3))
                    for g in range(2):
                        last = V.tensor_scalar(kT[:, g, :], E[:, 5, :], C("half", g, 1), None, ALU.mult)
                    last.then_inc(T["ssd_c"], 1)

            def clamp_to(dst, b, key, done=None):
                wait_full(key, b)
                V.tensor_tensor(dst, bank[b][:, 0:384], C("clamp"), ALU.min).then_inc(free[b], 1)
                dve.wait_ge(free[b], ev(key, b))
                r = V.scalar_tensor_tensor(out=dst, in0=C("clamp"), scalar=-1.0, in1=dst, op0=ALU.mult, op1=ALU.max)
                if done is not None:
                    r.then_inc(done, 1)
                return r

            def work1(k, pos):
                l = k[1]
                if pos == 1:
                    out_of(k, 0)
                    sumsq(u[:, :, 0:512], sq[:, :, :], HD, small[:, 0:16].rearrange("p (t h) -> p t h", t=2), T["fox_ss"])
                elif pos == 2:
                    wait_full((k, "zg"), X[2])
                    dve.wait_ge(glab_loaded, 16 * (l + 1))
                    dve.wait_ge(norm_rstd, 2 * l + 1)
                    for t in range(NT):
                        last = V.scalar_tensor_tensor(out=z[:, t, 0:256], in0=bank[X[2]][:, 256 * t:256 * t + 256], scalar=nstat[:, 4 + t:5 + t],
                                                      in1=glab[:, :], op0=ALU.mult, op1=ALU.add)
                    last.then_inc(free[X[2]], 1)
                    wait_full((k, "nt"), X[1])
                    for t in range(NT):
                        last = V.scalar_tensor_tensor(out=z[:, t, 256:268], in0=bank[X[1]][:, 28 * t + 16:28 * t + 28],
                                                      scalar=nstat[:, 4 + t:5 + t], in1=brow[:, l, :], op0=ALU.mult, op1=ALU.add)
                    last.then_inc(free[X[1]], 1)
                    dve.wait_ge(free[X[1]], ev((k, "nt"), X[1]))
                    V.scalar_tensor_tensor(out=zlog[:, :, :], in0=z[:, :, :], scalar=-1.0, in1=z[:, :, :], op0=ALU.mult,
                                           op1=ALU.max).then_inc(T["z_abs"], 1)
                elif pos == 3:
                    dve.wait_ge(T["z_log"], at("z_log", l))
                    V.scalar_tensor_tensor(out=dtv[:, :, :], in0=z[:, :, 260:268], scalar=0.0, in1=zlog[:, :, 260:268],
                                           op0=ALU.max, op1=ALU.add)
                    link(V.scalar_tensor_tensor(out=z[:, :, 0:260], in0=z[:, :, 0:260], scalar=0.0, in1=zlog[:, :, 0:260],
                                                op0=ALU.min, op1=ALU.subtract))
                    V.tensor_scalar(z[:, :, 0:256], z[:, :, 0:256], 1.0 / 16.0, None, ALU.mult)
                    if l == 0:
                        dve.wait_ge(setup_s, 1)
                    V.scalar_tensor_tensor(out=z[:, :, 260:268], in0=dtv[:, :, :], scalar=-1.0,
                                           in1=heads8[:, l, 0:8].unsqueeze(1).to_broadcast([P, NT, 8]), op0=ALU.mult,
                                           op1=ALU.mult).then_inc(T["decay"], 1)
                    dve.wait_ge(T["fox_rstd"], at("fox_rstd", l))
                    q = heads(u[:, :, 0:512])
                    V.tensor_tensor(q, q, bc(small[:, 0:16].rearrange("p (t h) -> p t h", t=2), HD), ALU.mult).then_inc(T["fox_qn"], 1)
                elif pos in (6, 7):
                    for h in (0, 1) if pos == 6 else (2, 3):
                        maxima((k, f"fs{h}"), X[h], h, "fox_max", l, h + 1)
                    if pos == 6:
                        for i in (2, 3):
                            dve.wait_ge(free[X[i]], ev((k, "cum"), X[i]))
                        out_of(k, 1)
                        out_of(k, 2)
                        for e, t, o in ((2, 0, "gk"), (0, 0, "gk"), (1, 0, "gq"), (4, 1, "gk"), (3, 1, "gq"), (5, 1, "gq")):
                            last = V.tensor_tensor(E[:, e, :], E[:, e, :], u[:, t, U1[o]:U1[o] + 256], ALU.mult)
                        last.then_inc(T["gla_prod"], 1)
                elif pos in (8, 9):
                    h = 0 if pos == 8 else 2
                    wait_full((k, f"ft{h}"), X[h])
                    V.tensor_copy(Pm[:, h, :], bank[X[h]][:, 0:384]).then_inc(free[X[h]], 1)
                elif pos == 10:
                    for h in range(4):
                        dve.wait_ge(free[X[h]], ev((k, f"fs{h}"), X[h]))
                    link(V.reciprocal(small[:, 40:48], small[:, 32:40]))
                    wait_full((k, "fy"), X[0])
                    V.tensor_tensor(heads(u[:, :, 0:256]), heads(two(bank[X[0]][:, :])),
                                    bc(small[:, 40:48].rearrange("p (t h) -> p t h", t=2), HD), ALU.mult).then_inc(free[X[0]], 1)
                elif pos == 11:
                    b = X[2]
                    wait_full((k, "gt"), b)
                    V.tensor_copy(kE[:, :, :].rearrange("p a b -> p (a b)"), bank[b][:, 0:256])
                    for m in range(2):
                        last = V.tensor_scalar(qD[:, m].rearrange("p a b -> p (a b)"), bank[b][:, 256:512], C("halfs", m, 1), None, ALU.mult)
                    last.then_inc(free[b], 1)
                elif pos == 13:
                    for h in range(4):
                        clamp_to(Pm[:, h, :], X[h], (k, f"gs{h}"), T["gla_p"])
                elif pos in (14, 16, 19):
                    convolve(k, (14, 16, 19).index(pos))
                elif pos == 17:
                    convolved(k, 1)
                elif pos == 15:
                    convolved(k, 0)
                    gated_norm(k, (k, "gy"), U1["gq"], U1["gr"], 1, "y_gla")
                elif pos == 18:
                    for h in range(4):
                        b, r = X[h], qD[:, h % 2].rearrange("p a b -> p (a b)")
                        wait_full((k, f"rs{h}"), b)
                        dve.wait_ge(T["ret_decay"], at("ret_decay", l, h + 1))
                        V.tensor_tensor(Pm[:, h, 0:256], bank[b][:, 0:256], r, ALU.mult)
                        V.tensor_tensor(Pm[:, h, 256:384], bank[b][:, 256:384], r[:, 0:P], ALU.mult).then_inc(free[b], 1)
                elif pos == 20:
                    convolved(k, 2)
                    gated_norm(k, (k, "ry"), U1["rq"], U1["rg"], 2, "y_ret")
                elif pos == 22:
                    for g in range(2):
                        link(clamp_to(cbm[:, g, :], X[2 + g], (k, "cb")))
                    for t in range(NT):
                        dve.wait_ge(free[X[t]], ev((k, "xs"), X[t]))
                    V.tensor_tensor(heads(u[:, :, 256:768]), heads(u[:, :, U1["xbc"]:U1["xbc"] + 512]), bc(dtv[:, :, :], HD),
                                    ALU.mult).then_inc(T["ssd_x"], 1)
                elif pos in (24, 27):
                    for h in range(4) if pos == 24 else range(4, 8):
                        dve.wait_ge(free[X[h % 4]], ev((k, f"sg{h}"), X[h % 4]))
                        V.tensor_tensor(Pm[:, h % 4, :], Pm[:, h % 4, :], cbm[:, h // 4, :], ALU.mult).then_inc(T["ssd_p"], 1)
                    if pos == 24:
                        dve.wait_ge(T["z_tanh"], at("z_tanh", l))
                        link(V.scalar_tensor_tensor(out=tgz[:, :, :], in0=tgz[:, :, :], scalar=1.0,
                                                    in1=u[:, :, U1["z"]:U1["z"] + 512], op0=ALU.add, op1=ALU.mult))
                elif pos in (26, 29):
                    r = 0 if pos == 26 else 1
                    key, b = (k, f"sy{r}"), X[0]
                    wait_full(key, b)
                    dve.wait_ge(T["ssd_dx"], at("ssd_dx", l, r + 1))
                    V.tensor_tensor(u[:, :, U1["xbc"] + 256 * r:U1["xbc"] + 256 * r + 256], two(bank[b][:, :]), qM[:, r],
                                    ALU.add).then_inc(free[b], 1)
                    if r == 1:
                        dve.wait_ge(free[b], ev(key, b))
                        yv = u[:, :, U1["xbc"]:U1["xbc"] + 512]
                        link(V.tensor_tensor(yv, yv, tgz[:, :, :], ALU.mult))
                        scr = qM[:, :, :, :].rearrange("p a b c -> p (a b c)").rearrange("p (t n) -> p t n", t=2)
                        sumsq(yv, scr, 256, small[:, 48:52].rearrange("p (t h) -> p t h", t=2), T["br_ss"])
                        dve.wait_ge(T["br_rstd"], at("br_rstd", l, 3))
                        V.tensor_tensor(heads(yv, 256), heads(yv, 256), bc(small[:, 48:52].rearrange("p (t h) -> p t h", t=2), 256),
                                        ALU.mult).then_inc(T["y_ssd"], 1)

            def work2(k, pos):
                l = k[1]
                if pos == 3:
                    for h in range(4):
                        maxima((k, f"as{h}"), X[h], h, "moba_max", l, h + 1)
                elif pos == 5:
                    for h in (0, 2):
                        wait_full((k, f"at{h}"), X[h])
                        V.tensor_copy(P2m[:, h, :], bank[X[h]][:, 0:384]).then_inc(free[X[h]], 1)
                    out_of(k, 1)
                    out_of(k, 2)
                    cx = u[:, :, U2["cb"]:U2["cb"] + 256]
                    V.tensor_tensor(cx, cx, u[:, :, U2["xb"]:U2["xb"] + 256], ALU.mult).then_inc(T["conv_in"], 1)
                elif pos == 6:
                    cw = lambda tap, j: conv2[:, l, 2 * tap + j:2 * tap + j + 1]
                    b = X[0]
                    wait_full((k, "cx"), b)
                    for j in range(2):
                        last = V.tensor_scalar(ybT[:, j, :], bank[b][:, j * 256:j * 256 + 256], cw(2, j), None, ALU.mult)
                    link(last)
                    for sh in (1, 2):
                        for j in range(2):
                            dst = ybT[:, j, sh:S]
                            last = V.scalar_tensor_tensor(out=dst, in0=bank[b][:, j * 256:j * 256 + S - sh], scalar=cw(2 - sh, j), in1=dst,
                                                          op0=ALU.mult, op1=ALU.add)
                        if sh == 1:
                            link(last)
                    last.then_inc(free[b], 1)
                    dve.wait_ge(free[b], ev((k, "cx"), b))
                    b = X[1]
                    wait_full((k, "cx"), b)
                    yb = ybT[:, :, :].rearrange("p a b -> p (a b)")
                    V.tensor_tensor(yb, yb, bank[b][:, :], ALU.mult).then_inc(free[b], 1)
                    dve.wait_ge(free[b], ev((k, "cx"), b))
                    V.memset(small[:, 60:61], 0.0).then_inc(T["y_conv"], 1)
                elif pos == 7:
                    for h in range(4):
                        dve.wait_ge(free[X[h]], ev((k, f"as{h}"), X[h]))
                    link(V.reciprocal(small[:, 40:48], small[:, 32:40]))
                    wait_full((k, "ay"), X[2])
                    V.tensor_tensor(heads(u[:, :, 0:256]), heads(two(bank[X[2]][:, :])),
                                    bc(small[:, 40:48].rearrange("p (t h) -> p t h", t=2), HD), ALU.mult).then_inc(free[X[2]], 1)
                elif pos in (12, 17):
                    r = 0 if pos == 12 else 1
                    for i in range(4):
                        maxima((k, f"ds{4 * r + i}"), X[i], i, "dif_max", l, 0)
                    for i in range(4):
                        dve.wait_ge(free[X[i]], ev((k, f"ds{4 * r + i}"), X[i]))
                    link(V.reciprocal(small[:, 40:48], small[:, 32:40]))
                    for t in range(NT):
                        for i in (1, 3):
                            cc = 40 + 4 * t + i
                            last = V.tensor_scalar(small[:, cc:cc + 1], small[:, cc:cc + 1], lam[:, l, 2:3], None, ALU.mult)
                    link(last)
                    for i in range(2):
                        for t, s in ((0, slice(0, P)), (1, slice(P, 3 * P))):
                            cc = 40 + 4 * t + 2 * i + 1
                            last = V.tensor_scalar(P2m[:, 2 * i + 1, s], P2m[:, 2 * i + 1, s], small[:, cc:cc + 1], None, ALU.mult)
                        link(last)
                        for t, s in ((0, slice(0, P)), (1, slice(P, 3 * P))):
                            cc = 40 + 4 * t + 2 * i
                            last = V.scalar_tensor_tensor(out=P2m[:, 2 * i, s], in0=P2m[:, 2 * i, s], scalar=small[:, cc:cc + 1],
                                                          in1=P2m[:, 2 * i + 1, s], op0=ALU.mult, op1=ALU.add)
                        last.then_inc(T["dif_p"], 1)
                elif pos in (14, 19):
                    r = 0 if pos == 14 else 1
                    wait_full((k, f"dt{2 * r}"), X[0])
                    V.tensor_copy(P2m[:, 0, :], bank[X[0]][:, 0:384]).then_inc(free[X[0]], 1)
                elif pos in (15, 20):
                    r = 0 if pos == 15 else 1
                    b, key = X[2], (k, f"dy{r}")
                    wait_full(key, b)
                    V.tensor_copy(u[:, :, U2["qd"] + 128 * r:U2["qd"] + 128 * r + 128], two(bank[b][:, :])[:, :, 0:128]).then_inc(free[b], 1)
                    if r == 1:
                        dve.wait_ge(free[b], ev(key, b))
                        yv = u[:, :, U2["qd"]:U2["qd"] + 256]
                        sumsq(yv, qM2[:, 0], HD, small[:, 48:56].rearrange("p (t h) -> p t h", t=2), T["d_ss"])
                elif pos == 21:
                    dve.wait_ge(T["d_rstd"], at("d_rstd", l))
                    yv = heads(u[:, :, U2["qd"]:U2["qd"] + 256])
                    V.tensor_tensor(yv, yv, bc(small[:, 48:56].rearrange("p (t h) -> p t h", t=2), HD), ALU.mult).then_inc(T["y_dif"], 1)

            def mixer(k):
                c0, l = CH[k], k[1]
                first = k[0] == "mix1"
                nb, work, ny = (16, work1, 5) if first else (13, work2, 4)
                for pos in range(2 * nb):
                    conv(c0 + pos + 2)
                    work(k, pos)
                    if c0 + pos == 1:
                        setup()
                        wait_full("bias_rows", X[3])
                        V.tensor_copy(tabT[0:8, :], bank[X[3]][0:8, 0:384]).then_inc(free[X[3]], 1)
                    if c0 + pos == 4:
                        negative_lambda()
                yc = cols1[:, l, 16:26] if first else cols2[:, l, 17:25]
                for i in range(ny):
                    lo_tiles(X[i % 4], T["y_hi" if first else "y_hi_b"], at("y_hi" if first else "y_hi_b", l, i + 1), i,
                             lambda kt: yc[:, kt:kt + 1])
                pos = 2 * nb
                mixb = 8 if first else 5

                def share(br, banks, t, n):
                    b = banks[2 * t + n]
                    gg = gates[:, t, br * 1024 + n * 512:br * 1024 + n * 512 + 512]
                    dst = u[:, t, n * 512:n * 512 + 512] if br == 0 else gg
                    V.scalar_tensor_tensor(out=dst, in0=gg, scalar=1.0, in1=bank[b][:, :], op0=ALU.add, op1=ALU.mult).then_inc(free[b], 1)

                for br in range(4):
                    banks = (0, 1, 2, 3) if br % 2 == 0 else X
                    for j in range(2 if first and br == 3 else 1):
                        conv(c0 + pos + 2)
                        pos += 1
                    if br < 3:
                        dve.wait_ge(w_used, c0 + pos)
                    out_of(k, mixb + 2 * br)
                    out_of(k, mixb + 2 * br + 1)
                    if br == 3:
                        break
                    for t in range(NT):
                        for n in range(2):
                            share(br, banks, t, n)
                name = "whole" if first else "whole_b"

                def last_shares(n):
                    for t in range(NT):
                        share(3, X, t, n)

                def last_sums(n):
                    dve.wait_ge(T["merged" if first else "merged_b"], at("merged" if first else "merged_b", l, 8))
                    for t in range(NT):
                        b = X[2 * t + n]
                        dve.wait_ge(free[b], ev((k, "up", 3), b))
                        m = u[:, t, n * 512:n * 512 + 512]
                        V.tensor_tensor(m, m, gates[:, t, 3072 + n * 512:3072 + n * 512 + 512], ALU.add).then_inc(T[name], 1)

                def split(half):
                    for i in (2 * half, 2 * half + 1):
                        lo_tiles(X[i], T["m_hi" if first else "m_hi_b"], at("m_hi" if first else "m_hi_b", l, i + 1), i, lambda kt: 0.5)

                dve.wait_ge(half_done, HALF[k, "up"])
                last_shares(0)
                last_sums(0)
                dve.wait_ge(w_used, c0 + pos)
                last_shares(1)
                split(0)
                last_sums(1)
                split(1)
                for j in range(4):
                    conv(c0 + pos + 2)
                    pos += 1
                for n in range(2):
                    if n == 0:
                        dve.wait_ge(half_done, HALF[k, "out"])
                    else:
                        dve.wait_ge(w_used, c0 + pos)
                    for t in range(NT):
                        b = 2 * t + n
                        xx = x[:, t, n * 512:n * 512 + 512]
                        V.tensor_tensor(xx, bank[b][:, :], xx, ALU.add).then_inc(free[b], 1)

            def feed_forward(k, J):
                c0, f0 = CH[k], FFB[k]

                def up_done(j, it, c):
                    conv(c0 + c + 2, it)
                    for t in range(NT):
                        b = gbank(j, t)
                        dve.wait_ge(silu_done, f0 + 2 * j + t + 1 + 4 * it)
                        V.scalar_tensor_tensor(out=gprod[:, t, :], in0=bank[b][:, FB:2 * FB], scalar=nstat[:, 4 + t:5 + t],
                                               in1=silu[:, t, :], op0=ALU.mult, op1=ALU.mult).then_inc(free[b], 1)

                def turn(j, it):
                    for t in range(NT):
                        b = gbank(j, t)
                        dve.wait_ge(ghi_done, f0 + 2 * j + t + 1 + 4 * it)
                        V.tensor_tensor(glo[:, :, t, :], bank[b][:, 0:FB].rearrange("p (a b) -> p a b", a=2),
                                        ghi[:, :, t, :].bitcast(F32), ALU.subtract).then_inc(free[b], 1)

                walk(dve, J, lambda j, it, c: conv(c0 + c + 2, it), turn, up_done, lambda j, it, c: conv(c0 + c + 2, it))
                for n in range(2):
                    if n == 0:
                        dve.wait_ge(half_done, HALF[k, "D"])
                    else:
                        dve.wait_ge(w_used, c0 + 3 * J)
                    for t in range(NT):
                        b = X[2 * t + n]
                        xx = x[:, t, n * 512:n * 512 + 512]
                        V.tensor_tensor(xx, bank[b][:, :], xx, ALU.add).then_inc(free[b], 1)

            def pick_tokens(e):
                for t in range(NT):
                    where = jobpos[:, t, bass.ds(e, 1)]
                    V.tensor_scalar(pick[:, t, :], C("slots"), where, None, ALU.is_equal)
                    last = V.tensor_scalar(pick_g[:, t, :], C("slots"), where, jobgate[:, t, bass.ds(e, 1)], ALU.is_equal, ALU.mult)
                last.then_inc(pick_ready, 1)

            def gathered(k, e):
                for i in range(2):
                    b, rows = 2 + i, slice(4 * i, 4 * i + 4)
                    dve.wait_ge(gather_hi, 2 * e + i + 1)
                    V.tensor_tensor(xlo[:, rows, 0:P], bank[b][:, :].rearrange("p (m n) -> p m n", m=4),
                                    xhi[:, rows, 0:P].bitcast(F32), ALU.subtract).then_inc(free[b], 1)

            def scattered(k, e):
                for b, (t, n) in zip((X[2], X[3], 2, 3), ((0, 0), (0, 1), (1, 0), (1, 1))):
                    xx = x[:, t, n * 512:n * 512 + 512]
                    dve.wait_ge(full[b], fl((k, "scatter"), b) + JF[b] * e)
                    V.tensor_tensor(xx, bank[b][:, :], xx, ALU.add).then_inc(free[b], 1)

            def expert_job(k, J, e):
                c0, per, f0 = CH[k], 3 * J, FFB[k]

                def up_done(j, it, c):
                    conv(c0 + c + 2, it, e, per)
                    dve.wait_ge(silu_done, f0 + j + 1 + 2 * it + J * e)
                    V.tensor_tensor(gprod[:, 0, :], bank[j % 2][:, FB:2 * FB], silu[:, 0, :], ALU.mult).then_inc(free[j % 2], 1)

                def turn(j, it):
                    dve.wait_ge(ghi_done, f0 + j + 1 + 2 * it + J * e)
                    V.tensor_tensor(glo[:, :, 0, :], bank[j % 2][:, 0:FB].rearrange("p (a b) -> p a b", a=2),
                                    ghi[:, :, 0, :].bitcast(F32), ALU.subtract).then_inc(free[j % 2], 1)

                def middle():
                    scattered(k, e)
                    b = X[2]
                    dve.wait_ge(full[b], fl((k, "turned"), b) + JF[b] * e)
                    V.tensor_copy(pick_t[:, :, :].rearrange("p t n -> p (t n)"), bank[b][:, 0:NT * P]).then_inc(free[b], 1)
                    pick_tokens(e + 1)

                walk(dve, J, lambda j, it, c: conv(c0 + c + 2, it, e, per), turn, up_done,
                     lambda j, it, c: conv(c0 + c + 2, it, e, per), middle, lambda: gathered(k, e + 1))

            def route(k):
                b, key = X[0], (k, "router")
                V.memset(pick_t[:, :, :], 0.0)
                V.memset(y[:, :], 0.0)
                V.memset(jobtab[:, :, :], -1.0)
                wait_full((k, "logits"), b)
                V.tensor_copy(lgT[:, :], bank[b][0:NE, 0:S]).then_inc(free[b], 1)
                wait_full(key, b)
                dve.wait_ge(norm_rstd, len([p for p in phases if p[0] == "norm"]))
                V.tensor_tensor(lg8[:, :, :], two(bank[b][:, 0:16]), nstat[:, 4:6].unsqueeze(2).to_broadcast([P, NT, NE]),
                                ALU.mult).then_inc(free[b], 1)
                dve.wait_ge(free[b], ev(key, b))
                for t in range(NT):
                    last = V.max(m8[:, t, :], lg8[:, t, :])
                link(last)
                for t in range(NT):
                    V.max_index(i8[:, t, :], m8[:, t, :], lg8[:, t, :])
                    last = V.tensor_scalar(top2[:, t, 1:2], m8[:, t, 0:1], -1.0, None, ALU.mult)
                last.then_inc(route_m, 1)
                dve.wait_ge(route_m, 1)
                link(V.tensor_copy(i8f[:, :, :], i8[:, :, 0:2]))
                for t in range(NT):
                    last = V.tensor_scalar(chosen[:, t, :], C("experts"), i8f[:, t, 0:1], None, ALU.is_equal)
                link(last)
                for t in range(NT):
                    last = V.scalar_tensor_tensor(out=chosen[:, t, :], in0=C("experts"), scalar=i8f[:, t, 1:2], in1=chosen[:, t, :],
                                                  op0=ALU.is_equal, op1=ALU.add)
                last.then_inc(chosen_ready, 1)
                dve.wait_ge(route_e, 1)
                link(V.tensor_scalar_add(top2[:, :, 2:3], top2[:, :, 0:1], 1.0))
                link(V.reciprocal(top2[:, :, 2:3], top2[:, :, 2:3]))
                link(V.tensor_tensor(top2[:, :, 3:4], top2[:, :, 2:3], top2[:, :, 0:1], ALU.mult))
                for t in range(NT):
                    V.tensor_scalar(gate8[:, t, :], C("experts"), i8f[:, t, 0:1], top2[:, t, 2:3], ALU.is_equal, ALU.mult)
                    last = V.tensor_scalar(lg8[:, t, :], C("experts"), i8f[:, t, 1:2], top2[:, t, 3:4], ALU.is_equal, ALU.mult)
                link(last)
                V.tensor_tensor(jobgate[:, :, 0:NE], gate8[:, :, :], lg8[:, :, :], ALU.add)
                b, key = X[1], (k, "rank")
                wait_full(key, b)
                V.tensor_copy(rank[:, :, :].rearrange("p t n -> p (t n)"), bank[b][:, 0:24]).then_inc(free[b], 1)
                dve.wait_ge(free[b], ev(key, b))
                link(V.scalar_tensor_tensor(out=rank[:, 0:NT, :], in0=chosen[:, :, :], scalar=1e6, in1=rank[:, 0:NT, :],
                                            op0=ALU.mult, op1=ALU.add))
                link(V.tensor_scalar(jobpos[:, :, 0:NE], rank[:, 0:NT, :], 1000001.0, None, ALU.subtract))
                pick_tokens(0)
                link(V.tensor_scalar(over[:, 0, :], rank[:, 2, :], float(P), None, ALU.is_gt))
                V.tensor_reduce(jobs_f[:, MORE:MORE + 1], over[:, 0, :], AX, ALU.add)
                link(V.tensor_tensor(over[:, 1, :], over[:, 0, :], C("countdown"), ALU.mult))
                link(V.max(over[:, 2, :], over[:, 1, :]))
                for i in range(MORE):
                    link(V.tensor_scalar(over[:, 3, :], over[:, 1, :], over[:, 2, i:i + 1], None, ALU.is_equal))
                    link(V.tensor_tensor(prod8[:, :, :], jobtab[:, :, 0:NE], over[:, 3, :].unsqueeze(1).to_broadcast([P, 2 * NT, NE]),
                                         ALU.mult))
                    link(V.tensor_reduce(jobtab[:, :, NE + i:NE + i + 1], prod8[:, :, :], AX, ALU.add))
                V.tensor_scalar(jobpos[:, :, NE:NE + MORE], jobpos[:, :, NE:NE + MORE], float(P), None, ALU.subtract)
                link(V.tensor_scalar(jobs_f[:, 0:MORE], over[:, 2, 0:MORE], -1.0, float(NE), ALU.mult, ALU.add))
                link(V.tensor_scalar(jobs_f[:, 0:MORE], jobs_f[:, 0:MORE], float(NE - 1), None, ALU.min))
                link(V.tensor_scalar_add(jobs_f[:, MORE:MORE + 1], jobs_f[:, MORE:MORE + 1], float(NE)))
                V.tensor_copy(jobs_i[:, :], jobs_f[:, :]).then_inc(routed, 1)
                dve.wait_ge(routed, 1)

            def setup():
                dve.wait_ge(cst_loaded, 16)
                dve.wait_ge(par_loaded, 16 * NPAR_POOL)
                dve.wait_ge(par_sp_loaded, 16 * NPAR_SP)
                link(V.tensor_copy(posf[:, :], posi[:, :]))
                for t in range(NT):
                    last = V.tensor_scalar(ang[:, 0, t, :], C("freq"), posf[:, t:t + 1], None, ALU.mult)
                link(last)
                A, Kt_, R = ang[:, 0], ang[:, 2], ang[:, 3]
                link(V.tensor_scalar(Kt_, A, 1.0 / (2 * math.pi), 12582912.0, ALU.mult, ALU.add))
                link(V.tensor_scalar(Kt_, Kt_, 12582912.0, None, ALU.subtract))
                link(V.scalar_tensor_tensor(out=A, in0=Kt_, scalar=-6.28125, in1=A, op0=ALU.mult, op1=ALU.add))
                link(V.scalar_tensor_tensor(out=A, in0=Kt_, scalar=-TWO_PI_2, in1=A, op0=ALU.mult, op1=ALU.add))
                link(V.scalar_tensor_tensor(out=A, in0=Kt_, scalar=-TWO_PI_3, in1=A, op0=ALU.mult, op1=ALU.add))
                link(V.tensor_scalar(A, A, 3.1415925, -3.1415925, ALU.min, ALU.max))
                link(V.tensor_scalar(ang[:, 1], A, math.pi / 2, None, ALU.add))
                link(V.tensor_scalar(R, ang[:, 1], math.pi, -2 * math.pi, ALU.is_gt, ALU.mult))
                link(V.tensor_tensor(ang[:, 1], ang[:, 1], R, ALU.add))
                link(V.tensor_scalar(ang[:, 1], ang[:, 1], 3.1415925, -3.1415925, ALU.min, ALU.max))
                for l in range(L1):
                    for m in range(2):
                        V.tensor_scalar(cols1[:, l, 58 + m:59 + m], cols1[:, l, 26:27], C("halfs", m, 1), None, ALU.mult)
                    V.tensor_scalar(cols1[:, l, 22:26], cols1[:, l, 22:26], 0.5, None, ALU.mult)
                    V.tensor_scalar(cols1[:, l, 28:58], cols1[:, l, 28:58], 0.5, None, ALU.mult)
                    link(V.tensor_scalar(cols1[:, l, 18:21:2], cols1[:, l, 18:21:2], 0.5, None, ALU.mult))
                    last = V.tensor_copy(cols1[:, l, 19:22:2], cols1[:, l, 18:21:2])
                for i in range(2):
                    last = V.tensor_tensor(lam_in[:, :, 2 * i], lam_in[:, :, 2 * i], lam_in[:, :, 2 * i + 1], ALU.mult)
                for l in range(L1):
                    V.tensor_scalar(cols2[:, l, 23:24], cols2[:, l, 23:24], 1.0 - LAM_INIT[l], None, ALU.mult)
                    last = V.tensor_scalar(lam[:, l, 3:4], C("ones", 0, 1), LAM_INIT[l], None, ALU.mult)
                link(last)
                for l in range(L1):
                    V.tensor_copy(cols2[:, l, 24:25], cols2[:, l, 23:24])
                for i in range(2):
                    last = V.tensor_reduce(lam[:, :, i:i + 1], lam_in[:, :, 2 * i], AX, ALU.add)
                last.then_inc(setup_v, 1)

            def negative_lambda():
                link(V.tensor_tensor(lam[:, :, 2:3], lam[:, :, 1:2], lam[:, :, 0:1], ALU.subtract))
                link(V.tensor_tensor(lam[:, :, 2:3], lam[:, :, 2:3], lam[:, :, 3:4], ALU.subtract))

            for b in range(8):
                V.memset(small[:, 56 + b:57 + b], 0.0).then_inc(free[b], 1)
            V.memset(epst[:, 0:1], 1e-6)
            V.memset(epst[:, 1:2], 1e-5)
            V.memset(cols1[:, :, 16:18], 1.0)
            V.memset(cols2[:, :, 17:21], 1.0).then_inc(tiles_set, 1)
            dve.wait_ge(tiles_set, 1)
            n = 0
            for k in phases:
                if k[0] == "norm":
                    norm(k, n)
                    n += 1
                elif k[0] in ("mix1", "mix2"):
                    mixer(k)
                elif k[0] != "moe":
                    feed_forward(k, FFJ[k[0]])
                else:
                    route(k)
                    gathered(k, 0)
                    nj = each_job(dve, lambda e: expert_job(k, FFJ["moe"], e))
                    scattered(k, nj)
            norm(("norm", 0, None), n)

        @block.gpsimd
        def _(pool):
            G = nc.gpsimd
            links = [0]
            loads = [0, 0]

            def link(ins):
                links[0] += 1
                ins.then_inc(pool_link, 1)
                pool.wait_ge(pool_link, links[0])

            def load(dst, src, second=False):
                loads[second] += 1
                pool.dma_start(dst, src).then_inc(par2_loaded if second else par_loaded, 16)

            pool.dma_start(onehot[:, :], a["onehot"]).then_inc(bias_loaded, 16)
            pool.dma_start(tab[0:32, :], a["bias_table_2"]).then_inc(bias_loaded, 16)
            pool.dma_start(tab[32:33, :], a["ones8"]).then_inc(bias_loaded, 16)
            pool.dma_start(glab[:, :], a["gla_b"][0].partition_broadcast(P)).then_inc(glab_loaded, 16)
            load(posi[:, :], a["positions"][0].rearrange("(t p) -> p t", p=P))
            load(heads8[:, :, 0:8], a["ssd_a_log"].partition_broadcast(P))
            load(heads8[:, :, 8:16], a["ssd_d"].partition_broadcast(P))

            for name, cc in (("fox_qn", 26), ("fox_kn", 27)):
                for h in range(2):
                    load(cols1[64 * h:64 * h + 64, :, cc], a[name].rearrange("l p -> p l"))
            assert loads[0] == NPAR_POOL, loads

            def build(k, h, col, slot):
                for j, (m, t) in enumerate((("after", 0), ("ones", 1), ("after", 1))):
                    last = G.tensor_scalar(Bld[:, slot, j * P:j * P + P], C(m), z[:, t, col:col + 1], None, ALU.mult)
                last.then_inc(T["builds"], 1)

            def mix1(k):
                l, c0 = k[1], CH[k]
                if l == 0:
                    pool.wait_ge(free[X[3]], ev("bias_rows", X[3]))
                    pool.dma_start(scratch, tabT[0:8, :]).then_inc(rows_out, 16)
                    pool.wait_ge(rows_out, 16)
                pool.wait_ge(T["decay"], at("decay", l))
                for h in range(4):
                    build(k, h, 256 + h, h)
                for n in (3, 4):
                    for t in range(NT):
                        pool.wait_ge(free[gbank(n, t)], ev((k, "gemm", n), gbank(n, t)))
                if l == 0:
                    pool.wait_ge(setup_s, 1)
                for t in range(NT):
                    v = u[:, t, U1["rq"]:U1["rq"] + 512].rearrange("p (h j d) -> p h j d", j=2, d=32)
                    x1, x2 = v[:, :, 0, :], v[:, :, 1, :]
                    sn, cs = (rot[:, i, t, :].unsqueeze(1).to_broadcast([P, 8, 32]) for i in range(2))
                    t0, t1, t2 = (rope_t[:, i, t] for i in range(3))
                    G.tensor_tensor(t0, x1, cs, ALU.mult)
                    G.tensor_tensor(t1, x2, sn, ALU.mult)
                    link(G.tensor_tensor(t2, x1, sn, ALU.mult))
                    link(G.tensor_tensor(x1, t0, t1, ALU.subtract))
                    link(G.tensor_tensor(t0, x2, cs, ALU.mult))
                    last = G.tensor_tensor(x2, t2, t0, ALU.add)
                last.then_inc(T["rope"], 1)
                for h in range(4):
                    pool.wait_ge(full[X[h]], fl((k, f"fs{h}"), X[h]))
                    build(k, h, 260 + h, h)
                pool.wait_ge(T["xbc"], at("xbc", l, 3))
                for t in range(NT):
                    pool.wait_ge(free[X[t]], ev((k, "xs"), X[t]))
                for r in range(2):
                    for t in range(NT):
                        xs = u[:, t, U1["xbc"] + 256 * r:U1["xbc"] + 256 * r + 256].rearrange("p (h d) -> p h d", d=HD)
                        last = G.tensor_tensor(qM[:, r, t, :].rearrange("p (h d) -> p h d", d=HD), xs,
                                               heads8[:, l, 8 + 4 * r:12 + 4 * r].unsqueeze(2).to_broadcast([P, 4, HD]), ALU.mult)
                    last.then_inc(T["ssd_dx"], 1)
                for h in range(4, 8):
                    pool.wait_ge(full[X[h % 4]], fl((k, f"sg{h - 4}"), X[h % 4]))
                    build(k, h, 260 + h, h % 4)

            def merge(k):
                l, name = k[1], "merged" if k[0] == "mix1" else "merged_b"
                for br in range(1, 3):
                    banks = (0, 1, 2, 3) if br % 2 == 0 else X
                    for t in range(NT):
                        for n in range(2):
                            b0, b = 2 * t + n, banks[2 * t + n]
                            if br == 1:
                                pool.wait_ge(free[b0], ev((k, "up", 0), b0))
                            else:
                                pool.wait_ge(T[name], at(name, l, 4 * (br - 2) + 2 * t + n + 1))
                            pool.wait_ge(free[b], ev((k, "up", br), b))
                            m = u[:, t, n * 512:n * 512 + 512]
                            G.tensor_tensor(m, m, gates[:, t, br * 1024 + n * 512:br * 1024 + n * 512 + 512], ALU.add).then_inc(T[name], 1)

            for k, ready in zip(phases, XREADY):
                if k[0] == "norm" and k[2] == "mix2" and k[1] == 0:
                    for b, v in ready:
                        pool.wait_ge(free[b], v)
                    pool.dma_start(biasT[:, :, :], bass.AP(scratch.tensor, 0, [[1, P], [384, 8], [1, S]])).then_inc(bias_in, 16)
                    for l in range(L1):
                        load(wgrp[:, l], a["pool_w_2"][l].rearrange("g c d -> c g d"), True)
                    load(router[:, :, :], a["moe_router_2"][0].rearrange("(k p) n -> p k n", p=P), True)
                    load(poolw[:, :, :], a["poolw"], True)
                    assert loads[1] == NPAR2, loads
                elif k[0] == "norm" and k[2] == "moe":
                    for b, v in ready:
                        pool.wait_ge(free[b], v)
                    pool.wait_ge(moe_gain_in, 16)
                    for t in range(NT):
                        G.tensor_tensor(hrow[:, t, :], x[:, t, :], mgain[:, :], ALU.mult).then_inc(rows_gained, 1)
                elif k[0] == "norm" and k[2] == "mix1" and k[1] > 0:
                    for b, v in ready:
                        pool.wait_ge(free[b], v)
                    pool.dma_start(glab[:, :], a["gla_b"][k[1]].partition_broadcast(P)).then_inc(glab_loaded, 16)
                elif k[0] == "mix1":
                    mix1(k)
                    merge(k)
                elif k[0] == "mix2":
                    merge(k)
                    if k[1] == L1 - 1 and ("moe", k[1]) in phases:
                        pool.wait_ge(full[X[2]], fl((k, "dy1"), X[2]))
                        pool.dma_start(mgain[:, :], a["ffn_norm_g_2"][k[1]].partition_broadcast(P)).then_inc(moe_gain_in, 16)
            for b, v in last_x:
                pool.wait_ge(free[b], v)
            pool.dma_start(fgain[:, :], a["final_norm_g_2"].partition_broadcast(P)).then_inc(fgain_in, 16)


FFJ = {"ffn1": FH1 // FB, "ffn2": FH1 // FB, "moe": FH2 // FB}
LAM_INIT = [0.8 - 0.6 * math.exp(-0.3 * i) for i in range(L1)]
LOG_GAMMA = [float(np.log(np.float32(1.0) - np.float32(2.0) ** np.float32(-5.0 - h))) for h in range(RH)]
TWO_PI_2 = float(np.float32(2 * math.pi - 6.28125))
TWO_PI_3 = 2 * math.pi - 6.28125 - TWO_PI_2
NPAR_POOL = 3 + 4
NPAR_SP = 4 + 8 * L1 + 2 + 1
NNARROW = 6
NPAR2 = L1 + 2

_INS = ["x", "positions", "ln1", "ln2", "w_in", "fox_bf", "fox_qn", "fox_kn", "gla_w2", "gla_b", "gla_norm", "ret_norm",
        "ssd_conv_w", "ssd_conv_b", "ssd_dt_bias", "ssd_a_log", "ssd_d", "ssd_norm", "w_up_a", "w_up_b", "w_up_c", "w_up_d",
        "w_out", "w_ffn_in", "w_ffn_out", "bias_table_2", "mix_norm_g_2", "w_in_2", "conv_w_2", "pool_w_2", "pool_scale_2",
        "diff_lambda_2", "diff_subln_g_2", "branch_proj_2", "w_out_2", "ffn_norm_g_2", "dense_w1_2", "dense_w3_2",
        "dense_w2_2", "moe_router_2", "moe_w1_2", "moe_w3_2", "moe_w2_2", "final_norm_g_2"]


def kernel(**inputs):
    import concourse.bacc as bacc
    from concourse.bass_utils import run_bass_kernel_spmd as run

    nc = bacc.Bacc("TRN2", target_bir_lowering=False, num_devices=1)
    arrays = {name: np.ascontiguousarray(inputs[name]) for name in _INS}
    arrays.update(cst=constants(), ident=identity(), onehot=bias_buckets(), poolw=pool_matrices(), ones8=np.ones((1, 8), np.float32))
    a = {name: nc.dram_tensor(f"in_{name}", v.shape, mybir.dt.from_np(v.dtype), kind="ExternalInput").ap()
         for name, v in arrays.items()}
    out = nc.dram_tensor("out", (S, D), F32, kind="ExternalOutput").ap()
    program(nc, a, out)
    r = run(nc, [{f"in_{name}": v for name, v in arrays.items()}], core_ids=[0])
    return r.results[0]["out"].reshape(1, S, D)
```
